# Optimizing a Trainium2 kernel written in Bass

```python
import jax, jax.numpy as jnp
from jax import lax
import numpy as np
import math

D_MODEL = 1024
BATCH = 1
SEQ = 512
DEPTH = 2

N_MIXERS = 2
BLOCK_Q = 128
EPS = 1e-6
FOX_HEADS = 16
FOX_HEAD_DIM = D_MODEL // FOX_HEADS
FOX_IN = 3 * D_MODEL + FOX_HEADS
FORGET_BIAS_INIT = 3.0
MLA_HEADS = 16
MLA_Q_RANK = 384
MLA_KV_RANK = 256
MLA_NOPE_DIM = 64
MLA_ROPE_DIM = 32
MLA_V_DIM = 64
MLA_QK_DIM = MLA_NOPE_DIM + MLA_ROPE_DIM
MLA_IN = MLA_Q_RANK + MLA_KV_RANK + MLA_ROPE_DIM
ROPE_THETA = 10000.0
N_GROUPS = 4
EXPERTS_PER_GROUP = 4
N_EXPERTS = N_GROUPS * EXPERTS_PER_GROUP
TOP_K_IN_GROUP = 2
D_EXPERT = 256

N_FOX_LAYERS = (DEPTH + 1) // 2
N_MLA_LAYERS = DEPTH // 2


def rmsnorm(x, g):
    xf = x.astype(jnp.float32)
    y = xf * lax.rsqrt(jnp.mean(xf * xf, axis=-1, keepdims=True) + EPS)
    return (y * g.astype(jnp.float32)).astype(x.dtype)

def rope(x, positions):
    half = MLA_ROPE_DIM // 2
    inv_freq = ROPE_THETA ** (-jnp.arange(0, half, dtype=jnp.float32) / half)
    ang = positions.astype(jnp.float32)[..., None] * inv_freq
    cos = jnp.cos(ang)[:, :, None, :]
    sin = jnp.sin(ang)[:, :, None, :]
    xf = x.astype(jnp.float32)
    x1, x2 = xf[..., :half], xf[..., half:]
    out = jnp.concatenate([x1 * cos - x2 * sin, x1 * sin + x2 * cos], axis=-1)
    return out.astype(x.dtype)

def causal_block_attention(q, k, v, scale, cum=None):
    B, H, S, dk = q.shape
    nb = S // BLOCK_Q
    qb = q.reshape(B, H, nb, BLOCK_Q, dk).transpose(2, 0, 1, 3, 4)
    kpos = jnp.arange(S)

    def one_block(args):
        i, qi = args
        s = jnp.einsum('bhqd,bhkd->bhqk', qi, k).astype(jnp.float32) * scale
        if cum is not None:
            ci = lax.dynamic_slice_in_dim(cum, i * BLOCK_Q, BLOCK_Q, axis=2)
            s = s + ci[..., :, None] - cum[..., None, :]
        qpos = i * BLOCK_Q + jnp.arange(BLOCK_Q)
        mask = kpos[None, :] <= qpos[:, None]
        s = jnp.where(mask, s, -jnp.inf)
        p = jax.nn.softmax(s, axis=-1)
        return jnp.einsum('bhqk,bhkd->bhqd', p.astype(v.dtype), v)

    o = lax.map(one_block, (jnp.arange(nb), qb))
    return o.transpose(1, 2, 0, 3, 4).reshape(B, H, S, v.shape[-1])

def fox_mixer(h, w_in, b_f, q_norm, k_norm, w_out):
    B, S, D = h.shape
    proj = h @ w_in
    q = proj[..., :D].reshape(B, S, FOX_HEADS, FOX_HEAD_DIM)
    k = proj[..., D:2 * D].reshape(B, S, FOX_HEADS, FOX_HEAD_DIM)
    v = proj[..., 2 * D:3 * D].reshape(B, S, FOX_HEADS, FOX_HEAD_DIM)
    f_logit = proj[..., 3 * D:]
    q = rmsnorm(q, q_norm)
    k = rmsnorm(k, k_norm)
    log_f = jax.nn.log_sigmoid((f_logit + b_f).astype(jnp.float32))
    cum = jnp.cumsum(log_f, axis=1).transpose(0, 2, 1)
    o = causal_block_attention(q.transpose(0, 2, 1, 3), k.transpose(0, 2, 1, 3),
                               v.transpose(0, 2, 1, 3), FOX_HEAD_DIM ** -0.5, cum)
    o = o.transpose(0, 2, 1, 3).reshape(B, S, D)
    return o @ w_out

def mla_mixer(h, positions, w_in, q_lat_norm, kv_lat_norm, w_uq, w_ukv, q_norm, k_norm, w_out):
    B, S, D = h.shape
    proj = h @ w_in
    cq = rmsnorm(proj[..., :MLA_Q_RANK], q_lat_norm)
    ckv = rmsnorm(proj[..., MLA_Q_RANK:MLA_Q_RANK + MLA_KV_RANK], kv_lat_norm)
    k_rope = proj[..., MLA_Q_RANK + MLA_KV_RANK:]
    q = (cq @ w_uq).reshape(B, S, MLA_HEADS, MLA_QK_DIM)
    kv = (ckv @ w_ukv).reshape(B, S, MLA_HEADS, MLA_NOPE_DIM + MLA_V_DIM)
    k_nope, v = kv[..., :MLA_NOPE_DIM], kv[..., MLA_NOPE_DIM:]
    k = jnp.concatenate(
        [k_nope, jnp.broadcast_to(k_rope[:, :, None, :], (B, S, MLA_HEADS, MLA_ROPE_DIM))], axis=-1)
    q = rmsnorm(q, q_norm)
    k = rmsnorm(k, k_norm)
    q = jnp.concatenate([q[..., :MLA_NOPE_DIM], rope(q[..., MLA_NOPE_DIM:], positions)], axis=-1)
    k = jnp.concatenate([k[..., :MLA_NOPE_DIM], rope(k[..., MLA_NOPE_DIM:], positions)], axis=-1)
    o = causal_block_attention(q.transpose(0, 2, 1, 3), k.transpose(0, 2, 1, 3),
                               v.transpose(0, 2, 1, 3), MLA_QK_DIM ** -0.5)
    o = o.transpose(0, 2, 1, 3).reshape(B, S, MLA_HEADS * MLA_V_DIM)
    return o @ w_out

def hier_moe(h, w_grp, b_grp, w_rt, b_rt, w_gate, w_up, w_down):
    B, S, D = h.shape
    T = B * S
    t = h.reshape(T, D)
    g_logits = (t @ w_grp).astype(jnp.float32) + b_grp.astype(jnp.float32)
    g_prob = jax.nn.softmax(g_logits, axis=-1)
    g_top, g_idx = lax.top_k(g_prob, 1)
    e_logits = ((t @ w_rt).astype(jnp.float32) + b_rt.astype(jnp.float32)).reshape(
        T, N_GROUPS, EXPERTS_PER_GROUP)
    sel = jnp.broadcast_to(g_idx[:, :, None], (T, 1, EXPERTS_PER_GROUP))
    in_group = jnp.take_along_axis(e_logits, sel, axis=1)[:, 0]
    e_top, e_idx = lax.top_k(in_group, TOP_K_IN_GROUP)
    w = jax.nn.softmax(e_top, axis=-1) * g_top
    expert_id = g_idx * EXPERTS_PER_GROUP + e_idx
    combine = jnp.sum(jax.nn.one_hot(expert_id, N_EXPERTS, dtype=jnp.float32) * w[..., None], axis=1)
    a = jnp.einsum('td,edf->tef', t, w_gate)
    u = jnp.einsum('td,edf->tef', t, w_up)
    hidden = jax.nn.silu(a) * u * combine[..., None].astype(t.dtype)
    out = jnp.einsum('tef,efd->td', hidden, w_down)
    return out.reshape(B, S, D)

def first_inputs(seed: int = 0) -> dict:
    key = jax.random.key(seed)
    ks = jax.random.split(key, 32)
    D = D_MODEL
    nrm = lambda k, shape, scale: jax.random.normal(k, shape, jnp.float32) * scale
    gain = lambda k, shape: 1.0 + 0.02 * jax.random.normal(k, shape, jnp.float32)
    offsets = jax.random.randint(ks[2], (BATCH, 1), 0, 1024, dtype=jnp.int32)
    return {
        "x": nrm(ks[0], (BATCH, SEQ, D), 1.0),
        "c": nrm(ks[1], (BATCH, D), 1.0),
        "positions": offsets + jnp.arange(SEQ, dtype=jnp.int32)[None, :],
        "w_ada": nrm(ks[3], (DEPTH, D, 6 * D), 0.5 * D ** -0.5),
        "b_ada": nrm(ks[4], (DEPTH, 6 * D), 0.01),
        "mix_norm": gain(ks[5], (DEPTH, D)),
        "ffn_norm": gain(ks[6], (DEPTH, D)),
        "fox_w_in": nrm(ks[7], (N_FOX_LAYERS, D, FOX_IN), D ** -0.5),
        "fox_b_f": FORGET_BIAS_INIT + nrm(ks[8], (N_FOX_LAYERS, FOX_HEADS), 0.5),
        "fox_q_norm": gain(ks[9], (N_FOX_LAYERS, FOX_HEAD_DIM)),
        "fox_k_norm": gain(ks[10], (N_FOX_LAYERS, FOX_HEAD_DIM)),
        "fox_w_out": nrm(ks[11], (N_FOX_LAYERS, D, D), D ** -0.5),
        "mla_w_in": nrm(ks[12], (N_MLA_LAYERS, D, MLA_IN), D ** -0.5),
        "mla_q_lat_norm": gain(ks[13], (N_MLA_LAYERS, MLA_Q_RANK)),
        "mla_kv_lat_norm": gain(ks[14], (N_MLA_LAYERS, MLA_KV_RANK)),
        "mla_w_uq": nrm(ks[15], (N_MLA_LAYERS, MLA_Q_RANK, MLA_HEADS * MLA_QK_DIM), MLA_Q_RANK ** -0.5),
        "mla_w_ukv": nrm(ks[16], (N_MLA_LAYERS, MLA_KV_RANK, MLA_HEADS * (MLA_NOPE_DIM + MLA_V_DIM)),
                         MLA_KV_RANK ** -0.5),
        "mla_q_norm": gain(ks[17], (N_MLA_LAYERS, MLA_QK_DIM)),
        "mla_k_norm": gain(ks[18], (N_MLA_LAYERS, MLA_QK_DIM)),
        "mla_w_out": nrm(ks[19], (N_MLA_LAYERS, MLA_HEADS * MLA_V_DIM, D), (MLA_HEADS * MLA_V_DIM) ** -0.5),
        "moe_w_grp": nrm(ks[20], (DEPTH, D, N_GROUPS), D ** -0.5),
        "moe_b_grp": nrm(ks[21], (DEPTH, N_GROUPS), 0.01),
        "moe_w_rt": nrm(ks[22], (DEPTH, D, N_EXPERTS), D ** -0.5),
        "moe_b_rt": nrm(ks[23], (DEPTH, N_EXPERTS), 0.01),
        "moe_w_gate": nrm(ks[24], (DEPTH, N_EXPERTS, D, D_EXPERT), D ** -0.5),
        "moe_w_up": nrm(ks[25], (DEPTH, N_EXPERTS, D, D_EXPERT), D ** -0.5),
        "moe_w_down": nrm(ks[26], (DEPTH, N_EXPERTS, D_EXPERT, D), D_EXPERT ** -0.5),
    }

def first_block(x, c, positions, w_ada, b_ada, mix_norm, ffn_norm,
              fox_w_in, fox_b_f, fox_q_norm, fox_k_norm, fox_w_out,
              mla_w_in, mla_q_lat_norm, mla_kv_lat_norm, mla_w_uq, mla_w_ukv, mla_q_norm, mla_k_norm,
              mla_w_out,
              moe_w_grp, moe_b_grp, moe_w_rt, moe_b_rt, moe_w_gate, moe_w_up, moe_w_down):
    c_act = jax.nn.silu(c)
    for i in range(DEPTH):
        mod = c_act @ w_ada[i] + b_ada[i]
        sh1, sc1, g1, sh2, sc2, g2 = [m[:, None, :] for m in jnp.split(mod, 6, axis=-1)]
        h = rmsnorm(x, mix_norm[i]) * (1.0 + sc1) + sh1
        j = i // N_MIXERS
        if i % N_MIXERS == 0:
            y = fox_mixer(h, fox_w_in[j], fox_b_f[j], fox_q_norm[j], fox_k_norm[j], fox_w_out[j])
        else:
            y = mla_mixer(h, positions, mla_w_in[j], mla_q_lat_norm[j], mla_kv_lat_norm[j],
                          mla_w_uq[j], mla_w_ukv[j], mla_q_norm[j], mla_k_norm[j], mla_w_out[j])
        x = x + g1 * y
        h = rmsnorm(x, ffn_norm[i]) * (1.0 + sc2) + sh2
        x = x + g2 * hier_moe(h, moe_w_grp[i], moe_b_grp[i], moe_w_rt[i], moe_b_rt[i],
                              moe_w_gate[i], moe_w_up[i], moe_w_down[i])
    return x


DEPTH_2 = 1

CHUNK = 64
MIX_WIDTH = D_MODEL
CONV_WIDTH = MIX_WIDTH // 2
CONV_KSIZE = 31
RW_WIDTH = MIX_WIDTH - CONV_WIDTH
RW_HEAD_DIM = 64
RW_HEADS = RW_WIDTH // RW_HEAD_DIM
LORA_W = 64
LORA_A = 64
LORA_G = 128
RW_PROJ = 3 * RW_WIDTH + LORA_W + LORA_A + LORA_G
IN_PROJ = 2 * CONV_WIDTH + RW_PROJ
PEER_HEADS = 8
PEER_NKEYS = 128
PEER_TOPK = 16
PEER_QDIM = 256
PEER_N_EXPERTS = PEER_NKEYS * PEER_NKEYS
PEER_TOKEN_BLOCK = 128
ALPHA = (2.0 * DEPTH_2) ** 0.25
BETA = (8.0 * DEPTH_2) ** -0.25
LN_EPS = 1e-5
GN_EPS = 64e-5


def layer_norm(x, g=None, b=None, eps=LN_EPS):
    xf = x.astype(jnp.float32)
    mu = jnp.mean(xf, axis=-1, keepdims=True)
    var = jnp.mean(jnp.square(xf - mu), axis=-1, keepdims=True)
    y = (xf - mu) * lax.rsqrt(var + eps)
    if g is not None:
        y = y * g + b
    return y

def adaln(x, shift, scale):
    return layer_norm(x) * (1.0 + scale[:, None, :]) + shift[:, None, :]

def rwkv7_scan(r, decay, k, v, kk, a):
    bsz, _, nh, nd = r.shape
    xs = tuple(jnp.moveaxis(t.astype(jnp.float32), 1, 0) for t in (r, decay, k, v, kk, a))

    def step(state, inp):
        r_t, w_t, k_t, v_t, kk_t, a_t = inp
        sa = jnp.einsum('bhvk,bhk->bhv', state, -kk_t)
        state = (state * w_t[:, :, None, :]
                 + sa[..., None] * (kk_t * a_t)[:, :, None, :]
                 + v_t[..., None] * k_t[:, :, None, :])
        y_t = jnp.einsum('bhvk,bhk->bhv', state, r_t)
        return state, y_t

    state0 = jnp.zeros((bsz, nh, nd, nd), jnp.float32)
    _, ys = lax.scan(step, state0, xs)
    return jnp.moveaxis(ys, 0, 1)

def second_inputs(seed: int = 0) -> dict:
    key = jax.random.key(seed)
    ks = jax.random.split(key, 40)
    f32 = jnp.float32

    def nrm(k, shape, scale):
        return jax.random.normal(k, shape, f32) * scale

    s_in = D_MODEL ** -0.5
    col_scale = s_in * jnp.concatenate([
        jnp.full((CONV_WIDTH,), BETA, f32),
        jnp.ones((CONV_WIDTH,), f32),
        jnp.ones((2 * RW_WIDTH,), f32),
        jnp.full((RW_WIDTH,), BETA, f32),
        jnp.ones((LORA_W + LORA_A + LORA_G,), f32),
    ])
    return {
        "x": nrm(ks[0], (BATCH, SEQ, D_MODEL), 1.0),
        "c": nrm(ks[1], (BATCH, D_MODEL), 1.0),
        "cond_w": nrm(ks[2], (D_MODEL, 6 * D_MODEL), 0.5 * D_MODEL ** -0.5),
        "cond_b": nrm(ks[3], (6 * D_MODEL,), 0.02),
        "w_in": jax.random.normal(ks[4], (D_MODEL, IN_PROJ), f32) * col_scale,
        "mu_shift": jax.random.uniform(ks[5], (RW_PROJ,), f32),
        "conv_w": nrm(ks[6], (CONV_KSIZE, CONV_WIDTH), CONV_KSIZE ** -0.5),
        "conv_b": nrm(ks[7], (CONV_WIDTH,), 0.02),
        "conv_ln_g": 1.0 + nrm(ks[8], (CONV_WIDTH,), 0.05),
        "conv_ln_b": nrm(ks[9], (CONV_WIDTH,), 0.02),
        "rw_w0": jnp.linspace(-7.0, -2.0, RW_WIDTH, dtype=f32) + nrm(ks[10], (RW_WIDTH,), 0.1),
        "rw_w2": nrm(ks[11], (LORA_W, RW_WIDTH), 0.1 * LORA_W ** -0.5),
        "rw_a0": nrm(ks[12], (RW_WIDTH,), 0.1),
        "rw_a2": nrm(ks[13], (LORA_A, RW_WIDTH), LORA_A ** -0.5),
        "rw_g2": nrm(ks[14], (LORA_G, RW_WIDTH), LORA_G ** -0.5),
        "rw_kk": 0.85 + nrm(ks[15], (RW_WIDTH,), 0.05),
        "rw_ka": 1.0 + nrm(ks[16], (RW_WIDTH,), 0.05),
        "rw_rk": nrm(ks[17], (RW_HEADS, RW_HEAD_DIM), 0.1),
        "rw_lnx_g": 1.0 + nrm(ks[18], (RW_WIDTH,), 0.05),
        "rw_lnx_b": nrm(ks[19], (RW_WIDTH,), 0.02),
        "w_out": nrm(ks[20], (MIX_WIDTH, D_MODEL), BETA * MIX_WIDTH ** -0.5),
        "ln1_g": 1.0 + nrm(ks[21], (D_MODEL,), 0.05),
        "ln1_b": nrm(ks[22], (D_MODEL,), 0.02),
        "peer_wq": nrm(ks[23], (D_MODEL, PEER_HEADS * PEER_QDIM), s_in),
        "peer_k1": nrm(ks[24], (PEER_HEADS, PEER_NKEYS, PEER_QDIM // 2), (PEER_QDIM // 2) ** -0.5),
        "peer_k2": nrm(ks[25], (PEER_HEADS, PEER_NKEYS, PEER_QDIM // 2), (PEER_QDIM // 2) ** -0.5),
        "peer_u": nrm(ks[26], (PEER_N_EXPERTS, D_MODEL), BETA * s_in),
        "peer_v": nrm(ks[27], (PEER_N_EXPERTS, D_MODEL), BETA),
        "ln2_g": 1.0 + nrm(ks[28], (D_MODEL,), 0.05),
        "ln2_b": nrm(ks[29], (D_MODEL,), 0.02),
    }

def second_block(x, c, cond_w, cond_b, w_in, mu_shift, conv_w, conv_b, conv_ln_g, conv_ln_b,
              rw_w0, rw_w2, rw_a0, rw_a2, rw_g2, rw_kk, rw_ka, rw_rk, rw_lnx_g, rw_lnx_b,
              w_out, ln1_g, ln1_b, peer_wq, peer_k1, peer_k2, peer_u, peer_v, ln2_g, ln2_b):
    bsz, seq, dm = x.shape

    mod = jax.nn.silu(c) @ cond_w + cond_b
    shift1, scale1, gate1, shift2, scale2, gate2 = jnp.split(mod, 6, axis=-1)

    for _ in range(DEPTH_2):
        h = adaln(x, shift1, scale1)
        p = h @ w_in
        p_conv = p[..., :2 * CONV_WIDTH]
        p_rw = p[..., 2 * CONV_WIDTH:]

        u = p_conv[..., :CONV_WIDTH] * jax.nn.sigmoid(p_conv[..., CONV_WIDTH:])
        u = lax.conv_general_dilated(
            u, conv_w.astype(u.dtype)[:, None, :], window_strides=(1,),
            padding=[(CONV_KSIZE - 1, 0)], dimension_numbers=('NWC', 'WIO', 'NWC'),
            feature_group_count=CONV_WIDTH) + conv_b
        y_conv = jax.nn.silu(layer_norm(u, conv_ln_g, conv_ln_b))

        p_prev = jnp.pad(p_rw[:, :-1], ((0, 0), (1, 0), (0, 0)))
        xm = p_rw + (p_prev - p_rw) * mu_shift
        o = 0
        r = xm[..., o:o + RW_WIDTH]; o += RW_WIDTH
        k = xm[..., o:o + RW_WIDTH]; o += RW_WIDTH
        v = xm[..., o:o + RW_WIDTH]; o += RW_WIDTH
        wd = xm[..., o:o + LORA_W]; o += LORA_W
        ad = xm[..., o:o + LORA_A]; o += LORA_A
        gd = xm[..., o:o + LORA_G]
        w_log = -jax.nn.softplus(-(rw_w0 + jnp.tanh(wd) @ rw_w2)) - 0.5
        decay = jnp.exp(-jnp.exp(w_log.astype(jnp.float32)))
        a = jax.nn.sigmoid(rw_a0 + ad @ rw_a2)
        g = jax.nn.sigmoid(gd) @ rw_g2
        heads = lambda t: t.reshape(bsz, seq, RW_HEADS, RW_HEAD_DIM)
        kk = heads(k * rw_kk).astype(jnp.float32)
        kk = kk / jnp.maximum(jnp.linalg.norm(kk, axis=-1, keepdims=True), 1e-12)
        k = k * (1.0 + (a - 1.0) * rw_ka)
        rh, kh, vh, ah = heads(r), heads(k), heads(v), heads(a)
        y_rw = rwkv7_scan(rh, heads(decay), kh, vh, kk, ah)
        y_rw = layer_norm(y_rw, eps=GN_EPS).reshape(bsz, seq, RW_WIDTH) * rw_lnx_g + rw_lnx_b
        bonus = jnp.sum(rh * kh * rw_rk, axis=-1, keepdims=True) * vh
        y_rw = (y_rw + bonus.reshape(bsz, seq, RW_WIDTH)) * g

        y1 = jnp.concatenate([y_conv, y_rw], axis=-1) @ w_out
        x = layer_norm(ALPHA * x + gate1[:, None, :] * y1, ln1_g, ln1_b)

        h2 = adaln(x, shift2, scale2)
        q = (h2 @ peer_wq).reshape(bsz, seq, PEER_HEADS, PEER_QDIM).astype(jnp.float32)
        half = PEER_QDIM // 2
        s1 = jnp.einsum('bshd,hnd->bshn', q[..., :half], peer_k1.astype(jnp.float32))
        s2 = jnp.einsum('bshd,hnd->bshn', q[..., half:], peer_k2.astype(jnp.float32))
        v1, i1 = lax.top_k(s1, PEER_TOPK)
        v2, i2 = lax.top_k(s2, PEER_TOPK)
        cand = (v1[..., :, None] + v2[..., None, :]).reshape(bsz, seq, PEER_HEADS, PEER_TOPK * PEER_TOPK)
        sc, ci = lax.top_k(cand, PEER_TOPK)
        experts = (jnp.take_along_axis(i1, ci // PEER_TOPK, axis=-1) * PEER_NKEYS
                   + jnp.take_along_axis(i2, ci % PEER_TOPK, axis=-1))
        gates = jax.nn.softmax(sc, axis=-1)

        n_tok = bsz * seq
        nblk = n_tok // PEER_TOKEN_BLOCK
        hk = PEER_HEADS * PEER_TOPK
        h_blk = h2.reshape(nblk, PEER_TOKEN_BLOCK, dm)
        e_blk = experts.reshape(nblk, PEER_TOKEN_BLOCK, hk)
        g_blk = gates.reshape(nblk, PEER_TOKEN_BLOCK, hk)

        def peer_block(args):
            hb, eb, gb = args
            u_sel = jnp.take(peer_u, eb, axis=0)
            z = jnp.einsum('td,tkd->tk', hb, u_sel)
            act = jax.nn.gelu(z, approximate=False) * gb
            return jnp.einsum('tk,tkd->td', act, jnp.take(peer_v, eb, axis=0))

        y2 = lax.map(peer_block, (h_blk, e_blk, g_blk)).reshape(bsz, seq, dm)
        x = layer_norm(ALPHA * x + gate2[:, None, :] * y2, ln2_g, ln2_b)

    return x


def setup_inputs(seed=0):
    out = dict(first_inputs(seed))
    for name, value in second_inputs(seed + 1).items():
        if name != "x":
            out[name + "_2"] = value
    return out


def reference(
    x, c, positions, w_ada, b_ada, mix_norm, ffn_norm, fox_w_in, fox_b_f, fox_q_norm,
    fox_k_norm, fox_w_out, mla_w_in, mla_q_lat_norm, mla_kv_lat_norm, mla_w_uq, mla_w_ukv,
    mla_q_norm, mla_k_norm, mla_w_out, moe_w_grp, moe_b_grp, moe_w_rt, moe_b_rt, moe_w_gate,
    moe_w_up, moe_w_down, c_2, cond_w_2, cond_b_2, w_in_2, mu_shift_2, conv_w_2, conv_b_2,
    conv_ln_g_2, conv_ln_b_2, rw_w0_2, rw_w2_2, rw_a0_2, rw_a2_2, rw_g2_2, rw_kk_2, rw_ka_2,
    rw_rk_2, rw_lnx_g_2, rw_lnx_b_2, w_out_2, ln1_g_2, ln1_b_2, peer_wq_2, peer_k1_2, peer_k2_2,
    peer_u_2, peer_v_2, ln2_g_2, ln2_b_2,
):
    x = first_block(
        x, c, positions, w_ada, b_ada, mix_norm, ffn_norm, fox_w_in, fox_b_f, fox_q_norm,
        fox_k_norm, fox_w_out, mla_w_in, mla_q_lat_norm, mla_kv_lat_norm, mla_w_uq, mla_w_ukv,
        mla_q_norm, mla_k_norm, mla_w_out, moe_w_grp, moe_b_grp, moe_w_rt, moe_b_rt, moe_w_gate,
        moe_w_up, moe_w_down,
    )
    return second_block(
        x, c_2, cond_w_2, cond_b_2, w_in_2, mu_shift_2, conv_w_2, conv_b_2, conv_ln_g_2,
        conv_ln_b_2, rw_w0_2, rw_w2_2, rw_a0_2, rw_a2_2, rw_g2_2, rw_kk_2, rw_ka_2, rw_rk_2,
        rw_lnx_g_2, rw_lnx_b_2, w_out_2, ln1_g_2, ln1_b_2, peer_wq_2, peer_k1_2, peer_k2_2,
        peer_u_2, peer_v_2, ln2_g_2, ln2_b_2,
    )


_drawn_inputs = setup_inputs


def setup_inputs(seed=0):
    import zlib

    import numpy as np

    out = dict(_drawn_inputs(seed))
    spreads = {}
    factors = {'b_ada': 3.082,
     'mix_norm': 7.409,
     'ffn_norm': 3.352,
     'fox_q_norm': 7.809,
     'fox_k_norm': 8.0,
     'mla_q_lat_norm': 8.0,
     'mla_kv_lat_norm': 8.0,
     'mla_q_norm': 8.0,
     'mla_k_norm': 8.0,
     'moe_b_grp': 8.0,
     'moe_b_rt': 8.0,
     'cond_b_2': 5.15,
     'conv_b_2': 8.0,
     'conv_ln_g_2': 55.103,
     'conv_ln_b_2': 200.0,
     'rw_w2_2': 38.852,
     'rw_a0_2': 8.0,
     'rw_kk_2': 61.047,
     'rw_ka_2': 35.507,
     'rw_rk_2': 4.498,
     'rw_lnx_g_2': 64.0,
     'rw_lnx_b_2': 200.0,
     'ln1_b_2': 2.804,
     'ln2_b_2': 2.781}
    for name, (base, spread) in spreads.items():
        noise = np.random.default_rng([zlib.crc32(name.encode()), seed]).standard_normal(out[name].shape)
        drawn = base * np.exp(spread * noise) if base else spread * noise
        out[name] = __import__('jax').numpy.asarray(drawn.astype(out[name].dtype))
    for name, factor in factors.items():
        out[name] = (out[name] * factor).astype(out[name].dtype)
    return out
```

```python
import math
from contextlib import ExitStack

import numpy as np
import concourse.bass as bass
from concourse import mybir

F32 = mybir.dt.float32
I32 = mybir.dt.int32
U32 = mybir.dt.uint32
ACT = mybir.ActivationFunctionType
ALU = mybir.AluOpType
AX = mybir.AxisListType.X

P = 128
SEQ = 512
TILES = SEQ // P
D = 1024
KD = D // P
BANK = 512
EPS = 1e-6
LN_EPS = 1e-5
GN_EPS = 64e-5
HEADS = 16
FOX_DK = D // HEADS
DV = 64
Q_RANK, KV_RANK, NOPE, ROPE = 384, 256, 64, 32
QK = NOPE + ROPE
GROUPS, PER_GROUP, EXPERTS, D_EXPERT = 4, 4, 16, 256
NEG = -3.0e38
TWO_PI = 2.0 * math.pi


class Stage:

    def __init__(self, nc, name):
        self.nc, self.name, self.ctx, self.sems = nc, name, ExitStack(), []

    def sb(self, name, shape, dtype=F32):
        return self.ctx.enter_context(self.nc.sbuf_tensor(f"{self.name}_{name}", list(shape), dtype))

    def ps(self, name, shape, dtype=F32):
        return self.ctx.enter_context(self.nc.psum_tensor(f"{self.name}_{name}", list(shape), dtype))

    def sem(self, name):
        self.sems.append(self.ctx.enter_context(self.nc.semaphore(f"{self.name}_{name}")))
        return self.sems[-1]

    def __enter__(self):
        return self

    def __exit__(self, *error):
        if error[0] is None and self.sems:
            with self.nc.Block() as block:
                @block.gpsimd
                def _(pool):
                    for sem in self.sems:
                        pool.sem_clear(sem)
        return self.ctx.__exit__(*error)


class Chain:

    def __init__(self, eng, sem):
        self.eng, self.sem, self.n = eng, sem, 0

    def __call__(self, ins):
        self.n = self.n + 1
        ins.then_inc(self.sem, 1)
        self.eng.wait_ge(self.sem, self.n)


def constants(nc, a, g):
    with Stage(nc, "const") as s:
        loaded = s.sem("loaded")
        with nc.Block() as block:
            @block.sync
            def _(sp):
                sp.dma_start(g.ident[:], a["ident"]).then_inc(loaded, 16)
                sp.dma_start(g.causal[:], a["causal"]).then_inc(loaded, 16)
                sp.dma_start(g.iota[:], a["iota"]).then_inc(loaded, 16)
                sp.dma_start(g.x[:], a["x"].rearrange("o (t p) d -> p (o t) d", p=P)).then_inc(loaded, 16)
                sp.wait_ge(loaded, 64)


def modulation(nc, g, name, c_dram, w_dram, b_dram):
    CH, SLOTS = 6 * D // BANK, 3
    with Stage(nc, name) as s:
        c_col, c_act = s.sb("c_col", [P, KD]), s.sb("c_act", [P, KD])
        c_rep = s.sb("c_rep", [P, KD, P])
        bias = s.sb("bias", [1, 6 * D])
        ones = s.sb("ones", [1, P])
        ring = s.sb("ring", [P, SLOTS, KD, BANK])
        acc = s.ps("acc", [P, SLOTS, BANK])
        small, acted, rep = s.sem("small"), s.sem("acted"), s.sem("rep")
        w_in = [s.sem(f"w_in{u}") for u in range(SLOTS)]
        summed, kept = s.sem("summed"), s.sem("kept")
        mod = g.mod[:].rearrange("p j d -> p (j d)")
        with nc.Block() as block:
            @block.sync
            def _(sp):
                sp.dma_start(c_col[:], c_dram).then_inc(small, 16)
                sp.dma_start(bias[:], b_dram).then_inc(small, 16)
                for u in range(SLOTS):
                    sp.dma_start(ring[:, u], w_dram[u]).then_inc(w_in[u], 16)
                with sp.Fori(0, CH // SLOTS - 1) as i:
                    for u in range(SLOTS):
                        sp.wait_ge(summed, SLOTS * i + u + 1)
                        sp.dma_start(ring[:, u], w_dram[bass.ds(SLOTS * i + u + SLOTS, 1)].rearrange(
                            "o p k n -> p (o k) n")).then_inc(w_in[u], 16)

            @block.scalar
            def _(act):
                act.wait_ge(small, 32)
                nc.scalar.activation(c_act[:], c_col[:], ACT.Silu).then_inc(acted, 1)
                act.sem_inc(kept, SLOTS)
                with act.Fori(0, CH // SLOTS) as i:
                    for u in range(SLOTS):
                        act.wait_ge(summed, SLOTS * i + u + 1)
                        nc.scalar.copy(mod[:, bass.ds((SLOTS * i + u) * BANK, BANK)], acc[:, u]).then_inc(kept, 1)

            @block.vector
            def _(dve):
                nc.vector.memset(ones[:], 1.0).then_inc(rep, 1)
                dve.wait_ge(acted, 1)
                nc.vector.tensor_copy(c_rep[:], c_act[:].unsqueeze(2).to_broadcast([P, KD, P])).then_inc(rep, 1)

            @block.tensor
            def _(pe):
                pe.wait_ge(rep, 2)
                pe.wait_ge(small, 32)
                with pe.Fori(0, CH // SLOTS) as i:
                    for u in range(SLOTS):
                        pe.wait_ge(w_in[u], 16 * i + 16)
                        pe.wait_ge(kept, SLOTS * i + u + 1)
                        for k in range(KD):
                            nc.tensor.matmul(acc[:, u], c_rep[:, k], ring[:, u, k], start=(k == 0), stop=False)
                        nc.tensor.matmul(acc[:, u], ones[:], bias[:, bass.ds((SLOTS * i + u) * BANK, BANK)],
                                         start=False, stop=True).then_inc(summed, 1)


def normed(nc, g, name, kind, scale_at, shift_at, gain=None):
    with Stage(nc, name) as s:
        h = s.sb("h", [P, 2, D])
        square = s.sb("square", [P, D])
        gain_row, factor = s.sb("gain_row", [P, D]), s.sb("factor", [P, D])
        stat = s.sb("stat", [P, TILES, 2, 6])
        ms, rstd, mean = s.sb("ms", [P, TILES, 2]), s.sb("rstd", [P, TILES]), s.sb("mean", [P, TILES])
        root = s.sb("root", [P, TILES])
        pt = s.ps("pt", [P, 2, KD, P])
        loaded, order, squared = s.sem("loaded"), s.sem("order"), s.sem("squared")
        scaled, turned, kept, shifted = s.sem("scaled"), s.sem("turned"), s.sem("kept"), s.sem("shifted")
        ready, rooted = s.sem("ready"), s.sem("rooted")
        with nc.Block() as block:
            @block.sync
            def _(sp):
                if gain is not None:
                    sp.dma_start(gain_row[:], gain).then_inc(loaded, 16)

            @block.scalar
            def _(act):
                if kind == "rms":
                    for t in range(TILES):
                        if t:
                            act.wait_ge(squared, t)
                        nc.scalar.activation(square[:], g.x[:, t], ACT.Square,
                                             accum_out=ms[:, t, 0:1]).then_inc(squared, 1)
                act.wait_ge(ready, 1)
                nc.scalar.activation(root[:], mean[:], ACT.Sqrt).then_inc(rooted, 1)
                for t in range(TILES):
                    act.wait_ge(turned, t + 1)
                    for half in range(2):
                        ks = slice(half * KD // 2, (half + 1) * KD // 2)
                        nc.scalar.copy(g.hT[:, ks, t * P:(t + 1) * P], pt[:, t % 2, ks]).then_inc(kept, 1)

            @block.vector
            def _(dve):
                then = Chain(dve, order)
                if gain is not None:
                    dve.wait_ge(loaded, 16)
                    then(nc.vector.scalar_tensor_tensor(factor[:], g.mod[:, scale_at], 1.0, gain_row[:], ALU.add, ALU.mult))
                else:
                    then(nc.vector.tensor_scalar(factor[:], g.mod[:, scale_at], 1.0, None, ALU.add))
                if kind == "rms":
                    dve.wait_ge(squared, TILES)
                    then(nc.vector.tensor_scalar(mean[:], ms[:, :, 0], 1.0 / D, EPS, ALU.mult, ALU.add))
                else:
                    for t in range(TILES):
                        for half in range(2):
                            then(nc.vector.bn_stats(stat[:, t, half], g.x[:, t, half * D // 2:(half + 1) * D // 2]))
                        then(nc.vector.bn_aggr(ms[:, t], stat[:, t]))
                    then(nc.vector.tensor_scalar(mean[:], ms[:, :, 1], LN_EPS, None, ALU.add))
                nc.vector.tensor_scalar(mean[:], mean[:], 0.0, None, ALU.max).then_inc(ready, 1)
                dve.wait_ge(rooted, 1)
                then(nc.vector.reciprocal(rstd[:], root[:]))
                for t in range(TILES):
                    if t >= 2:
                        dve.wait_ge(turned, t - 1)
                    if kind == "rms":
                        then(nc.vector.scalar_tensor_tensor(h[:, t % 2], g.x[:, t], rstd[:, t:t + 1], factor[:],
                                                            ALU.mult, ALU.mult))
                    else:
                        then(nc.vector.tensor_scalar(h[:, t % 2], g.x[:, t], ms[:, t, 0:1], rstd[:, t:t + 1],
                                                     ALU.subtract, ALU.mult))
                        then(nc.vector.tensor_tensor(h[:, t % 2], h[:, t % 2], factor[:], ALU.mult))
                    nc.vector.tensor_tensor(h[:, t % 2], h[:, t % 2], g.mod[:, shift_at], ALU.add).then_inc(shifted, 1)

            @block.tensor
            def _(pe):
                for t in range(TILES):
                    pe.wait_ge(shifted, t + 1)
                    if t >= 2:
                        pe.wait_ge(kept, 2 * (t - 1))
                    for k in range(KD):
                        last = nc.tensor.transpose(pt[:, t % 2, k], h[:, t % 2, k * P:(k + 1) * P], g.ident[:])
                    last.then_inc(turned, 1)


def project_rows(nc, name, lhs, kc, w_dram, chunks, width, keep=None, gate=None, x=None, alpha=1.0):
    with Stage(nc, name) as s:
        ring = s.sb("ring", [P, 2, kc, width])
        part = s.sb("part", [P, 2, width])
        acc = s.ps("acc", [P, 2, TILES, BANK])
        w_in = [s.sem(f"w_in{u}") for u in range(2)]
        summed, kept, gated = s.sem("summed"), s.sem("kept"), s.sem("gated")
        pairs = chunks // 2
        assert chunks == 2 * pairs

        def chunk_loop(eng, body):
            if pairs == 1:
                for u in range(2):
                    body(0, u)
            else:
                with eng.Fori(0, pairs) as i:
                    for u in range(2):
                        body(i, u)

        with nc.Block() as block:
            @block.sync
            def _(sp):
                for u in range(2):
                    sp.dma_start(ring[:, u], w_dram[u]).then_inc(w_in[u], 16)
                if pairs > 1:
                    with sp.Fori(0, pairs - 1) as i:
                        for u in range(2):
                            sp.wait_ge(summed, TILES * (2 * i + u) + TILES)
                            sp.dma_start(ring[:, u], w_dram[bass.ds(2 * i + u + 2, 1)].rearrange(
                                "o p k n -> p (o k) n")).then_inc(w_in[u], 16)

            @block.tensor
            def _(pe):
                def body(i, u):
                    pe.wait_ge(w_in[u], 16 * i + 16)
                    for t in range(TILES):
                        pe.wait_ge(kept, TILES * (2 * i + u) + t + 1)
                        for k in range(kc):
                            last = nc.tensor.matmul(acc[:, u, t, :width], lhs[:, k, t * P:(t + 1) * P], ring[:, u, k],
                                                    start=(k == 0), stop=(k == kc - 1))
                        last.then_inc(summed, 1)
                chunk_loop(pe, body)

            if keep is not None:
                @block.scalar
                def _(act):
                    act.sem_inc(kept, 2 * TILES)

                    def body(i, u):
                        for t in range(TILES):
                            act.wait_ge(summed, TILES * (2 * i + u) + t + 1)
                            nc.scalar.copy(keep[:, t, bass.ds((2 * i + u) * width, width)],
                                           acc[:, u, t, :width]).then_inc(kept, 1)
                    chunk_loop(act, body)
            else:
                @block.vector
                def _(dve):
                    dve.sem_inc(kept, 2 * TILES)
                    for n in range(chunks):
                        cols = slice(n * width, (n + 1) * width)
                        for t in range(TILES):
                            m = n * TILES + t
                            dve.wait_ge(summed, m + 1)
                            nc.vector.tensor_tensor(part[:, m % 2], acc[:, n % 2, t, :width], gate[:, cols],
                                                    ALU.mult).then_inc(kept, 1)
                            dve.wait_ge(kept, 2 * TILES + m + 1)
                            nc.vector.scalar_tensor_tensor(x[:, t, cols], x[:, t, cols], alpha, part[:, m % 2],
                                                           ALU.mult, ALU.add).then_inc(gated, 1)


def project_cols(nc, name, rhs, kc, w_dram, chunks, keep):
    with Stage(nc, name) as s:
        ring = s.sb("ring", [P, 2, kc, P])
        acc = s.ps("acc", [P, 2, BANK])
        w_in = [s.sem(f"w_in{u}") for u in range(2)]
        summed, kept = s.sem("summed"), s.sem("kept")
        pairs = chunks // 2
        assert chunks == 2 * pairs and pairs > 1
        with nc.Block() as block:
            @block.sync
            def _(sp):
                for u in range(2):
                    sp.dma_start(ring[:, u], w_dram[u]).then_inc(w_in[u], 16)
                with sp.Fori(0, pairs - 1) as i:
                    for u in range(2):
                        sp.wait_ge(summed, 2 * i + u + 1)
                        sp.dma_start(ring[:, u], w_dram[bass.ds(2 * i + u + 2, 1)].rearrange(
                            "o p k n -> p (o k) n")).then_inc(w_in[u], 16)

            @block.tensor
            def _(pe):
                with pe.Fori(0, pairs) as i:
                    for u in range(2):
                        pe.wait_ge(w_in[u], 16 * i + 16)
                        pe.wait_ge(kept, 2 * i + u + 1)
                        for k in range(kc):
                            last = nc.tensor.matmul(acc[:, u], ring[:, u, k], rhs[:, k], start=(k == 0), stop=(k == kc - 1))
                        last.then_inc(summed, 1)

            @block.scalar
            def _(act):
                act.sem_inc(kept, 2)
                with act.Fori(0, pairs) as i:
                    for u in range(2):
                        act.wait_ge(summed, 2 * i + u + 1)
                        nc.scalar.copy(keep[:, bass.ds(2 * i + u, 1)], acc[:, u]).then_inc(kept, 1)


def turn_rows(nc, g, name, rows, chunks, turned):
    with Stage(nc, name) as s:
        pt = s.ps("pt", [P, 4, TILES, P])
        done, kept = s.sem("done"), s.sem("kept")
        with nc.Block() as block:
            @block.tensor
            def _(pe):
                for c in range(chunks):
                    if c >= 4:
                        pe.wait_ge(kept, c - 3)
                    for t in range(TILES):
                        last = nc.tensor.transpose(pt[:, c % 4, t], rows[:, t, c * P:(c + 1) * P], g.ident[:])
                    last.then_inc(done, 1)

            @block.scalar
            def _(act):
                for c in range(chunks):
                    act.wait_ge(done, c + 1)
                    nc.scalar.copy(turned[:, c], pt[:, c % 4].rearrange("p t n -> p (t n)")).then_inc(kept, 1)
def head_norms(nc, name, jobs, dk, heads=HEADS):
    with Stage(nc, name) as s:
        n = len(jobs) * TILES
        square = s.sb("square", [P, 2, heads, dk])
        total, root, inv = (s.sb(x, [P, n, heads]) for x in ("total", "root", "inv"))
        gains = [s.sb(f"gain{j}", [P, dk]) for j in range(len(jobs))]
        loaded, squared, summed, rooted = s.sem("loaded"), s.sem("squared"), s.sem("summed"), s.sem("rooted")
        order, halfway, normed_ = s.sem("order"), s.sem("halfway"), s.sem("normed")

        def tile(m):
            rows, _, _ = jobs[m // TILES]
            return rows[:, m % TILES].rearrange("p (h d) -> p h d", d=dk)

        with nc.Block() as block:
            @block.sync
            def _(sp):
                for j, (_, gain, _) in enumerate(jobs):
                    sp.dma_start(gains[j][:], gain).then_inc(loaded, 16)

            @block.scalar
            def _(act):
                for m in range(n):
                    if m >= 2:
                        act.wait_ge(summed, m - 1)
                    nc.scalar.activation(square[:, m % 2], tile(m), ACT.Square).then_inc(squared, 1)
                act.wait_ge(order, 1)
                nc.scalar.activation(root[:], total[:], ACT.Sqrt).then_inc(rooted, 1)

            @block.vector
            def _(dve):
                for m in range(n):
                    dve.wait_ge(squared, m + 1)
                    nc.vector.tensor_reduce(total[:, m], square[:, m % 2], AX, ALU.add).then_inc(summed, 1)
                dve.wait_ge(summed, n)
                then = Chain(dve, order)
                then(nc.vector.tensor_scalar(total[:], total[:], 1.0 / dk, EPS, ALU.mult, ALU.add))
                dve.wait_ge(rooted, 1)
                then(nc.vector.reciprocal(inv[:], root[:]))
                for j, (_, _, scale) in enumerate(jobs):
                    if scale != 1.0:
                        part = inv[:, j * TILES:(j + 1) * TILES]
                        then(nc.vector.tensor_scalar(part, part, scale, None, ALU.mult))
                dve.wait_ge(loaded, 16 * len(jobs))
                for m in range(n):
                    nc.vector.tensor_tensor(tile(m), tile(m), inv[:, m].unsqueeze(2).to_broadcast([P, heads, dk]),
                                            ALU.mult).then_inc(halfway, 1)
                    dve.wait_ge(halfway, m + 1)
                    nc.vector.tensor_tensor(tile(m), tile(m), gains[m // TILES][:].unsqueeze(1).to_broadcast([P, heads, dk]),
                                            ALU.mult).then_inc(normed_, 1)


def forget_gates(nc, g, name, w_dram, b_dram, scratch, cum_q, cum_k):
    with Stage(nc, name) as s:
        w, b = s.sb("w", [P, KD, HEADS]), s.sb("b", [HEADS, 1])
        z, low, ones = (s.sb(x, [HEADS, SEQ]) for x in ("z", "low", "ones"))
        size, small, soft = (s.sb(x, [HEADS, SEQ]) for x in ("size", "small", "soft"))
        logs, cum = s.sb("logs", [HEADS, SEQ]), s.sb("cum", [HEADS, SEQ])
        logits, turned = s.ps("logits", [HEADS, SEQ]), s.ps("turned", [P, TILES, HEADS])
        loaded, summed, order, steps = s.sem("loaded"), s.sem("summed"), s.sem("order"), s.sem("steps")
        stored, spread, turn = s.sem("stored"), s.sem("spread"), s.sem("turn")
        with nc.Block() as block:
            @block.sync
            def _(sp):
                sp.dma_start(w[:], w_dram).then_inc(loaded, 16)
                sp.dma_start(b[:], b_dram).then_inc(loaded, 16)
                sp.wait_ge(order, 6)
                sp.dma_start(scratch, cum[:]).then_inc(stored, 16)
                sp.wait_ge(stored, 16)
                sp.dma_start(cum_k[:], scratch.partition_broadcast(P)).then_inc(spread, 16)
                sp.wait_ge(spread, 16)

            @block.tensor
            def _(pe):
                pe.wait_ge(loaded, 32)
                for k in range(KD):
                    last = nc.tensor.matmul(logits[:], w[:, k], g.hT[:, k], start=(k == 0), stop=(k == KD - 1))
                last.then_inc(summed, 1)
                pe.wait_ge(order, 6)
                for t in range(TILES):
                    last = nc.tensor.transpose(turned[:, t], cum[:, t * P:(t + 1) * P], g.ident[:HEADS, :HEADS])
                last.then_inc(turn, 1)

            @block.scalar
            def _(act):
                then = Chain(act, steps)
                act.wait_ge(order, 2)
                then(nc.scalar.activation(size[:], z[:], ACT.Abs))
                then(nc.scalar.activation(small[:], size[:], ACT.Exp, scale=-1.0))
                then(nc.scalar.activation(soft[:], small[:], ACT.Ln, bias=1.0))

            @block.vector
            def _(dve):
                then = Chain(dve, order)
                then(nc.vector.memset(ones[:], 1.0))
                dve.wait_ge(loaded, 32)
                dve.wait_ge(summed, 1)
                then(nc.vector.tensor_scalar(z[:], logits[:], b[:], None, ALU.add))
                then(nc.vector.tensor_scalar(low[:], z[:], 0.0, None, ALU.min))
                dve.wait_ge(steps, 3)
                then(nc.vector.tensor_tensor(logs[:], low[:], soft[:], ALU.subtract))
                then(nc.vector.tensor_scalar(z[:], ones[:], 0.0, None, ALU.mult))
                then(nc.vector.tensor_tensor_scan(cum[:], ones[:], logs[:], 0.0, ALU.mult, ALU.add))
                dve.wait_ge(turn, 1)
                then(nc.vector.tensor_copy(cum_q[:], turned[:]))


def attention(nc, g, name, q, k, v, o, dk, v_step=DV, v_at=0, cum_q=None, cum_k=None):
    with Stage(nc, name) as s:
        qs, ks = s.sb("qs", [P, TILES, dk]), s.sb("ks", [P, TILES, dk])
        qT, kT = s.sb("qT", [dk, SEQ]), s.sb("kT", [dk, SEQ])
        z, p = s.sb("z", [P, 2, SEQ]), s.sb("p", [P, 2, SEQ])
        pT = s.sb("pT", [P, 2, TILES, P])
        low, total, inv = s.sb("low", [P, 2]), s.sb("total", [P, 2]), s.sb("inv", [P, 2])
        tq, tk = s.ps("tq", [dk, SEQ]), s.ps("tk", [dk, SEQ])
        scores, tp = s.ps("scores", [P, 2, SEQ]), s.ps("tp", [P, 2, TILES, P])
        out = s.ps("out", [P, 2, BANK])
        copied, turned, kept = s.sem("copied"), s.sem("turned"), s.sem("kept")
        scored, biased, masked, maxed = s.sem("scored"), s.sem("biased"), s.sem("masked"), s.sem("maxed")
        raised, p_turned, p_kept = s.sem("raised"), s.sem("p_turned"), s.sem("p_kept")
        started = s.sem("started")
        mixed, inverted, done = s.sem("mixed"), s.sem("inverted"), s.sem("done")
        AHEAD = 2
        with nc.Block() as block:
            @block.gpsimd
            def _(pool):
                with pool.Fori(0, HEADS) as h:
                    pool.wait_ge(turned, h + 1)
                    nc.gpsimd.tensor_copy(qs[:], q[:, :, bass.ds(h * dk, dk)]).then_inc(copied, 1)
                    nc.gpsimd.tensor_copy(ks[:], k[:, :, bass.ds(h * dk, dk)]).then_inc(copied, 1)

            @block.tensor
            def _(pe):
                pe.sem_inc(turned, 1)
                pe.sem_inc(scored, 1)
                pe.sem_inc(p_turned, AHEAD)
                pe.sem_inc(mixed, AHEAD)
                with pe.Fori(0, HEADS) as h:
                    def score(i):
                        n, width = TILES * h + i, (i + 1) * P
                        pe.wait_ge(biased, n + 1)
                        nc.tensor.matmul(scores[:, i % 2, :width], qT[:, i * P:(i + 1) * P], kT[:, :width],
                                         start=True, stop=True).then_inc(scored, 1)

                    def turn(i):
                        n = TILES * h + i
                        pe.wait_ge(raised, n + 1 + AHEAD)
                        pe.wait_ge(p_kept, n + 1)
                        for j in range(i + 1):
                            last = nc.tensor.transpose(tp[:, i % 2, j], p[:, i % 2, j * P:(j + 1) * P], g.ident[:])
                        last.then_inc(p_turned, 1)

                    def mix(i):
                        n = TILES * h + i
                        pe.wait_ge(p_kept, n + 1 + AHEAD)
                        pe.wait_ge(done, n + 1)
                        for j in range(i + 1):
                            last = nc.tensor.matmul(out[:, i % 2, :DV], pT[:, i % 2, j], v[:, j, bass.ds(h * v_step + v_at, DV)],
                                                    start=(j == 0), stop=(j == i))
                        last.then_inc(mixed, 1)

                    pe.wait_ge(copied, 2 * h + 2)
                    pe.wait_ge(kept, 2 * h + 2)
                    pe.sem_inc(started, 1)
                    for src, dst in ((qs, tq), (ks, tk)):
                        for t in range(TILES):
                            last = nc.tensor.transpose(dst[:, t * P:(t + 1) * P], src[:, t], g.ident[:])
                    last.then_inc(turned, 1)
                    pe.wait_ge(kept, 2 * h + 4)
                    score(0)
                    score(1)
                    turn(0)
                    score(2)
                    turn(1)
                    mix(0)
                    score(3)
                    turn(2)
                    mix(1)
                    turn(3)
                    mix(2)
                    mix(3)

            @block.scalar
            def _(act):
                act.sem_inc(kept, 2)
                act.sem_inc(raised, AHEAD)
                act.sem_inc(p_kept, AHEAD)
                with act.Fori(0, HEADS) as h:
                    def raise_(i):
                        n, width = TILES * h + i, (i + 1) * P
                        act.wait_ge(maxed, n + 1)
                        act.wait_ge(p_turned, n + 1)
                        act.wait_ge(done, n + 1)
                        nc.scalar.activation(p[:, i % 2, :width], z[:, i % 2, :width], ACT.Exp, bias=low[:, i % 2:i % 2 + 1],
                                             accum_out=total[:, i % 2:i % 2 + 1]).then_inc(raised, 1)

                    def keep(i):
                        n = TILES * h + i
                        act.wait_ge(p_turned, n + 1 + AHEAD)
                        act.wait_ge(mixed, n + 1)
                        nc.scalar.copy(pT[:, i % 2, :i + 1], tp[:, i % 2, :i + 1]).then_inc(p_kept, 1)

                    act.wait_ge(turned, h + 2)
                    act.wait_ge(scored, TILES * h + 1)
                    nc.scalar.copy(qT[:], tq[:]).then_inc(kept, 1)
                    nc.scalar.copy(kT[:], tk[:]).then_inc(kept, 1)
                    raise_(0)
                    raise_(1)
                    keep(0)
                    raise_(2)
                    keep(1)
                    raise_(3)
                    keep(2)
                    keep(3)

            @block.vector
            def _(dve):
                dve.sem_inc(biased, AHEAD)
                dve.sem_inc(done, AHEAD)
                with dve.Fori(0, HEADS) as h:
                    def bias(i):
                        n, width = TILES * h + i, (i + 1) * P
                        dve.wait_ge(scored, n + 2)
                        dve.wait_ge(raised, n + 1)
                        if cum_q is None:
                            nc.vector.tensor_copy(z[:, i % 2, :width], scores[:, i % 2, :width]).then_inc(biased, 1)
                        else:
                            nc.vector.scalar_tensor_tensor(
                                z[:, i % 2, :width], scores[:, i % 2, :width], cum_q[:, i, bass.ds(h, 1)],
                                cum_k[:, bass.ds(h, 1), :width].rearrange("p o t -> p (o t)"),
                                ALU.add, ALU.subtract).then_inc(biased, 1)
                        dve.wait_ge(biased, n + 1 + AHEAD)
                        diagonal = z[:, i % 2, i * P:width]
                        nc.vector.tensor_tensor(diagonal, diagonal, g.causal[:], ALU.add).then_inc(masked, 1)
                        dve.wait_ge(masked, n + 1)
                        nc.vector.tensor_reduce(low[:, i % 2:i % 2 + 1], z[:, i % 2, :width], AX, ALU.max,
                                                negate=True).then_inc(maxed, 1)

                    def divide(i):
                        n = TILES * h + i
                        dve.wait_ge(mixed, n + 1 + AHEAD)
                        nc.vector.reciprocal(inv[:, i % 2:i % 2 + 1], total[:, i % 2:i % 2 + 1]).then_inc(inverted, 1)
                        dve.wait_ge(inverted, n + 1)
                        nc.vector.tensor_scalar(o[:, i, bass.ds(h * DV, DV)], out[:, i % 2, :DV], inv[:, i % 2:i % 2 + 1],
                                                None, ALU.mult).then_inc(done, 1)

                    bias(0)
                    bias(1)
                    bias(2)
                    divide(0)
                    bias(3)
                    divide(1)
                    divide(2)
                    divide(3)
def route(nc, g, name, w_dram, b_dram):
    N = GROUPS + EXPERTS
    with Stage(nc, name) as s:
        w, b = s.sb("w", [P, KD, N]), s.sb("b", [P, N])
        by_group, by_expert = s.sb("by_group", [P, TILES, 8]), s.sb("by_expert", [P, TILES, EXPERTS])
        best, best_at = s.sb("best", [P, TILES, 8]), s.sb("best_at", [P, TILES, 8], U32)
        group, is_group = s.sb("group", [P, TILES, 1]), s.sb("is_group", [P, TILES, GROUPS])
        lowered, raised = s.sb("lowered", [P, TILES, GROUPS]), s.sb("raised", [P, TILES, GROUPS])
        total, top = s.sb("total", [P, TILES, 1]), s.sb("top", [P, TILES, 1])
        chosen = s.sb("chosen", [P, TILES, GROUPS, PER_GROUP])
        inside = s.sb("inside", [P, TILES, 8])
        pair, pair_at = s.sb("pair", [P, TILES, 8]), s.sb("pair_at", [P, TILES, 8], U32)
        ids, weights = s.sb("ids", [P, TILES, 2]), s.sb("weights", [P, TILES, 2])
        gap, ratio = s.sb("gap", [P, TILES, 1]), s.sb("ratio", [P, TILES, 1])
        first, second = s.sb("first", [P, TILES, EXPERTS]), s.sb("second", [P, TILES, EXPERTS])
        logits = s.ps("logits", [P, TILES, N])
        loaded, summed, order = s.sem("loaded"), s.sem("summed"), s.sem("order")
        low_ready, raised_ready = s.sem("low_ready"), s.sem("raised_ready")
        iota = lambda n: g.iota[:, :n].unsqueeze(1).to_broadcast([P, TILES, n])
        with nc.Block() as block:
            @block.sync
            def _(sp):
                sp.dma_start(w[:], w_dram).then_inc(loaded, 16)
                sp.dma_start(b[:], b_dram).then_inc(loaded, 16)

            @block.tensor
            def _(pe):
                pe.wait_ge(loaded, 32)
                for t in range(TILES):
                    for k in range(KD):
                        last = nc.tensor.matmul(logits[:, t], g.hT[:, k, t * P:(t + 1) * P], w[:, k],
                                                start=(k == 0), stop=(k == KD - 1))
                last.then_inc(summed, 1)

            @block.scalar
            def _(act):
                act.wait_ge(low_ready, 1)
                nc.scalar.activation(raised[:], lowered[:], ACT.Exp).then_inc(raised_ready, 1)
                act.wait_ge(low_ready, 2)
                nc.scalar.activation(ratio[:], gap[:], ACT.Exp).then_inc(raised_ready, 1)

            @block.vector
            def _(dve):
                then = Chain(dve, order)
                v = nc.vector
                then(v.memset(by_group[:], NEG))
                then(v.memset(inside[:], NEG))
                dve.wait_ge(loaded, 32)
                dve.wait_ge(summed, 1)
                then(v.tensor_tensor(by_group[:, :, :GROUPS], logits[:, :, :GROUPS],
                                     b[:, :GROUPS].unsqueeze(1).to_broadcast([P, TILES, GROUPS]), ALU.add))
                then(v.tensor_tensor(by_expert[:], logits[:, :, GROUPS:],
                                     b[:, GROUPS:].unsqueeze(1).to_broadcast([P, TILES, EXPERTS]), ALU.add))
                for t in range(TILES):
                    then(v.max(best[:, t], by_group[:, t]))
                    then(v.max_index(best_at[:, t], best[:, t], by_group[:, t]))
                then(v.tensor_copy(group[:], best_at[:, :, 0:1]))
                v.tensor_tensor(lowered[:], by_group[:, :, :GROUPS], best[:, :, 0:1].to_broadcast([P, TILES, GROUPS]),
                                ALU.subtract).then_inc(low_ready, 1)
                then(v.tensor_tensor(is_group[:], iota(GROUPS), group[:].to_broadcast([P, TILES, GROUPS]), ALU.is_equal))
                for t in range(TILES):
                    then(v.tensor_tensor(chosen[:, t], by_expert[:, t].rearrange("p (a e) -> p a e", a=GROUPS),
                                         is_group[:, t].unsqueeze(2).to_broadcast([P, GROUPS, PER_GROUP]), ALU.mult))
                    then(v.tensor_reduce(inside[:, t, :PER_GROUP], chosen[:, t].rearrange("p a e -> p e a"), AX, ALU.add))
                    then(v.max(pair[:, t], inside[:, t]))
                    then(v.max_index(pair_at[:, t], pair[:, t], inside[:, t]))
                v.tensor_tensor(gap[:], pair[:, :, 1:2], pair[:, :, 0:1], ALU.subtract).then_inc(low_ready, 1)
                then(v.tensor_copy(ids[:], pair_at[:, :, 0:2]))
                then(v.scalar_tensor_tensor(ids[:], group[:].to_broadcast([P, TILES, 2]), float(PER_GROUP), ids[:],
                                            ALU.mult, ALU.add))
                dve.wait_ge(raised_ready, 2)
                then(v.tensor_reduce(total[:], raised[:], AX, ALU.add))
                then(v.reciprocal(top[:], total[:]))
                then(v.tensor_scalar(total[:], ratio[:], 1.0, None, ALU.add))
                then(v.reciprocal(gap[:], total[:]))
                then(v.tensor_tensor(weights[:, :, 0:1], gap[:], top[:], ALU.mult))
                then(v.tensor_tensor(weights[:, :, 1:2], weights[:, :, 0:1], ratio[:], ALU.mult))
                for j, part in enumerate((first, second)):
                    then(v.tensor_tensor(part[:], iota(EXPERTS), ids[:, :, j:j + 1].to_broadcast([P, TILES, EXPERTS]), ALU.is_equal))
                    then(v.tensor_tensor(part[:], part[:], weights[:, :, j:j + 1].to_broadcast([P, TILES, EXPERTS]), ALU.mult))
                then(v.tensor_tensor(g.comb[:], first[:], second[:], ALU.add))


def experts(nc, g, name, gate_dram, up_dram, down_dram, gate_row):
    FC, HALVES, BANKS = D_EXPERT // P, D // BANK, 4
    OUTS = TILES * HALVES
    with Stage(nc, name) as s:
        w_up = s.sb("w_up", [P, 2, 2, KD, D_EXPERT])
        w_down = s.sb("w_down", [P, 2, FC, D])
        bent = s.sb("bent", [P, FC, SEQ])
        hidden = s.sb("hidden", [P, 2, FC, SEQ])
        acc = s.sb("acc", [P, TILES, HALVES, BANK])
        risen = s.ps("risen", [P, FC, 2, SEQ])
        low = s.ps("low", [P, BANKS, BANK])
        up_in = [s.sem(f"up_in{u}") for u in range(2)]
        down_in = [s.sem(f"down_in{u}") for u in range(2)]
        lifted, bent_done, made = s.sem("lifted"), s.sem("bent_done"), s.sem("made")
        lowered, added, zeroed, gated = s.sem("lowered"), s.sem("added"), s.sem("zeroed"), s.sem("gated")
        with nc.Block() as block:
            def one(dram, e):
                return dram[e] if isinstance(e, int) else dram[bass.ds(e, 1)].rearrange("o p k n -> p (o k) n")

            @block.sync
            def _(sp):
                def load_up(e, u):
                    sp.dma_start(w_up[:, u, 0], one(gate_dram, e)).then_inc(up_in[u], 16)
                    sp.dma_start(w_up[:, u, 1], one(up_dram, e)).then_inc(up_in[u], 16)

                def load_down(e, u):
                    sp.dma_start(w_down[:, u], one(down_dram, e)).then_inc(down_in[u], 16)

                for u in range(2):
                    load_up(u, u)
                    load_down(u, u)
                with sp.Fori(0, EXPERTS // 2 - 1) as i:
                    for u in range(2):
                        e = 2 * i + u
                        sp.wait_ge(lifted, FC * e + FC)
                        load_up(e + 2, u)
                        sp.wait_ge(lowered, OUTS * e + OUTS)
                        load_down(e + 2, u)

            @block.tensor
            def _(pe):
                def lift(e, u):
                    pe.wait_ge(up_in[u], 32 * (e // 2) + 32 if isinstance(e, int) else 16 * (e - u) + 32)
                    for f in range(FC):
                        pe.wait_ge(made, FC * e + f + 1)
                        for j in range(2):
                            for k in range(KD):
                                last = nc.tensor.matmul(risen[:, f, j], w_up[:, u, j, k, f * P:(f + 1) * P], g.hT[:, k],
                                                        start=(k == 0), stop=(k == KD - 1))
                        last.then_inc(lifted, 1)

                def lower(e, u):
                    pe.wait_ge(down_in[u], 16 * (e // 2) + 16 if isinstance(e, int) else 8 * (e - u) + 16)
                    pe.wait_ge(made, FC * e + 2 * FC)
                    for m in range(OUTS):
                        t, half = m // HALVES, m % HALVES
                        pe.wait_ge(added, OUTS * e + m + 1)
                        for f in range(FC):
                            last = nc.tensor.matmul(low[:, m % BANKS], hidden[:, u, f, t * P:(t + 1) * P],
                                                    w_down[:, u, f, half * BANK:(half + 1) * BANK],
                                                    start=(f == 0), stop=(f == FC - 1))
                        last.then_inc(lowered, 1)

                lift(0, 0)
                with pe.Fori(0, EXPERTS // 2 - 1) as i:
                    lift(2 * i + 1, 1)
                    lower(2 * i, 0)
                    lift(2 * i + 2, 0)
                    lower(2 * i + 1, 1)
                lift(EXPERTS - 1, 1)
                lower(EXPERTS - 2, 0)
                lower(EXPERTS - 1, 1)

            @block.scalar
            def _(act):
                with act.Fori(0, EXPERTS) as e:
                    for f in range(FC):
                        act.wait_ge(lifted, FC * e + f + 1)
                        act.wait_ge(made, FC * e + f + 1)
                        nc.scalar.activation(bent[:, f], risen[:, f, 0], ACT.Silu).then_inc(bent_done, 1)

            @block.vector
            def _(dve):
                def make(e, u, peeled=False):
                    for f in range(FC):
                        dve.wait_ge(bent_done, FC * e + f + 1)
                        if not peeled:
                            dve.wait_ge(lowered, OUTS * (e - 1))
                        nc.vector.tensor_tensor(hidden[:, u, f], bent[:, f], risen[:, f, 1], ALU.mult).then_inc(made, 1)

                def add(e):
                    dve.wait_ge(added, OUTS * e + BANKS)
                    for m in range(OUTS):
                        t, half = m // HALVES, m % HALVES
                        dve.wait_ge(lowered, OUTS * e + m + 1)
                        weight = g.comb[:, t, e:e + 1] if isinstance(e, int) else g.comb[:, t, bass.ds(e, 1)]
                        nc.vector.scalar_tensor_tensor(acc[:, t, half], low[:, m % BANKS], weight, acc[:, t, half],
                                                       ALU.mult, ALU.add).then_inc(added, 1)

                dve.sem_inc(made, FC)
                dve.sem_inc(added, BANKS)
                nc.vector.memset(acc[:], 0.0).then_inc(zeroed, 1)
                dve.wait_ge(zeroed, 1)
                make(0, 0, True)
                make(1, 1, True)
                add(0)
                with dve.Fori(1, EXPERTS // 2) as i:
                    make(2 * i, 0)
                    add(2 * i - 1)
                    make(2 * i + 1, 1)
                    add(2 * i)
                add(EXPERTS - 1)
                dve.wait_ge(added, OUTS * EXPERTS + BANKS)
                for t in range(TILES):
                    rows = acc[:, t].rearrange("p a n -> p (a n)")
                    nc.vector.tensor_tensor(rows, rows, gate_row, ALU.mult).then_inc(gated, 1)
                    dve.wait_ge(gated, t + 1)
                    nc.vector.tensor_tensor(g.x[:, t], g.x[:, t], rows, ALU.add).then_inc(zeroed, 1)
def split_latents(nc, g, name, kv, rope_rows, pos_dram, freq_dram, k, cos, sin):
    HALF = ROPE // 2
    BIG = 1.5 * 2.0 ** 23
    TURN_HI = 6.28125
    TURN_LO = TWO_PI - TURN_HI
    with Stage(nc, name) as s:
        pos_i, pos = s.sb("pos_i", [P, TILES], I32), s.sb("pos", [P, TILES])
        freq = s.sb("freq", [P, HALF])
        angle, turns, size = (s.sb(x, [P, TILES, HALF]) for x in ("angle", "turns", "size"))
        loaded, order, ready, split = s.sem("loaded"), s.sem("order"), s.sem("ready"), s.sem("split")
        kv_heads = [kv[:, t].rearrange("p (h d) -> p h d", h=HEADS) for t in range(TILES)]
        k_heads = [k[:, t].rearrange("p (h d) -> p h d", h=HEADS) for t in range(TILES)]
        with nc.Block() as block:
            @block.sync
            def _(sp):
                sp.dma_start(pos_i[:], pos_dram).then_inc(loaded, 16)
                sp.dma_start(freq[:], freq_dram).then_inc(loaded, 16)

            @block.gpsimd
            def _(pool):
                for t in range(TILES):
                    nc.gpsimd.tensor_copy(k_heads[t][:, :, :NOPE], kv_heads[t][:, :, :NOPE]).then_inc(split, 1)

            @block.vector
            def _(dve):
                then = Chain(dve, order)
                v = nc.vector
                dve.wait_ge(loaded, 32)
                then(v.tensor_copy(pos[:], pos_i[:]))
                then(v.tensor_tensor(angle[:], pos[:].unsqueeze(2).to_broadcast([P, TILES, HALF]),
                                     freq[:].unsqueeze(1).to_broadcast([P, TILES, HALF]), ALU.mult))
                then(v.tensor_scalar(turns[:], angle[:], 1.0 / TWO_PI, None, ALU.mult))
                then(v.tensor_scalar(turns[:], turns[:], BIG, None, ALU.add))
                then(v.tensor_scalar(turns[:], turns[:], -BIG, None, ALU.add))
                for part in (TURN_HI, TURN_LO):
                    then(v.scalar_tensor_tensor(angle[:], turns[:], -part, angle[:], ALU.mult, ALU.add))
                then(v.tensor_scalar(angle[:], angle[:], 3.1415925, -3.1415925, ALU.min, ALU.max))
                then(v.scalar_tensor_tensor(size[:], angle[:], -1.0, angle[:], ALU.mult, ALU.max))
                v.tensor_scalar(size[:], size[:], -1.0, math.pi / 2, ALU.mult, ALU.add).then_inc(ready, 1)
                for t in range(TILES):
                    v.tensor_copy(k_heads[t][:, :, NOPE:],
                                  rope_rows[:, t].unsqueeze(1).to_broadcast([P, HEADS, ROPE])).then_inc(split, 1)

            @block.scalar
            def _(act):
                act.wait_ge(ready, 1)
                nc.scalar.activation(sin[:], angle[:], ACT.Sin).then_inc(split, 1)
                nc.scalar.activation(cos[:], size[:], ACT.Sin).then_inc(split, 1)


def rotate(nc, name, rows, cos, sin):
    HALF = ROPE // 2
    with Stage(nc, name) as s:
        parts = s.sb("parts", [P, 2, 4, HEADS, HALF])
        times, turned = s.sem("times"), s.sem("turned")
        jobs = [(r, t) for r in rows for t in range(TILES)]
        with nc.Block() as block:
            @block.vector
            def _(dve):
                v = nc.vector
                for n, (r, t) in enumerate(jobs):
                    heads = r[:, t].rearrange("p (h d) -> p h d", h=HEADS)
                    x1, x2 = heads[:, :, NOPE:NOPE + HALF], heads[:, :, NOPE + HALF:]
                    c, d = (y[:, t].unsqueeze(1).to_broadcast([P, HEADS, HALF]) for y in (cos, sin))
                    part = parts[:, n % 2]
                    if n >= 2:
                        dve.wait_ge(turned, 2 * (n - 1))
                    for j, (a, b) in enumerate(((x1, c), (x2, d), (x1, d), (x2, c))):
                        v.tensor_tensor(part[:, j], a, b, ALU.mult).then_inc(times, 1)
                    dve.wait_ge(times, 4 * n + 4)
                    v.tensor_tensor(x1, part[:, 0], part[:, 1], ALU.subtract).then_inc(turned, 1)
                    v.tensor_tensor(x2, part[:, 2], part[:, 3], ALU.add).then_inc(turned, 1)
CONV, TAPS = 512, 31
CC = CONV // P
RW, RW_HEADS, RW_DIM = 512, 8, 64
RC = RW // P
LORA = 64
IN_CHUNKS = 22
SPAN = 32
BLOCKS = P // SPAN
SPANS = SEQ // SPAN
ALPHA = 2.0 ** 0.25


def turn_cols(nc, g, name, cols, chunks, keeps):
    with Stage(nc, name) as s:
        pt = s.ps("pt", [P, 2, chunks, P])
        done, kept = s.sem("done"), s.sem("kept")
        with nc.Block() as block:
            @block.tensor
            def _(pe):
                for t in range(TILES):
                    if t >= 2:
                        pe.wait_ge(kept, t - 1)
                    for c in range(chunks):
                        last = nc.tensor.transpose(pt[:, t % 2, c], cols[:, c, t * P:(t + 1) * P], g.ident[:])
                    last.then_inc(done, 1)

            @block.scalar
            def _(act):
                for t in range(TILES):
                    act.wait_ge(done, t + 1)
                    nc.scalar.copy(keeps[t], pt[:, t % 2].rearrange("p c n -> p (c n)")).then_inc(kept, 1)


def gated_conv(nc, g, name, pT, w_dram, b_dram, out):
    PAD = TAPS - 1
    with Stage(nc, name) as s:
        w, b = s.sb("w", [P, CC, TAPS]), s.sb("b", [P, CC])
        bent = s.sb("bent", [P, CC, SEQ])
        u = s.sb("u", [P, CC, PAD + SEQ])
        loaded, bent_done, order = s.sem("loaded"), s.sem("bent_done"), s.sem("order")
        with nc.Block() as block:
            @block.sync
            def _(sp):
                sp.dma_start(w[:], w_dram).then_inc(loaded, 16)
                sp.dma_start(b[:], b_dram).then_inc(loaded, 16)

            @block.scalar
            def _(act):
                nc.scalar.activation(bent[:], pT[:, CC:2 * CC], ACT.Sigmoid).then_inc(bent_done, 1)

            @block.vector
            def _(dve):
                v = nc.vector
                v.memset(u[:, :, :PAD], 0.0).then_inc(order, 1)
                dve.wait_ge(bent_done, 1)
                v.tensor_tensor(u[:, :, PAD:], pT[:, :CC], bent[:], ALU.mult).then_inc(order, 1)
                dve.wait_ge(order, 2)
                dve.wait_ge(loaded, 32)
                for j in range(TAPS):
                    for c in range(CC):
                        if j == 0:
                            v.tensor_scalar(out[:, c], u[:, c, :SEQ], w[:, c, 0:1], b[:, c:c + 1],
                                            ALU.mult, ALU.add).then_inc(order, 1)
                        else:
                            dve.wait_ge(order, 2 + CC * (j - 1) + c + 1)
                            v.scalar_tensor_tensor(out[:, c], u[:, c, j:j + SEQ], w[:, c, j:j + 1], out[:, c],
                                                   ALU.mult, ALU.add).then_inc(order, 1)


def conv_norm(nc, g, name, rows, g_dram, b_dram, y):
    with Stage(nc, name) as s:
        gain, shift = s.sb("gain", [P, CONV]), s.sb("shift", [P, CONV])
        stat, ms = s.sb("stat", [P, TILES, 6]), s.sb("ms", [P, TILES, 2])
        root, rstd = s.sb("root", [P, TILES]), s.sb("rstd", [P, TILES])
        loaded, order, rooted, ready, shifted, bent = (s.sem(x) for x in ("loaded", "order", "rooted", "ready", "shifted", "bent"))
        with nc.Block() as block:
            @block.sync
            def _(sp):
                sp.dma_start(gain[:], g_dram).then_inc(loaded, 16)
                sp.dma_start(shift[:], b_dram).then_inc(loaded, 16)

            @block.scalar
            def _(act):
                act.wait_ge(ready, 1)
                nc.scalar.activation(root[:], rstd[:], ACT.Sqrt).then_inc(rooted, 1)
                for t in range(TILES):
                    act.wait_ge(shifted, t + 1)
                    nc.scalar.activation(y[:, t, :CONV], rows[:, t], ACT.Silu).then_inc(bent, 1)

            @block.vector
            def _(dve):
                then = Chain(dve, order)
                v = nc.vector
                for t in range(TILES):
                    then(v.bn_stats(stat[:, t], rows[:, t]))
                    then(v.bn_aggr(ms[:, t], stat[:, t]))
                v.tensor_scalar(rstd[:], ms[:, :, 1], LN_EPS, None, ALU.add).then_inc(ready, 1)
                dve.wait_ge(rooted, 1)
                then(v.reciprocal(rstd[:], root[:]))
                dve.wait_ge(loaded, 32)
                for t in range(TILES):
                    then(v.tensor_scalar(rows[:, t], rows[:, t], ms[:, t, 0:1], rstd[:, t:t + 1], ALU.subtract, ALU.mult))
                    then(v.tensor_tensor(rows[:, t], rows[:, t], gain[:], ALU.mult))
                    v.tensor_tensor(rows[:, t], rows[:, t], shift[:], ALU.add).then_inc(shifted, 1)


def rwkv_inputs(nc, g, name, a, pT, o):
    R_AT, K_AT, V_AT, WA_AT, G_AT = 0, RC, 2 * RC, 3 * RC, 3 * RC + 1
    N = 3 * RC + 2
    p = pT[:, 2 * CC:]
    with Stage(nc, name) as s:
        mu = s.sb("mu", [P, N])
        col = s.sb("col", [P, 5, RC])
        w2a2, g2 = s.sb("w2a2", [P, RW]), s.sb("g2", [P, RW])
        pairs, heads = s.sb("pairs", [P, P]), s.sb("heads", [P, 2])
        xm, diff = p, s.sb("diff", [P, SEQ])
        bent = s.sb("bent", [P, SEQ])
        fresh = s.sb("fresh", [P, SEQ])
        logd, total, k2 = o.alpha, o.grown, o.kappa
        a_, tmp = g.hT[:, :RC], g.hT[:, RC:]
        kk = s.sb("kk", [P, RC, SEQ])
        acc = s.ps("acc", [P, 4, SEQ])
        loaded, order, rooted = s.sem("loaded"), s.sem("order"), s.sem("rooted")
        mixed, bent_done, sent, taken = s.sem("mixed"), s.sem("bent_done"), s.sem("sent"), s.sem("taken")
        squared, normed_, grown, ready, rows = s.sem("squared"), s.sem("normed"), s.sem("grown"), s.sem("ready"), s.sem("rows")
        LOADS = 7 * 16
        W0, A0, KK, KA, RK = range(5)
        with nc.Block() as block:
            @block.sync
            def _(sp):
                for dst, src in ((mu, "mu"), (col, "rw_col"), (w2a2, "w2a2"), (g2, "rw_g2"), (pairs, "pairs"),
                                 (heads, "heads"), (fresh, "fresh")):
                    sp.dma_start(dst[:], a[src]).then_inc(loaded, 16)

            @block.scalar
            def _(act):
                act.wait_ge(mixed, N)
                nc.scalar.activation(bent[:LORA], xm[:LORA, WA_AT], ACT.Tanh).then_inc(bent_done, 1)
                nc.scalar.copy(bent[LORA:], xm[LORA:, WA_AT]).then_inc(bent_done, 1)
                nc.scalar.activation(xm[:, G_AT], xm[:, G_AT], ACT.Sigmoid).then_inc(bent_done, 1)
                for c in range(RC):
                    act.wait_ge(sent, 2 * c + 1)
                    nc.scalar.activation(logd[:, c], acc[:, 0], ACT.Sigmoid, bias=col[:, W0, c:c + 1]).then_inc(taken, 1)
                    act.wait_ge(sent, 2 * c + 2)
                    nc.scalar.activation(a_[:, c], acc[:, 1], ACT.Sigmoid, bias=col[:, A0, c:c + 1]).then_inc(taken, 1)
                for c in range(RC):
                    act.wait_ge(sent, 2 * RC + c + 1)
                    nc.scalar.activation(tmp[:, c], acc[:, 2], ACT.Sqrt).then_inc(rooted, 1)
                act.wait_ge(order, 2)
                nc.scalar.activation(o.beta[:], total[:], ACT.Exp, scale=-1.0).then_inc(grown, 1)
                nc.scalar.activation(o.alpha[:], logd[:], ACT.Exp).then_inc(grown, 1)
                act.wait_ge(grown, 1)
                nc.scalar.activation(o.grown[:], total[:], ACT.Exp).then_inc(grown, 1)
                for t in range(TILES):
                    act.wait_ge(rows, t + 1)
                    nc.scalar.copy(o.gate[:, t], acc[:, t % 2]).then_inc(taken, 1)
                act.wait_ge(rows, TILES + 1)
                nc.scalar.copy(o.bonus[:], acc[:, 3, :TILES * RW_HEADS].rearrange("p (t h) -> p t h", t=TILES)).then_inc(taken, 1)

            @block.tensor
            def _(pe):
                pe.wait_ge(loaded, LOADS)
                pe.wait_ge(bent_done, 3)
                for c in range(RC):
                    if c:
                        pe.wait_ge(taken, 2 * c - 1)
                    nc.tensor.matmul(acc[:, 0], w2a2[:LORA, c * P:(c + 1) * P], bent[:LORA], start=True, stop=True).then_inc(sent, 1)
                    if c:
                        pe.wait_ge(taken, 2 * c)
                    nc.tensor.matmul(acc[:, 1], w2a2[LORA:, c * P:(c + 1) * P], bent[LORA:], start=True, stop=True).then_inc(sent, 1)
                for c in range(RC):
                    pe.wait_ge(squared, c + 1)
                    if c:
                        pe.wait_ge(rooted, c)
                    nc.tensor.matmul(acc[:, 2], pairs[:], tmp[:, c], start=True, stop=True).then_inc(sent, 1)
                pe.wait_ge(taken, 2 * RC)
                for t in range(TILES):
                    if t >= 2:
                        pe.wait_ge(taken, 2 * RC + t - 1)
                    nc.tensor.matmul(acc[:, t % 2], xm[:, G_AT, t * P:(t + 1) * P], g2[:], start=True, stop=True).then_inc(rows, 1)
                pe.wait_ge(ready, RC)
                for t in range(TILES):
                    for c in range(RC):
                        at = t * RW_HEADS + 2 * c
                        last = nc.tensor.matmul(acc[:, 3, at:at + 2], kk[:, c, t * P:(t + 1) * P], heads[:], start=True, stop=True)
                last.then_inc(rows, 1)

            @block.vector
            def _(dve):
                v = nc.vector
                steps = s.sem("steps")
                then = Chain(dve, steps)
                dve.wait_ge(loaded, LOADS)
                for n in range(N):
                    then(v.tensor_tensor(diff[:, 1:], p[:, n, :SEQ - 1], p[:, n, 1:], ALU.subtract))
                    then(v.tensor_scalar(diff[:, 0:1], p[:, n, 0:1], -1.0, None, ALU.mult))
                    v.scalar_tensor_tensor(xm[:, n], diff[:], mu[:, n:n + 1], p[:, n], ALU.mult, ALU.add).then_inc(mixed, 1)
                    dve.wait_ge(mixed, n + 1)
                for c in range(RC):
                    then(v.tensor_scalar(kk[:, c], xm[:, K_AT + c], col[:, KK, c:c + 1], None, ALU.mult))
                    v.tensor_tensor(tmp[:, c], kk[:, c], kk[:, c], ALU.mult).then_inc(squared, 1)
                dve.wait_ge(taken, 2 * RC)
                then(v.tensor_scalar(logd[:], logd[:], -math.exp(-0.5), None, ALU.mult))
                for c in range(RC):
                    then(v.tensor_tensor_scan(total[:, c], fresh[:], logd[:, c], 0.0, ALU.mult, ALU.add))
                v.tensor_tensor(logd[:], total[:], logd[:], ALU.subtract).then_inc(order, 2)
                for c in range(RC):
                    then(v.tensor_scalar(k2[:, c], a_[:, c], -1.0, col[:, KA, c:c + 1], ALU.add, ALU.mult))
                    then(v.scalar_tensor_tensor(k2[:, c], k2[:, c], 1.0, xm[:, K_AT + c], ALU.add, ALU.mult))
                dve.wait_ge(rooted, RC)
                then(v.tensor_scalar(tmp, tmp, 1e-12, None, ALU.max))
                then(v.reciprocal(tmp, tmp))
                then(v.tensor_tensor(kk[:], kk[:], tmp, ALU.mult))
                dve.wait_ge(grown, 3)
                then(v.scalar_tensor_tensor(o.alpha[:], o.alpha[:], -1.0, kk[:], ALU.mult, ALU.mult))
                then(v.tensor_tensor(tmp, kk[:], a_, ALU.mult))
                for c in range(RC):
                    v.scalar_tensor_tensor(kk[:, c], xm[:, R_AT + c], col[:, RK, c:c + 1], k2[:, c],
                                           ALU.mult, ALU.mult).then_inc(ready, 1)
                dve.wait_ge(ready, RC)
                then(v.tensor_tensor(o.kappa[:], k2[:], o.beta[:], ALU.mult))
                then(v.tensor_tensor(o.beta[:], o.beta[:], tmp, ALU.mult))
                then(v.tensor_tensor(o.rho[:], o.grown[:], xm[:, R_AT:R_AT + RC], ALU.mult))
                then(v.tensor_copy(o.value[:], xm[:, V_AT:V_AT + RC]))
def rwkv(nc, g, name, a, o, y):
    UNITS = TILES * RW_HEADS
    units = [(t, c, h) for t in range(TILES) for h in range(2) for c in range(RC)]
    cols = [slice((2 * c + h) * RW_DIM, (2 * c + h + 1) * RW_DIM) for _, c, h in units]
    feats = [slice(h * RW_DIM, (h + 1) * RW_DIM) for _, _, h in units]
    toks = [slice(t * P, (t + 1) * P) for t, _, _ in units]
    flat = lambda buf: buf.rearrange("p a n -> p (a n)")
    own = ExitStack()
    rows = {x: own.enter_context(nc.sbuf_tensor(f"{name}_{x}_rows", [P, TILES, RW], F32)) for x in ("alpha", "beta", "kappa", "value")}
    cols_of = {"alpha": o.alpha, "beta": o.beta, "kappa": o.kappa, "value": o.value}
    for x, buf in rows.items():
        turn_cols(nc, g, f"{name}_turn_{x}", cols_of[x], RC, [buf[:, t] for t in range(TILES)])
    solved = own.enter_context(nc.sbuf_tensor(f"{name}_solved", [P, UNITS, P], F32))
    inner = nc.dram_tensor(f"{name}_inner", [BLOCKS, UNITS, SPAN, SPAN], F32, kind="Internal").ap()
    outer = nc.dram_tensor(f"{name}_outer", [BLOCKS, UNITS, SPAN, SPAN], F32, kind="Internal").ap()

    with Stage(nc, f"{name}_solve") as s:
        masks = s.sb("masks", [P, 4, P])
        m_all = s.sb("m_all", [P, UNITS, P])
        m_rows, t_cols = s.sb("m_rows", [P, SPAN, SPAN]), s.sb("t_cols", [P, SPAN, SPAN])
        prod = flat(g.hT[:, :SPAN * SPAN // SEQ]).rearrange("p (s t) -> p s t", s=SPAN)
        acc = s.ps("acc", [P, 4, RC, P])
        loaded, zeroed, paired, masked = s.sem("loaded"), s.sem("zeroed"), s.sem("paired"), s.sem("masked")
        stored, spread, times, found, back, placed = (s.sem(x) for x in ("stored", "spread", "times", "found", "back", "placed"))
        with nc.Block() as block:
            @block.sync
            def _(sp):
                sp.dma_start(masks[:], a["masks"]).then_inc(loaded, 16)
                sp.wait_ge(masked, UNITS // RC)
                for b in range(BLOCKS):
                    part = slice(b * SPAN, (b + 1) * SPAN)
                    sp.dma_start(inner[b].rearrange("m t s -> t m s"), m_all[part, :, part]).then_inc(stored, 16)
                sp.wait_ge(stored, 16 * BLOCKS)
                sp.dma_start(m_rows[:], inner.rearrange("b m t s -> (b m) t s")).then_inc(spread, 16)
                sp.wait_ge(found, SPAN)
                sp.dma_start(outer.rearrange("b m s t -> (b m) s t"), t_cols[:]).then_inc(back, 16)
                sp.wait_ge(back, 16)
                sp.wait_ge(zeroed, 1)
                for b in range(BLOCKS):
                    part = slice(b * SPAN, (b + 1) * SPAN)
                    sp.dma_start(solved[part, :, part], outer[b].rearrange("m s t -> s m t")).then_inc(placed, 16)
                sp.wait_ge(placed, 16 * BLOCKS)

            @block.gpsimd
            def _(pool):
                nc.gpsimd.memset(solved[:], 0.0).then_inc(zeroed, 1)

            @block.tensor
            def _(pe):
                for m, (t, c, h) in enumerate(units):
                    n = m // RC
                    if n >= 4 and c == 0:
                        pe.wait_ge(masked, n - 3)
                    last = nc.tensor.matmul(acc[:, n % 4, c], o.alpha[feats[m], c, toks[m]], o.beta[feats[m], c, toks[m]],
                                            start=True, stop=True)
                    if c == RC - 1:
                        last.then_inc(paired, 1)

            @block.vector
            def _(dve):
                v = nc.vector
                dve.wait_ge(loaded, 16)
                for n in range(UNITS // RC):
                    dve.wait_ge(paired, n + 1)
                    v.tensor_tensor(m_all[:, n * RC:(n + 1) * RC], acc[:, n % 4], masks[:, 0].unsqueeze(1).to_broadcast([P, RC, P]),
                                    ALU.mult).then_inc(masked, 1)
                v.memset(t_cols[:], 0.0).then_inc(times, 1)
                dve.wait_ge(times, 1)
                v.memset(flat(t_cols[:])[:, ::SPAN + 1], 1.0).then_inc(found, 1)
                dve.wait_ge(spread, 16)
                for i in range(1, SPAN):
                    dve.wait_ge(found, i)
                    v.tensor_tensor(prod[:, :i, :i], t_cols[:, :i, :i], m_rows[:, i, :i].unsqueeze(1).to_broadcast([P, i, i]),
                                    ALU.mult).then_inc(times, 1)
                    dve.wait_ge(times, i + 1)
                    v.tensor_reduce(t_cols[:, :i, i], prod[:, :i, :i], AX, ALU.add).then_inc(found, 1)

    step = own.enter_context(nc.sbuf_tensor(f"{name}_step", [P, RC, SPANS, RW_DIM], F32))
    lead = g.hT[:, :RC]
    pieces = [flat(g.hT[:, RC:])[:, :SPANS * RW_DIM], flat(g.hT[:, RC:])[:, SPANS * RW_DIM:], g.mod[:, 0], g.mod[:, 1]]
    new = [x.rearrange("p (n v) -> p n v", n=SPANS) for x in pieces]
    with Stage(nc, f"{name}_spans") as s:
        masks, span = s.sb("masks", [P, 4, P]), s.sb("span", [P, BLOCKS])
        nef = s.sb("nef", [P, 2, 3, P])
        nv, pq = s.sb("nv", [P, 2, RW_DIM]), s.sb("pq", [P, 2, 2, RW_DIM])
        beta_in, value_in, q_in = (s.sb(x, [P, 2, BLOCKS, RW_DIM]) for x in ("beta_in", "value_in", "q_in"))
        pair, mid = s.ps("pair", [P, 2, BANK]), s.ps("mid", [P, 2, BANK])
        out, state = s.ps("out", [P, 2, BANK]), s.ps("state", [P, 2, 2, BLOCKS, RW_DIM])
        loaded, paired, masked, nv_done, nv_kept = (s.sem(x) for x in ("loaded", "paired", "masked", "nv_done", "nv_kept"))
        pq_done, pq_kept, spread, q_spread, out_done = (s.sem(x) for x in ("pq_done", "pq_kept", "spread", "q_spread", "out_done"))
        out_kept, row_kept, state_done, state_kept = (s.sem(x) for x in ("out_kept", "row_kept", "state_done", "state_kept"))
        with nc.Block() as block:
            @block.sync
            def _(sp):
                sp.dma_start(masks[:], a["masks"]).then_inc(loaded, 16)
                sp.dma_start(span[:], a["span"]).then_inc(loaded, 16)

            @block.gpsimd
            def _(pool):
                pool.wait_ge(loaded, 32)
                here = span[:].unsqueeze(2).to_broadcast([P, BLOCKS, RW_DIM])
                for m, (t, c, h) in enumerate(units):
                    if m >= 2:
                        pool.wait_ge(state_done, m - 1)
                    for src, dst in (("beta", beta_in), ("value", value_in)):
                        nc.gpsimd.tensor_tensor(dst[:, m % 2], rows[src][:, t, cols[m]].unsqueeze(1).to_broadcast([P, BLOCKS, RW_DIM]),
                                                here, ALU.mult).then_inc(spread, 1)

            @block.tensor
            def _(pe):
                def open_(m):
                    t, c, h = units[m]
                    if m >= 2:
                        pe.wait_ge(masked, m - 1)
                    for j, (left, right) in enumerate(((o.kappa, o.alpha), (o.beta, o.rho), (o.kappa, o.rho))):
                        last = nc.tensor.matmul(pair[:, m % 2, j * P:(j + 1) * P], left[feats[m], c, toks[m]],
                                                right[feats[m], c, toks[m]], start=True, stop=True)
                    last.then_inc(paired, 1)

                def solve(m):
                    t, c, h = units[m]
                    pe.wait_ge(masked, m + 1)
                    if m >= 2:
                        pe.wait_ge(pq_kept, m - 1)
                    nc.tensor.matmul(mid[:, m % 2, P:P + RW_DIM], solved[:, m], rows["alpha"][:, t, cols[m]], start=True, stop=True)
                    nc.tensor.matmul(mid[:, m % 2, :RW_DIM], nef[:, m % 2, 0], rows["value"][:, t, cols[m]],
                                     start=True, stop=True).then_inc(nv_done, 1)
                    pe.wait_ge(nv_kept, m + 1)
                    nc.tensor.matmul(mid[:, m % 2, P + RW_DIM:2 * P], solved[:, m], nv[:, m % 2], start=True, stop=True).then_inc(pq_done, 1)

                def close(m):
                    t, c, h = units[m]
                    pe.wait_ge(pq_kept, m + 1)
                    if m >= 2:
                        pe.wait_ge(out_kept, m - 1)
                        pe.wait_ge(row_kept, m - 1)
                    nc.tensor.matmul(out[feats[m], m % 2, :P], pq[:, m % 2, 0], nef[:, m % 2, 1], start=True, stop=True)
                    nc.tensor.matmul(out[:, m % 2, P:P + RW_DIM], nef[:, m % 2, 1], pq[:, m % 2, 1], start=True, stop=False)
                    nc.tensor.matmul(out[:, m % 2, P:P + RW_DIM], nef[:, m % 2, 2], rows["value"][:, t, cols[m]],
                                     start=False, stop=True).then_inc(out_done, 1)
                    pe.wait_ge(spread, 2 * m + 2)
                    pe.wait_ge(q_spread, m + 1)
                    if m >= 2:
                        pe.wait_ge(state_kept, 2 * (m - 1))
                    nc.tensor.matmul(state[feats[m], m % 2, 0], pq[:, m % 2, 0], beta_in[:, m % 2], start=True, stop=True)
                    nc.tensor.matmul(state[feats[m], m % 2, 1], rows["beta"][:, t, cols[m]], q_in[:, m % 2], start=True, stop=False)
                    nc.tensor.matmul(state[feats[m], m % 2, 1], rows["kappa"][:, t, cols[m]], value_in[:, m % 2],
                                     start=False, stop=True).then_inc(state_done, 1)

                pe.wait_ge(loaded, 32)
                open_(0)
                for m in range(UNITS):
                    if m + 1 < UNITS:
                        open_(m + 1)
                    solve(m)
                    close(m)

            @block.scalar
            def _(act):
                for m, (t, c, h) in enumerate(units):
                    act.wait_ge(nv_done, m + 1)
                    if m >= 2:
                        act.wait_ge(pq_done, m - 1)
                    nc.scalar.copy(nv[:, m % 2], mid[:, m % 2, :RW_DIM]).then_inc(nv_kept, 1)
                    act.wait_ge(pq_done, m + 1)
                    if m >= 2:
                        act.wait_ge(state_done, m - 1)
                        act.wait_ge(q_spread, m - 1)
                    nc.scalar.copy(pq[:, m % 2].rearrange("p a n -> p (a n)"), mid[:, m % 2, P:2 * P]).then_inc(pq_kept, 1)
                    act.wait_ge(out_kept, m + 1)
                    nc.scalar.copy(y[:, t, CONV + cols[m].start:CONV + cols[m].stop], out[:, m % 2, P:P + RW_DIM]).then_inc(row_kept, 1)

            @block.vector
            def _(dve):
                v = nc.vector

                def mask(m):
                    dve.wait_ge(paired, m + 1)
                    if m >= 2:
                        dve.wait_ge(out_done, m - 1)
                    v.tensor_tensor(nef[:, m % 2], pair[:, m % 2, :3 * P].rearrange("p (j n) -> p j n", j=3), masks[:, 1:],
                                    ALU.mult).then_inc(masked, 1)

                dve.wait_ge(loaded, 32)
                mask(0)
                for m, (t, c, h) in enumerate(units):
                    if m + 1 < UNITS:
                        mask(m + 1)
                    dve.wait_ge(pq_kept, m + 1)
                    if m >= 2:
                        dve.wait_ge(state_done, m - 1)
                    v.tensor_tensor(q_in[:, m % 2], pq[:, m % 2, 1].unsqueeze(1).to_broadcast([P, BLOCKS, RW_DIM]),
                                    span[:].unsqueeze(2).to_broadcast([P, BLOCKS, RW_DIM]), ALU.mult).then_inc(q_spread, 1)
                    dve.wait_ge(out_done, m + 1)
                    v.tensor_tensor(lead[feats[m], c, toks[m]], out[feats[m], m % 2, :P], o.rho[feats[m], c, toks[m]],
                                    ALU.add).then_inc(out_kept, 1)
                    dve.wait_ge(state_done, m + 1)
                    spans = slice(t * BLOCKS, (t + 1) * BLOCKS)
                    v.tensor_tensor(step[feats[m], c, spans], state[feats[m], m % 2, 0],
                                    g.ident[feats[m], feats[m]].unsqueeze(1).to_broadcast([RW_DIM, BLOCKS, RW_DIM]), ALU.add).then_inc(state_kept, 1)
                    ends = o.grown[feats[m], c, t * P + SPAN - 1:(t + 1) * P:SPAN]
                    v.tensor_tensor(new[c][feats[m], spans], state[feats[m], m % 2, 1],
                                    ends.unsqueeze(2).to_broadcast([RW_DIM, BLOCKS, RW_DIM]), ALU.mult).then_inc(state_kept, 1)

    z = [flat((o.alpha, o.beta)[c // 2][:])[:, (c % 2) * SPANS * RW_DIM:(c % 2 + 1) * SPANS * RW_DIM].rearrange(
        "p (n v) -> p n v", n=SPANS) for c in range(RC)]
    apart = [flat(b[:]).rearrange("p (n h v) -> p n h v", n=SPANS, h=2) for b in (o.kappa, o.rho, rows["alpha"], rows["beta"])]
    with Stage(nc, f"{name}_state") as s:
        heads = s.sb("heads", [P, 2])
        acc = s.ps("acc", [P, 2, 2, RC, RW_DIM])
        rest = s.ps("rest", [P, 2, BANK])
        loaded, moved, stepped, apart_done, inter, added = (s.sem(x) for x in ("loaded", "moved", "stepped", "apart_done", "inter", "added"))
        with nc.Block() as block:
            @block.sync
            def _(sp):
                sp.dma_start(heads[:], a["heads"]).then_inc(loaded, 16)

            @block.tensor
            def _(pe):
                for n in range(1, SPANS - 1):
                    pe.wait_ge(stepped, 2 * RC * n)
                    for c in range(RC):
                        for h in range(2):
                            f = slice(h * RW_DIM, (h + 1) * RW_DIM)
                            last = nc.tensor.matmul(acc[f, n % 2, h, c], step[f, c, n], z[c][f, n], start=True, stop=True)
                    last.then_inc(moved, 1)
                pe.wait_ge(apart_done, 2 * RC)
                for t in range(TILES):
                    if t >= 2:
                        pe.wait_ge(added, t - 1)
                    for b in range(BLOCKS):
                        for c in range(RC):
                            at = t * P + b * SPAN
                            last = nc.tensor.matmul(rest[b * SPAN:(b + 1) * SPAN, t % 2, c * P:(c + 1) * P], lead[:, c, at:at + SPAN],
                                                    apart[c][:, t * BLOCKS + b], start=True, stop=True)
                    last.then_inc(inter, 1)

            @block.vector
            def _(dve):
                v = nc.vector
                for c in range(RC):
                    v.memset(z[c][:, 0], 0.0).then_inc(stepped, 1)
                    v.tensor_copy(z[c][:, 1], new[c][:, 0]).then_inc(stepped, 1)
                for n in range(1, SPANS - 1):
                    dve.wait_ge(moved, n)
                    for c in range(RC):
                        for h in range(2):
                            f = slice(h * RW_DIM, (h + 1) * RW_DIM)
                            v.scalar_tensor_tensor(z[c][f, n + 1], acc[f, n % 2, h, c], o.grown[f, c, (n + 1) * SPAN - 1:(n + 1) * SPAN],
                                                   new[c][f, n], ALU.mult, ALU.add).then_inc(stepped, 1)
                dve.wait_ge(loaded, 16)
                dve.wait_ge(stepped, 2 * RC * (SPANS - 1))
                for c in range(RC):
                    for h in range(2):
                        v.tensor_scalar(apart[c][:, :, h], z[c], heads[:, h:h + 1], None, ALU.mult).then_inc(apart_done, 1)
                for t in range(TILES):
                    dve.wait_ge(inter, t + 1)
                    v.tensor_tensor(y[:, t, CONV:], y[:, t, CONV:], rest[:, t % 2], ALU.add).then_inc(added, 1)

    with Stage(nc, f"{name}_norm") as s:
        gain, shift = s.sb("gain", [P, RW]), s.sb("shift", [P, RW])
        square = s.sb("square", [P, 2, RW_HEADS, RW_DIM])
        mean, var, root = (s.sb(x, [P, TILES, RW_HEADS]) for x in ("mean", "var", "root"))
        loaded, order, rooted, ready = s.sem("loaded"), s.sem("order"), s.sem("rooted"), s.sem("ready")
        wide = [P, RW_HEADS, RW_DIM]
        with nc.Block() as block:
            @block.sync
            def _(sp):
                sp.dma_start(gain[:], a["rw_gain"]).then_inc(loaded, 16)
                sp.dma_start(shift[:], a["rw_shift"]).then_inc(loaded, 16)

            @block.scalar
            def _(act):
                act.wait_ge(ready, 1)
                nc.scalar.activation(root[:], var[:], ACT.Sqrt).then_inc(rooted, 1)

            @block.vector
            def _(dve):
                v = nc.vector
                then = Chain(dve, order)
                part = lambda buf, t: buf[:, t].rearrange("p (h d) -> p h d", d=RW_DIM)
                ys = [y[:, t, CONV:].rearrange("p (h d) -> p h d", d=RW_DIM) for t in range(TILES)]
                for t in range(TILES):
                    then(v.tensor_reduce(mean[:, t], ys[t], AX, ALU.add))
                then(v.tensor_scalar(mean[:], mean[:], 1.0 / RW_DIM, None, ALU.mult))
                for t in range(TILES):
                    then(v.tensor_tensor(ys[t], ys[t], mean[:, t].unsqueeze(2).to_broadcast(wide), ALU.subtract))
                    then(v.tensor_tensor(square[:, t % 2], ys[t], ys[t], ALU.mult))
                    then(v.tensor_reduce(var[:, t], square[:, t % 2], AX, ALU.add))
                v.tensor_scalar(var[:], var[:], 1.0 / RW_DIM, GN_EPS, ALU.mult, ALU.add).then_inc(ready, 1)
                dve.wait_ge(rooted, 1)
                then(v.reciprocal(var[:], root[:]))
                dve.wait_ge(loaded, 32)
                for t in range(TILES):
                    then(v.tensor_tensor(ys[t], ys[t], var[:, t].unsqueeze(2).to_broadcast(wide), ALU.mult))
                    then(v.tensor_tensor(y[:, t, CONV:], y[:, t, CONV:], gain[:], ALU.mult))
                    then(v.tensor_tensor(y[:, t, CONV:], y[:, t, CONV:], shift[:], ALU.add))
                    then(v.tensor_tensor(square[:, t % 2], part(rows["value"], t), o.bonus[:, t].unsqueeze(2).to_broadcast(wide), ALU.mult))
                    then(v.tensor_tensor(ys[t], ys[t], square[:, t % 2], ALU.add))
                    then(v.tensor_tensor(y[:, t, CONV:], y[:, t, CONV:], o.gate[:, t], ALU.mult))
    own.close()


def layer_norm_rows(nc, g, name, g_dram, b_dram):
    with Stage(nc, name) as s:
        gain, shift = s.sb("gain", [P, D]), s.sb("shift", [P, D])
        stat, ms = s.sb("stat", [P, TILES, 2, 6]), s.sb("ms", [P, TILES, 2])
        root, rstd = s.sb("root", [P, TILES]), s.sb("rstd", [P, TILES])
        loaded, order, rooted, ready = s.sem("loaded"), s.sem("order"), s.sem("rooted"), s.sem("ready")
        with nc.Block() as block:
            @block.sync
            def _(sp):
                sp.dma_start(gain[:], g_dram).then_inc(loaded, 16)
                sp.dma_start(shift[:], b_dram).then_inc(loaded, 16)

            @block.scalar
            def _(act):
                act.wait_ge(ready, 1)
                nc.scalar.activation(root[:], rstd[:], ACT.Sqrt).then_inc(rooted, 1)

            @block.vector
            def _(dve):
                then = Chain(dve, order)
                v = nc.vector
                for t in range(TILES):
                    for half in range(2):
                        then(v.bn_stats(stat[:, t, half], g.x[:, t, half * D // 2:(half + 1) * D // 2]))
                    then(v.bn_aggr(ms[:, t], stat[:, t]))
                v.tensor_scalar(rstd[:], ms[:, :, 1], LN_EPS, None, ALU.add).then_inc(ready, 1)
                dve.wait_ge(rooted, 1)
                then(v.reciprocal(rstd[:], root[:]))
                dve.wait_ge(loaded, 32)
                for t in range(TILES):
                    then(v.tensor_scalar(g.x[:, t], g.x[:, t], ms[:, t, 0:1], rstd[:, t:t + 1], ALU.subtract, ALU.mult))
                    then(v.tensor_tensor(g.x[:, t], g.x[:, t], gain[:], ALU.mult))
                    then(v.tensor_tensor(g.x[:, t], g.x[:, t], shift[:], ALU.add))
KEYS, TOP, PEER_HEADS = 128, 16, 8
PICKS = PEER_HEADS * TOP
PART = 32
SET = 4


def top16(then, v, values, work, at):
    then(v.max(values[:, :8], work))
    then(v.max_index(at[:, :8], values[:, :8], work))
    then(v.match_replace(work, values[:, :8], work, NEG))
    then(v.max(values[:, 8:], work))
    then(v.max_index(at[:, 8:], values[:, 8:], work))


def peer_pick(nc, g, name, qT, keys_dram, picks):
    with Stage(nc, name) as s:
        keys = s.sb("keys", [P, 2 * PEER_HEADS, KEYS])
        score = s.sb("score", [P, 2, 4, KEYS])
        value, at = s.sb("value", [P, 2 * PEER_HEADS, TOP]), s.sb("at", [P, 2 * PEER_HEADS, TOP], U32)
        key = s.sb("key", [P, 2 * PEER_HEADS, TOP])
        both = s.sb("both", [P, TOP, TOP])
        best, place = s.sb("best", [P, PEER_HEADS, TOP]), s.sb("place", [P, PEER_HEADS, TOP], U32)
        half_at, half = s.sb("half_at", [P, PEER_HEADS, TOP], U32), s.sb("half", [P, PEER_HEADS, TOP])
        match = s.sb("match", [P, PEER_HEADS, TOP, TOP])
        low, raised = s.sb("low", [P, PEER_HEADS, TOP]), s.sb("raised", [P, 2, PEER_HEADS, TOP])
        total, inv = s.sb("total", [P, PEER_HEADS]), s.sb("inv", [P, PEER_HEADS])
        found = s.sb("found", [P, 2, 3, PICKS])
        acc, pt = s.ps("acc", [P, 2, 4, KEYS]), s.ps("pt", [P, 2, 3, P])
        loaded, scored, kept, order, used = (s.sem(x) for x in ("loaded", "scored", "kept", "order", "used"))
        low_done, raised_done, picked, turned, stored = (s.sem(x) for x in ("low_done", "raised_done", "picked", "turned", "stored"))
        SETS = 2 * PEER_HEADS // 4
        wide = [P, PEER_HEADS, TOP, TOP]
        with nc.Block() as block:
            @block.sync
            def _(sp):
                sp.dma_start(keys[:], keys_dram).then_inc(loaded, 16)

            @block.tensor
            def _(pe):
                def score_tile(t):
                    for q in range(SETS):
                        n = t * SETS + q
                        if n >= 2:
                            pe.wait_ge(kept, n - 1)
                        for j in range(4):
                            last = nc.tensor.matmul(acc[:, n % 2, j], qT[:, 4 * q + j, t * P:(t + 1) * P], keys[:, 4 * q + j],
                                                    start=True, stop=True)
                        last.then_inc(scored, 1)

                def turn(t):
                    pe.wait_ge(picked, t + 1)
                    if t >= 2:
                        pe.wait_ge(stored, t - 1)
                    for j in range(3):
                        last = nc.tensor.transpose(pt[:, t % 2, j], found[:, t % 2, j], g.ident[:])
                    last.then_inc(turned, 1)

                pe.wait_ge(loaded, 16)
                for t in range(TILES):
                    score_tile(t)
                    if t:
                        turn(t - 1)
                turn(TILES - 1)

            @block.scalar
            def _(act):
                for t in range(TILES):
                    for q in range(SETS):
                        n = t * SETS + q
                        act.wait_ge(scored, n + 1)
                        if n >= 2:
                            act.wait_ge(used, n - 1)
                        nc.scalar.copy(score[:, n % 2], acc[:, n % 2]).then_inc(kept, 1)
                    if t:
                        act.wait_ge(turned, t)
                        nc.scalar.copy(picks[:, :, (t - 1) * P:t * P], pt[:, (t - 1) % 2]).then_inc(stored, 1)
                    act.wait_ge(low_done, t + 1)
                    nc.scalar.activation(raised[:, t % 2], low[:], ACT.Exp).then_inc(raised_done, 1)
                act.wait_ge(turned, TILES)
                nc.scalar.copy(picks[:, :, (TILES - 1) * P:], pt[:, (TILES - 1) % 2]).then_inc(stored, 1)

            @block.vector
            def _(dve):
                v = nc.vector
                then = Chain(dve, order)
                for t in range(TILES):
                    for q in range(SETS):
                        n = t * SETS + q
                        dve.wait_ge(kept, n + 1)
                        for j in range(4):
                            top16(then, v, value[:, 4 * q + j], score[:, n % 2, j], at[:, 4 * q + j])
                        dve.sem_inc(used, 1)
                    then(v.tensor_copy(key[:], at[:]))
                    for h in range(PEER_HEADS):
                        then(v.tensor_tensor(both[:], value[:, 2 * h].unsqueeze(2).to_broadcast([P, TOP, TOP]),
                                             value[:, 2 * h + 1].unsqueeze(1).to_broadcast([P, TOP, TOP]), ALU.add))
                        top16(then, v, best[:, h], both[:].rearrange("p a b -> p (a b)"), place[:, h])
                    if t:
                        dve.wait_ge(raised_done, t)
                    v.tensor_tensor(low[:], best[:], best[:, :, 0:1].to_broadcast([P, PEER_HEADS, TOP]), ALU.subtract).then_inc(low_done, 1)
                    if t >= 2:
                        dve.wait_ge(turned, t - 1)
                    for j, (op, n) in enumerate(((ALU.logical_shift_right, 4), (ALU.bitwise_and, TOP - 1))):
                        then(v.tensor_scalar(half_at[:], place[:], n, None, op))
                        then(v.tensor_copy(half[:], half_at[:]))
                        for h in range(PEER_HEADS):
                            then(v.tensor_tensor(match[:, h], half[:, h].unsqueeze(2).to_broadcast([P, TOP, TOP]),
                                                 g.iota[:, :TOP].unsqueeze(1).to_broadcast([P, TOP, TOP]), ALU.is_equal))
                            then(v.tensor_tensor(match[:, h], match[:, h], key[:, 2 * h + j].unsqueeze(1).to_broadcast([P, TOP, TOP]),
                                                 ALU.mult))
                        then(v.tensor_reduce(found[:, t % 2, j].rearrange("p (h k) -> p h k", h=PEER_HEADS), match[:], AX, ALU.add))
                    dve.wait_ge(raised_done, t + 1)
                    then(v.tensor_reduce(total[:], raised[:, t % 2], AX, ALU.add))
                    then(v.reciprocal(inv[:], total[:]))
                    v.tensor_tensor(found[:, t % 2, 2].rearrange("p (h k) -> p h k", h=PEER_HEADS), raised[:, t % 2],
                                    inv[:].unsqueeze(2).to_broadcast([P, PEER_HEADS, TOP]), ALU.mult).then_inc(picked, 1)


def peer_weights(nc, g, name, picks, part, weights):
    GROUP = 8
    with Stage(nc, name) as s:
        first = s.sb("first", [P, 2, GROUP, KEYS])
        second = s.sb("second", [P, 2, GROUP, PART])
        acc = s.ps("acc", [P, 2, BANK])
        matched, first_made, second_made = s.sem("matched"), s.sem("first_made"), s.sem("second_made")
        summed, kept = s.sem("summed"), s.sem("kept")
        LOOPS = SEQ // (2 * GROUP)
        with nc.Block() as block:
            def spread(n, j, width):
                return picks[:, j, bass.ds(n * GROUP, GROUP)].unsqueeze(2).to_broadcast([P, GROUP, width])

            @block.vector
            def _(dve):
                with dve.Fori(0, LOOPS) as i:
                    for u in range(2):
                        n = 2 * i + u
                        dve.wait_ge(summed, n + 1)
                        nc.vector.tensor_tensor(first[:, u], g.iota[:].unsqueeze(1).to_broadcast([P, GROUP, KEYS]),
                                                spread(n, 0, KEYS), ALU.is_equal).then_inc(first_made, 1)
                        nc.vector.tensor_tensor(second[:, u], g.iota[:, part * PART:(part + 1) * PART].unsqueeze(1).to_broadcast(
                            [P, GROUP, PART]), spread(n, 1, PART), ALU.is_equal).then_inc(matched, 1)
                        dve.wait_ge(matched, n + 1)
                        nc.vector.tensor_tensor(second[:, u], second[:, u], spread(n, 2, PART), ALU.mult).then_inc(second_made, 1)

            @block.tensor
            def _(pe):
                pe.sem_inc(summed, 2)
                with pe.Fori(0, LOOPS) as i:
                    for u in range(2):
                        n = 2 * i + u
                        pe.wait_ge(first_made, n + 1)
                        pe.wait_ge(second_made, n + 1)
                        pe.wait_ge(kept, n + 1)
                        for j in range(GROUP):
                            last = nc.tensor.matmul(acc[:, u, j * PART:(j + 1) * PART], first[:, u, j], second[:, u, j],
                                                    start=True, stop=True)
                        last.then_inc(summed, 1)

            @block.scalar
            def _(act):
                act.sem_inc(kept, 2)
                with act.Fori(0, LOOPS) as i:
                    for u in range(2):
                        n = 2 * i + u
                        act.wait_ge(summed, n + 3)
                        nc.scalar.copy(weights[:, bass.ds(n * GROUP, GROUP), :],
                                       acc[:, u, :GROUP * PART].rearrange("p (t j) -> p t j", t=GROUP)).then_inc(kept, 1)


def peer_part(nc, g, name, u_dram, v_dram, part, weights, acc):
    SETS, HALVES, BANKS = PART // SET, D // BANK, 4
    OUTS = TILES * HALVES
    with Stage(nc, name) as s:
        w_u, w_v = s.sb("w_u", [P, SET, KD, P]), s.sb("w_v", [P, 2, SET, D])
        bent = s.sb("bent", [P, 2, SET, SEQ])
        risen, low = s.ps("risen", [P, SET, SEQ]), s.ps("low", [P, BANKS, BANK])
        u_in = [s.sem(f"u_in{c}") for c in range(SET)]
        v_in = [s.sem(f"v_in{u}") for u in range(2)]
        lifted, bent_done, made = s.sem("lifted"), s.sem("bent_done"), s.sem("made")
        lowered, added = s.sem("lowered"), s.sem("added")
        first = part * PART
        with nc.Block() as block:
            @block.sync
            def _(sp):
                def load_u(n, c):
                    src = u_dram[first + c] if isinstance(n, int) else u_dram[bass.ds(first + SET * n + c, 1)].rearrange("o p k n -> p (o k) n")
                    sp.dma_start(w_u[:, c], src).then_inc(u_in[c], 16)

                def load_v(n, u):
                    at = first + SET * n
                    src = v_dram[at:at + SET] if isinstance(n, int) else v_dram[bass.ds(at, SET)]
                    sp.dma_start(w_v[:, u], src.rearrange("c p d -> p c d")).then_inc(v_in[u], 16)

                for c in range(SET):
                    load_u(0, c)
                load_v(0, 0)
                load_v(1, 1)
                with sp.Fori(0, SETS - 1) as n:
                    for c in range(SET):
                        sp.wait_ge(lifted, SET * n + c + 1)
                        load_u(n + 1, c)

            @block.tensor
            def _(pe):
                def lift(n):
                    for c in range(SET):
                        pe.wait_ge(u_in[c], 16 * n + 16)
                        pe.wait_ge(made, SET * n + c + 1)
                        for k in range(KD):
                            last = nc.tensor.matmul(risen[:, c], w_u[:, c, k], g.hT[:, k], start=(k == 0), stop=(k == KD - 1))
                        last.then_inc(lifted, 1)

                def lower(n, u):
                    pe.wait_ge(v_in[u], 8 * (n - u) + 16)
                    pe.wait_ge(made, SET * n + 2 * SET)
                    for m in range(OUTS):
                        t, half = m // HALVES, m % HALVES
                        pe.wait_ge(added, OUTS * n + m + 1)
                        for c in range(SET):
                            last = nc.tensor.matmul(low[:, m % BANKS], bent[:, u, c, t * P:(t + 1) * P],
                                                    w_v[:, u, c, half * BANK:(half + 1) * BANK], start=(c == 0), stop=(c == SET - 1))
                        last.then_inc(lowered, 1)

                pe.sem_inc(lowered, 2 * OUTS)
                lift(0)
                with pe.Fori(0, SETS // 2 - 1) as i:
                    lift(2 * i + 1)
                    lower(2 * i, 0)
                    lift(2 * i + 2)
                    lower(2 * i + 1, 1)
                lift(SETS - 1)
                lower(SETS - 2, 0)
                lower(SETS - 1, 1)

            @block.scalar
            def _(act):
                def bend(n, u):
                    act.wait_ge(lowered, OUTS * n + OUTS)
                    for c in range(SET):
                        act.wait_ge(lifted, SET * n + c + 1)
                        nc.scalar.activation(bent[:, u, c], risen[:, c], ACT.Gelu).then_inc(bent_done, 1)

                bend(0, 0)
                with act.Fori(0, SETS // 2 - 1) as i:
                    for u in range(2):
                        n = 2 * i + u
                        bend(n + 1, 1 - u)
                        act.wait_ge(lowered, OUTS * n + OUTS + 2 * OUTS)
                        act.dma_start(w_v[:, u], v_dram[bass.ds(first + SET * (n + 2), SET)].rearrange(
                            "c p d -> p c d")).then_inc(v_in[u], 16)
                bend(SETS - 1, 1)

            @block.vector
            def _(dve):
                def make(n, u):
                    for c in range(SET):
                        dve.wait_ge(bent_done, SET * n + c + 1)
                        at = n * SET + c
                        here = weights[:, :, at] if isinstance(n, int) else weights[:, :, bass.ds(at, 1)].rearrange("p t o -> p (t o)")
                        nc.vector.tensor_tensor(bent[:, u, c], bent[:, u, c], here, ALU.mult).then_inc(made, 1)

                def add(n):
                    dve.wait_ge(added, OUTS * n + BANKS)
                    for m in range(OUTS):
                        t, half = m // HALVES, m % HALVES
                        dve.wait_ge(lowered, OUTS * n + m + 1 + 2 * OUTS)
                        nc.vector.tensor_tensor(acc[:, t, half], low[:, m % BANKS], acc[:, t, half], ALU.add).then_inc(added, 1)

                dve.sem_inc(made, SET)
                dve.sem_inc(added, BANKS)
                make(0, 0)
                with dve.Fori(0, SETS // 2 - 1) as i:
                    make(2 * i + 1, 1)
                    add(2 * i)
                    make(2 * i + 2, 0)
                    add(2 * i + 1)
                make(SETS - 1, 1)
                add(SETS - 2)
                add(SETS - 1)


def peer(nc, g, name, a):
    picks_ctx = nc.sbuf_tensor(f"{name}_picks", [P, 3, SEQ], F32)
    with picks_ctx as picks:
        with nc.sbuf_tensor(f"{name}_qT", [P, 2 * PEER_HEADS, SEQ], F32) as qT:
            project_cols(nc, f"{name}_q", g.hT, KD, a["peer_wq"], 2 * PEER_HEADS, qT)
            peer_pick(nc, g, f"{name}_pick", qT, a["peer_keys"], picks)
        acc = g.mod[:, 0:TILES].rearrange("p t (h n) -> p t h n", n=BANK)
        with Stage(nc, f"{name}_zero") as s:
            zeroed = s.sem("zeroed")
            with nc.Block() as block:
                @block.vector
                def _(dve):
                    nc.vector.memset(acc, 0.0).then_inc(zeroed, 1)
        with nc.sbuf_tensor(f"{name}_weights", [P, SEQ, PART], F32) as weights:
            for part in range(KEYS // PART):
                peer_weights(nc, g, f"{name}_weights{part}", picks, part, weights)
                peer_part(nc, g, f"{name}_part{part}", a["peer_u"], a["peer_v"], part, weights, acc)
        with Stage(nc, f"{name}_sum") as s:
            gated, added = s.sem("gated"), s.sem("added")
            with nc.Block() as block:
                @block.vector
                def _(dve):
                    for t in range(TILES):
                        rows = g.mod[:, t]
                        nc.vector.tensor_tensor(rows, rows, g.mod[:, 5], ALU.mult).then_inc(gated, 1)
                        dve.wait_ge(gated, t + 1)
                        nc.vector.scalar_tensor_tensor(g.x[:, t], g.x[:, t], ALPHA, rows, ALU.mult, ALU.add).then_inc(added, 1)
def build_program(nc, a, out):
    with ExitStack() as own:
        def sb(name, shape, dtype=F32):
            return own.enter_context(nc.sbuf_tensor(name, shape, dtype))

        g = Global()
        g.x = sb("x", [P, TILES, D])
        g.hT = sb("hT", [P, KD, SEQ])
        g.mod = sb("mod", [P, 6, D])
        g.ident, g.causal, g.iota = sb("ident", [P, P]), sb("causal", [P, P]), sb("iota", [P, P])
        g.comb = sb("comb", [P, TILES, EXPERTS])
        constants(nc, a, g)

        modulation(nc, g, "ada0", a["c"], a["w_ada"][0], a["b_ada"][0:1])
        normed(nc, g, "fox_norm", "rms", 1, 0, a["mix_gain"][0])
        fox(nc, g, a)
        moe(nc, g, a, 0)

        modulation(nc, g, "ada1", a["c"], a["w_ada"][1], a["b_ada"][1:2])
        normed(nc, g, "mla_norm", "rms", 1, 0, a["mix_gain"][1])
        mla(nc, g, a)
        moe(nc, g, a, 1)

        modulation(nc, g, "cond", a["c_2"], a["cond_w"], a["cond_b"])
        normed(nc, g, "hybrid_norm", "ln", 1, 0)
        hybrid(nc, g, a)
        layer_norm_rows(nc, g, "ln1", a["ln1_g"], a["ln1_b"])
        normed(nc, g, "peer_norm", "ln", 4, 3)
        peer(nc, g, "peer", a)
        layer_norm_rows(nc, g, "ln2", a["ln2_g"], a["ln2_b"])

        with Stage(nc, "store") as s:
            stored = s.sem("stored")
            with nc.Block() as block:
                @block.sync
                def _(sp):
                    sp.dma_start(out.rearrange("o (t p) d -> p (o t) d", p=P), g.x[:]).then_inc(stored, 16)
                    sp.wait_ge(stored, 16)


class Global:
    pass


def fox(nc, g, a):
    with ExitStack() as own:
        qkv = own.enter_context(nc.sbuf_tensor("fox_qkv", [P, TILES, 3 * D], F32))
        o = own.enter_context(nc.sbuf_tensor("fox_o", [P, TILES, D], F32))
        cum_q = own.enter_context(nc.sbuf_tensor("fox_cum_q", [P, TILES, HEADS], F32))
        cum_k = own.enter_context(nc.sbuf_tensor("fox_cum_k", [P, HEADS, SEQ], F32))
        sums = nc.dram_tensor("fox_sums", [HEADS, SEQ], F32, kind="Internal").ap()
        q, k, v = (qkv[:, :, j * D:(j + 1) * D] for j in range(3))
        project_rows(nc, "fox_in", g.hT, KD, a["fox_w_in"], 6, BANK, keep=qkv)
        forget_gates(nc, g, "fox_gates", a["fox_w_f"], a["fox_b_f"], sums, cum_q, cum_k)
        head_norms(nc, "fox_heads", [(q, a["fox_q_norm"], FOX_DK ** -0.5), (k, a["fox_k_norm"], 1.0)], FOX_DK)
        attention(nc, g, "fox_attn", q, k, v, o, FOX_DK, cum_q=cum_q, cum_k=cum_k)
        turn_rows(nc, g, "fox_turn", o, KD, g.hT)
        project_rows(nc, "fox_out", g.hT, KD, a["fox_w_out"], 2, BANK, gate=g.mod[:, 2], x=g.x)


def mla(nc, g, a):
    with ExitStack() as own:
        def sb(name, shape):
            return own.enter_context(nc.sbuf_tensor(f"mla_{name}", shape, F32))

        q, k, kv = sb("q", [P, TILES, HEADS * QK]), sb("k", [P, TILES, HEADS * QK]), sb("kv", [P, TILES, HEADS * (NOPE + DV)])
        low, o = sb("low", [P, TILES, Q_RANK + KV_RANK + ROPE]), sb("o", [P, TILES, HEADS * DV])
        cos, sin = sb("cos", [P, TILES, ROPE // 2]), sb("sin", [P, TILES, ROPE // 2])
        kq, kkv = Q_RANK // P, KV_RANK // P
        project_rows(nc, "mla_in", g.hT, KD, a["mla_w_in"], 2, (Q_RANK + KV_RANK + ROPE) // 2, keep=low)
        head_norms(nc, "mla_q_lat", [(low[:, :, :Q_RANK], a["mla_q_lat"], 1.0)], Q_RANK, heads=1)
        head_norms(nc, "mla_kv_lat", [(low[:, :, Q_RANK:Q_RANK + KV_RANK], a["mla_kv_lat"], 1.0)], KV_RANK, heads=1)
        turn_rows(nc, g, "mla_turn_low", low, kq + kkv, g.hT)
        project_rows(nc, "mla_uq", g.hT[:, :kq], kq, a["mla_w_uq"], 4, HEADS * QK // 4, keep=q)
        project_rows(nc, "mla_ukv", g.hT[:, kq:kq + kkv], kkv, a["mla_w_ukv"], 4, BANK, keep=kv)
        split_latents(nc, g, "mla_split", kv, low[:, :, Q_RANK + KV_RANK:], a["positions"], a["freq"], k, cos, sin)
        head_norms(nc, "mla_heads", [(q, a["mla_q_norm"], QK ** -0.5), (k, a["mla_k_norm"], 1.0)], QK)
        rotate(nc, "mla_rotate", (q, k), cos, sin)
        attention(nc, g, "mla_attn", q, k, kv, o, QK, v_step=NOPE + DV, v_at=NOPE)
        turn_rows(nc, g, "mla_turn", o, KD, g.hT)
        project_rows(nc, "mla_out", g.hT, KD, a["mla_w_out"], 2, BANK, gate=g.mod[:, 2], x=g.x)


def moe(nc, g, a, layer):
    normed(nc, g, f"moe_norm{layer}", "rms", 4, 3, a["ffn_gain"][layer])
    route(nc, g, f"moe_route{layer}", a["moe_w_route"][layer], a["moe_b_route"][layer])
    experts(nc, g, f"moe{layer}", a["moe_gate"][layer], a["moe_up"][layer], a["moe_down"][layer], g.mod[:, 5])


def hybrid(nc, g, a):
    with ExitStack() as own:
        y = own.enter_context(nc.sbuf_tensor("hybrid_y", [P, TILES, D], F32))
        o = Global()
        o.alpha, o.beta, o.kappa, o.rho, o.grown, o.value = (
            own.enter_context(nc.sbuf_tensor(f"rw_{x}", [P, RC, SEQ], F32))
            for x in ("alpha", "beta", "kappa", "rho", "grown", "value"))
        o.gate = own.enter_context(nc.sbuf_tensor("rw_gate", [P, TILES, RW], F32))
        o.bonus = own.enter_context(nc.sbuf_tensor("rw_bonus", [P, TILES, RW_HEADS], F32))
        with nc.sbuf_tensor("hybrid_pT", [P, IN_CHUNKS, SEQ], F32) as pT:
            project_cols(nc, "hybrid_in", g.hT, KD, a["w_in"], IN_CHUNKS, pT)
            with nc.sbuf_tensor("conv_cols", [P, CC, SEQ], F32) as conv, nc.sbuf_tensor("conv_rows", [P, TILES, CONV], F32) as conv_rows:
                gated_conv(nc, g, "conv", pT, a["conv_w"], a["conv_b"], conv)
                turn_cols(nc, g, "conv_turn", conv, CC, [conv_rows[:, t] for t in range(TILES)])
                conv_norm(nc, g, "conv_norm", conv_rows, a["conv_gain"], a["conv_shift"], y)
            rwkv_inputs(nc, g, "rw_in", a, pT, o)
        rwkv(nc, g, "rw", a, o, y)
        turn_rows(nc, g, "hybrid_turn", y, KD, g.hT)
        project_rows(nc, "hybrid_out", g.hT, KD, a["w_out"], 2, BANK, gate=g.mod[:, 2], x=g.x, alpha=ALPHA)




def row_chunks(w, width):
    k, n = w.shape
    return w.reshape(k // P, P, n // width, width).transpose(2, 1, 0, 3)


def in_columns(v):
    return v.reshape(-1, P).T


def everywhere(v):
    return np.broadcast_to(v[..., None, :], v.shape[:-1] + (P, v.shape[-1]))


def shape_constants():
    i = np.arange(P)
    same = i[:, None] // SPAN == i[None] // SPAN
    before, upto = i[:, None] < i[None], i[:, None] <= i[None]
    half = ROPE // 2
    return {
        "ident": np.eye(P),
        "causal": np.where(i[None] <= i[:, None], 0.0, NEG),
        "iota": np.broadcast_to(np.arange(P), (P, P)),
        "freq": everywhere(np.float32(10000.0) ** (-np.arange(half, dtype=np.float32) / np.float32(half))),
        "masks": np.stack([same & before.T, same & before, same & upto, same & upto], 1),
        "span": i[:, None] // SPAN == np.arange(BLOCKS)[None],
        "pairs": i[:, None] // RW_DIM == i[None] // RW_DIM,
        "heads": i[:, None] // RW_DIM == np.arange(2)[None],
        "fresh": np.broadcast_to(np.arange(SEQ) % SPAN != 0, (P, SEQ)),
    }


def laid_out(x):
    fox_w = x["fox_w_in"][0]
    route_w = np.concatenate([x["moe_w_grp"], x["moe_w_rt"]], 2)
    route_b = np.concatenate([x["moe_b_grp"], x["moe_b_rt"]], 1)
    layers = route_w.shape[0]

    def raising(w):
        return w.reshape(layers, EXPERTS, KD, P, D_EXPERT).transpose(0, 1, 3, 2, 4)

    return {
        "x": x["x"],
        "c": in_columns(x["c"][0]), "c_2": in_columns(x["c_2"][0]),
        "positions": in_columns(x["positions"][0]),
        "w_ada": np.stack([row_chunks(w, BANK) for w in x["w_ada"]]), "b_ada": x["b_ada"],
        "cond_w": row_chunks(x["cond_w_2"], BANK), "cond_b": x["cond_b_2"][None],
        "mix_gain": everywhere(x["mix_norm"]), "ffn_gain": everywhere(x["ffn_norm"]),
        "fox_w_in": row_chunks(fox_w[:, :3 * D], BANK),
        "fox_w_f": fox_w[:, 3 * D:].reshape(KD, P, HEADS).transpose(1, 0, 2),
        "fox_b_f": x["fox_b_f"][0][:, None],
        "fox_q_norm": everywhere(x["fox_q_norm"][0]), "fox_k_norm": everywhere(x["fox_k_norm"][0]),
        "fox_w_out": row_chunks(x["fox_w_out"][0], BANK),
        "mla_w_in": row_chunks(x["mla_w_in"][0], (Q_RANK + KV_RANK + ROPE) // 2),
        "mla_q_lat": everywhere(x["mla_q_lat_norm"][0]), "mla_kv_lat": everywhere(x["mla_kv_lat_norm"][0]),
        "mla_w_uq": row_chunks(x["mla_w_uq"][0], HEADS * QK // 4), "mla_w_ukv": row_chunks(x["mla_w_ukv"][0], BANK),
        "mla_q_norm": everywhere(x["mla_q_norm"][0]), "mla_k_norm": everywhere(x["mla_k_norm"][0]),
        "mla_w_out": row_chunks(x["mla_w_out"][0], BANK),
        "moe_w_route": route_w.reshape(layers, KD, P, -1).transpose(0, 2, 1, 3), "moe_b_route": everywhere(route_b),
        "moe_gate": raising(x["moe_w_gate"]), "moe_up": raising(x["moe_w_up"]),
        "moe_down": x["moe_w_down"].reshape(layers, EXPERTS, D_EXPERT // P, P, D).transpose(0, 1, 3, 2, 4),
        "w_in": row_chunks(x["w_in_2"], P), "mu": in_columns(x["mu_shift_2"]),
        "conv_w": x["conv_w_2"].T.reshape(CC, P, TAPS).transpose(1, 0, 2), "conv_b": in_columns(x["conv_b_2"]),
        "conv_gain": everywhere(x["conv_ln_g_2"]), "conv_shift": everywhere(x["conv_ln_b_2"]),
        "rw_col": np.stack([in_columns(x[n].reshape(-1)) for n in ("rw_w0_2", "rw_a0_2", "rw_kk_2", "rw_ka_2", "rw_rk_2")], 1),
        "w2a2": np.concatenate([x["rw_w2_2"], x["rw_a2_2"]], 0), "rw_g2": x["rw_g2_2"],
        "rw_gain": everywhere(x["rw_lnx_g_2"]), "rw_shift": everywhere(x["rw_lnx_b_2"]),
        "w_out": row_chunks(x["w_out_2"], BANK),
        "ln1_g": everywhere(x["ln1_g_2"]), "ln1_b": everywhere(x["ln1_b_2"]),
        "ln2_g": everywhere(x["ln2_g_2"]), "ln2_b": everywhere(x["ln2_b_2"]),
        "peer_wq": row_chunks(x["peer_wq_2"], P),
        "peer_keys": np.stack([x["peer_k1_2"], x["peer_k2_2"]], 1).reshape(2 * PEER_HEADS, KEYS, P).transpose(2, 0, 1),
        "peer_u": x["peer_u_2"].reshape(KEYS, KEYS, KD, P).transpose(1, 3, 2, 0),
        "peer_v": x["peer_v_2"].reshape(KEYS, KEYS, D).transpose(1, 0, 2),
    }


def kernel(**inputs):
    import concourse.bacc as bacc
    from concourse.bass_utils import run_bass_kernel_spmd

    nc = bacc.Bacc("TRN2", target_bir_lowering=False, num_devices=1)
    arrays = {n: np.ascontiguousarray(v) for n, v in laid_out({n: np.asarray(v) for n, v in inputs.items()}).items()}
    arrays.update({n: np.ascontiguousarray(v, dtype=np.float32) for n, v in shape_constants().items()})
    aps = {n: nc.dram_tensor(f"in_{n}", v.shape, mybir.dt.from_np(v.dtype), kind="ExternalInput").ap() for n, v in arrays.items()}
    out = nc.dram_tensor("out_rows", (1, SEQ, D), F32, kind="ExternalOutput").ap()
    build_program(nc, aps, out)
    result = run_bass_kernel_spmd(nc, [{f"in_{n}": v for n, v in arrays.items()}], core_ids=[0])
    return result.results[0]["out_rows"]
```

```python
import math
from contextlib import ExitStack

import numpy as np
import concourse.bass as bass
from concourse import mybir

F32 = mybir.dt.float32
F32R = mybir.dt.float32r
BF16 = mybir.dt.bfloat16
I32 = mybir.dt.int32
U32 = mybir.dt.uint32
ACT = mybir.ActivationFunctionType
ALU = mybir.AluOpType
AX = mybir.AxisListType.X

P = 128
SEQ = 512
TILES = SEQ // P
D = 1024
KD = D // P
BANK = 512
SIDE = 192
EPS = 1e-6
LN_EPS = 1e-5
GN_EPS = 64e-5
HEADS = 16
FOX_DK = D // HEADS
DV = 64
Q_RANK, KV_RANK, NOPE, ROPE = 384, 256, 64, 32
QK = NOPE + ROPE
GROUPS, PER_GROUP, EXPERTS, D_EXPERT = 4, 4, 16, 256
NEG = -3.0e38
TWO_PI = 2.0 * math.pi


class Stage:

    def __init__(self, nc, name):
        self.nc, self.name, self.ctx, self.sems = nc, name, ExitStack(), []

    def sb(self, name, shape, dtype=F32):
        return self.ctx.enter_context(self.nc.sbuf_tensor(f"{self.name}_{name}", list(shape), dtype))

    def ps(self, name, shape, dtype=F32):
        return self.ctx.enter_context(self.nc.psum_tensor(f"{self.name}_{name}", list(shape), dtype))

    def sem(self, name):
        self.sems.append(self.ctx.enter_context(self.nc.semaphore(f"{self.name}_{name}")))
        return self.sems[-1]

    def __enter__(self):
        return self

    def __exit__(self, *error):
        if error[0] is None and self.sems:
            with self.nc.Block() as block:
                @block.gpsimd
                def _(pool):
                    for sem in self.sems:
                        pool.sem_clear(sem)
        return self.ctx.__exit__(*error)


class Chain:

    def __init__(self, eng, sem):
        self.eng, self.sem, self.n = eng, sem, 0

    def __call__(self, ins):
        self.n = self.n + 1
        ins.then_inc(self.sem, 1)
        self.eng.wait_ge(self.sem, self.n)


def constants(nc, a, g):
    with Stage(nc, "const") as s:
        loaded = s.sem("loaded")
        with nc.Block() as block:
            @block.sync
            def _(sp):
                sp.dma_start(g.ident[:], a["ident"]).then_inc(loaded, 16)
                sp.dma_start(g.causal[:], a["causal"]).then_inc(loaded, 16)
                sp.dma_start(g.iota[:], a["iota"]).then_inc(loaded, 16)
                sp.dma_start(g.x[:], a["x"].rearrange("o (t p) d -> p (o t) d", p=P)).then_inc(loaded, 16)
                sp.wait_ge(loaded, 64)


def modulation(nc, g, name, c_dram, w_dram, b_dram):
    CH, SLOTS = 6 * D // BANK, 3
    with Stage(nc, name) as s:
        c_col, c_act = s.sb("c_col", [P, KD]), s.sb("c_act", [P, KD])
        c_rep = s.sb("c_rep", [P, KD, P])
        bias = s.sb("bias", [1, 6 * D])
        ones = s.sb("ones", [1, P])
        ring = s.sb("ring", [P, SLOTS, KD, BANK])
        acc = s.ps("acc", [P, SLOTS, BANK])
        small, acted, rep = s.sem("small"), s.sem("acted"), s.sem("rep")
        w_in = [s.sem(f"w_in{u}") for u in range(SLOTS)]
        summed, kept = s.sem("summed"), s.sem("kept")
        mod = g.mod[:].rearrange("p j d -> p (j d)")
        with nc.Block() as block:
            @block.sync
            def _(sp):
                sp.dma_start(c_col[:], c_dram).then_inc(small, 16)
                sp.dma_start(bias[:], b_dram).then_inc(small, 16)
                for u in range(SLOTS):
                    sp.dma_start(ring[:, u], w_dram[u]).then_inc(w_in[u], 16)
                with sp.Fori(0, CH // SLOTS - 1) as i:
                    for u in range(SLOTS):
                        sp.wait_ge(summed, SLOTS * i + u + 1)
                        sp.dma_start(ring[:, u], w_dram[bass.ds(SLOTS * i + u + SLOTS, 1)].rearrange(
                            "o p k n -> p (o k) n")).then_inc(w_in[u], 16)

            @block.scalar
            def _(act):
                act.wait_ge(small, 32)
                nc.scalar.activation(c_act[:], c_col[:], ACT.Silu).then_inc(acted, 1)
                act.sem_inc(kept, SLOTS)
                with act.Fori(0, CH // SLOTS) as i:
                    for u in range(SLOTS):
                        act.wait_ge(summed, SLOTS * i + u + 1)
                        nc.scalar.copy(mod[:, bass.ds((SLOTS * i + u) * BANK, BANK)], acc[:, u]).then_inc(kept, 1)

            @block.vector
            def _(dve):
                nc.vector.memset(ones[:], 1.0).then_inc(rep, 1)
                dve.wait_ge(acted, 1)
                nc.vector.tensor_copy(c_rep[:], c_act[:].unsqueeze(2).to_broadcast([P, KD, P])).then_inc(rep, 1)

            @block.tensor
            def _(pe):
                pe.wait_ge(rep, 2)
                pe.wait_ge(small, 32)
                with pe.Fori(0, CH // SLOTS) as i:
                    for u in range(SLOTS):
                        pe.wait_ge(w_in[u], 16 * i + 16)
                        pe.wait_ge(kept, SLOTS * i + u + 1)
                        for k in range(KD):
                            nc.tensor.matmul(acc[:, u], c_rep[:, k], ring[:, u, k], start=(k == 0), stop=False)
                        nc.tensor.matmul(acc[:, u], ones[:], bias[:, bass.ds((SLOTS * i + u) * BANK, BANK)],
                                         start=False, stop=True).then_inc(summed, 1)


def side_modulation(nc, g, name, sums_dram, b_dram):
    CH, BANKS = 6 * D // BANK, 4
    with Stage(nc, name) as s:
        sums = s.sb("sums", [P, 6 * D])
        ones, bias = s.sb("ones", [P, P]), s.sb("bias", [1, 6 * D])
        acc = s.ps("acc", [P, BANKS, BANK])
        loaded, ready, summed, kept = s.sem("loaded"), s.sem("ready"), s.sem("summed"), s.sem("kept")
        mod = g.mod[:].rearrange("p j d -> p (j d)")
        with nc.Block() as block:
            @block.sync
            def _(sp):
                sp.dma_start(bias[:], b_dram).then_inc(loaded, 16)
                sp.dma_start(sums[:].rearrange("p (c n) -> p c n", n=SIDE), sums_dram.rearrange("c p n -> p c n")).then_inc(loaded, 16)

            @block.vector
            def _(dve):
                nc.vector.memset(ones[:], 1.0).then_inc(ready, 1)
                dve.wait_ge(loaded, 32)
                for n in range(CH):
                    columns = slice(n * BANK, (n + 1) * BANK)
                    nc.vector.tensor_tensor(sums[0:1, columns], sums[0:1, columns], bias[:, columns], ALU.add).then_inc(ready, 1)

            @block.tensor
            def _(pe):
                for n in range(CH):
                    columns = slice(n * BANK, (n + 1) * BANK)
                    if n >= BANKS:
                        pe.wait_ge(kept, n - BANKS + 1)
                    pe.wait_ge(ready, n + 2)
                    nc.tensor.matmul(acc[:, n % BANKS], ones[:], sums[:, columns], start=True, stop=True).then_inc(summed, 1)

            @block.scalar
            def _(act):
                for n in range(CH):
                    act.wait_ge(summed, n + 1)
                    nc.scalar.copy(mod[:, n * BANK:(n + 1) * BANK], acc[:, n % BANKS]).then_inc(kept, 1)


def normed(nc, g, name, kind, scale_at, shift_at, gain=None):
    with Stage(nc, name) as s:
        h = s.sb("h", [P, 2, D])
        square = s.sb("square", [P, D])
        gain_row, factor = s.sb("gain_row", [P, D]), s.sb("factor", [P, D])
        stat = s.sb("stat", [P, TILES, 2, 6])
        ms, rstd, mean = s.sb("ms", [P, TILES, 2]), s.sb("rstd", [P, TILES]), s.sb("mean", [P, TILES])
        root = s.sb("root", [P, TILES])
        pt = s.ps("pt", [P, 2, KD, P])
        loaded, order, squared = s.sem("loaded"), s.sem("order"), s.sem("squared")
        scaled, turned, kept, shifted = s.sem("scaled"), s.sem("turned"), s.sem("kept"), s.sem("shifted")
        ready, rooted = s.sem("ready"), s.sem("rooted")
        with nc.Block() as block:
            @block.sync
            def _(sp):
                if gain is not None:
                    sp.dma_start(gain_row[:], gain).then_inc(loaded, 16)

            @block.scalar
            def _(act):
                if kind == "rms":
                    for t in range(TILES):
                        if t:
                            act.wait_ge(squared, t)
                        nc.scalar.activation(square[:], g.x[:, t], ACT.Square,
                                             accum_out=ms[:, t, 0:1]).then_inc(squared, 1)
                act.wait_ge(ready, 1)
                nc.scalar.activation(root[:], mean[:], ACT.Sqrt).then_inc(rooted, 1)
                for t in range(TILES):
                    act.wait_ge(turned, t + 1)
                    for half in range(2):
                        ks = slice(half * KD // 2, (half + 1) * KD // 2)
                        nc.scalar.copy(g.hT[:, ks, t * P:(t + 1) * P], pt[:, t % 2, ks]).then_inc(kept, 1)

            @block.vector
            def _(dve):
                then = Chain(dve, order)
                if gain is not None:
                    dve.wait_ge(loaded, 16)
                    then(nc.vector.scalar_tensor_tensor(factor[:], g.mod[:, scale_at], 1.0, gain_row[:], ALU.add, ALU.mult))
                else:
                    then(nc.vector.tensor_scalar(factor[:], g.mod[:, scale_at], 1.0, None, ALU.add))
                if kind == "rms":
                    dve.wait_ge(squared, TILES)
                    then(nc.vector.tensor_scalar(mean[:], ms[:, :, 0], 1.0 / D, EPS, ALU.mult, ALU.add))
                else:
                    for t in range(TILES):
                        for half in range(2):
                            then(nc.vector.bn_stats(stat[:, t, half], g.x[:, t, half * D // 2:(half + 1) * D // 2]))
                        then(nc.vector.bn_aggr(ms[:, t], stat[:, t]))
                    then(nc.vector.tensor_scalar(mean[:], ms[:, :, 1], LN_EPS, None, ALU.add))
                nc.vector.tensor_scalar(mean[:], mean[:], 0.0, None, ALU.max).then_inc(ready, 1)
                dve.wait_ge(rooted, 1)
                then(nc.vector.reciprocal(rstd[:], root[:]))
                for t in range(TILES):
                    if t >= 2:
                        dve.wait_ge(turned, t - 1)
                    if kind == "rms":
                        then(nc.vector.scalar_tensor_tensor(h[:, t % 2], g.x[:, t], rstd[:, t:t + 1], factor[:],
                                                            ALU.mult, ALU.mult))
                    else:
                        then(nc.vector.tensor_scalar(h[:, t % 2], g.x[:, t], ms[:, t, 0:1], rstd[:, t:t + 1],
                                                     ALU.subtract, ALU.mult))
                        then(nc.vector.tensor_tensor(h[:, t % 2], h[:, t % 2], factor[:], ALU.mult))
                    nc.vector.tensor_tensor(h[:, t % 2], h[:, t % 2], g.mod[:, shift_at], ALU.add).then_inc(shifted, 1)

            @block.tensor
            def _(pe):
                for t in range(TILES):
                    pe.wait_ge(shifted, t + 1)
                    if t >= 2:
                        pe.wait_ge(kept, 2 * (t - 1))
                    for k in range(KD):
                        last = nc.tensor.transpose(pt[:, t % 2, k], h[:, t % 2, k * P:(k + 1) * P], g.ident[:])
                    last.then_inc(turned, 1)


def project_rows(nc, name, lhs, kc, w_dram, chunks, width, keep=None, gate=None, x=None, alpha=1.0):
    with Stage(nc, name) as s:
        ring = s.sb("ring", [P, 2, kc, width])
        part = s.sb("part", [P, 2, width])
        acc = s.ps("acc", [P, 2, TILES, BANK])
        w_in = [s.sem(f"w_in{u}") for u in range(2)]
        summed, kept, gated = s.sem("summed"), s.sem("kept"), s.sem("gated")
        pairs = chunks // 2
        assert chunks == 2 * pairs

        def chunk_loop(eng, body):
            if pairs == 1:
                for u in range(2):
                    body(0, u)
            else:
                with eng.Fori(0, pairs) as i:
                    for u in range(2):
                        body(i, u)

        with nc.Block() as block:
            @block.sync
            def _(sp):
                for u in range(2):
                    sp.dma_start(ring[:, u], w_dram[u]).then_inc(w_in[u], 16)
                if pairs > 1:
                    with sp.Fori(0, pairs - 1) as i:
                        for u in range(2):
                            sp.wait_ge(summed, TILES * (2 * i + u) + TILES)
                            sp.dma_start(ring[:, u], w_dram[bass.ds(2 * i + u + 2, 1)].rearrange(
                                "o p k n -> p (o k) n")).then_inc(w_in[u], 16)

            @block.tensor
            def _(pe):
                def body(i, u):
                    pe.wait_ge(w_in[u], 16 * i + 16)
                    for t in range(TILES):
                        pe.wait_ge(kept, TILES * (2 * i + u) + t + 1)
                        for k in range(kc):
                            last = nc.tensor.matmul(acc[:, u, t, :width], lhs[:, k, t * P:(t + 1) * P], ring[:, u, k],
                                                    start=(k == 0), stop=(k == kc - 1))
                        last.then_inc(summed, 1)
                chunk_loop(pe, body)

            if keep is not None:
                @block.scalar
                def _(act):
                    act.sem_inc(kept, 2 * TILES)

                    def body(i, u):
                        for t in range(TILES):
                            act.wait_ge(summed, TILES * (2 * i + u) + t + 1)
                            nc.scalar.copy(keep[:, t, bass.ds((2 * i + u) * width, width)],
                                           acc[:, u, t, :width]).then_inc(kept, 1)
                    chunk_loop(act, body)
            else:
                @block.vector
                def _(dve):
                    dve.sem_inc(kept, 2 * TILES)
                    for n in range(chunks):
                        cols = slice(n * width, (n + 1) * width)
                        for t in range(TILES):
                            m = n * TILES + t
                            dve.wait_ge(summed, m + 1)
                            nc.vector.tensor_tensor(part[:, m % 2], acc[:, n % 2, t, :width], gate[:, cols],
                                                    ALU.mult).then_inc(kept, 1)
                            dve.wait_ge(kept, 2 * TILES + m + 1)
                            nc.vector.scalar_tensor_tensor(x[:, t, cols], x[:, t, cols], alpha, part[:, m % 2],
                                                           ALU.mult, ALU.add).then_inc(gated, 1)


def project_cols(nc, name, rhs, kc, w_dram, chunks, keep):
    with Stage(nc, name) as s:
        ring = s.sb("ring", [P, 2, kc, P])
        acc = s.ps("acc", [P, 2, BANK])
        w_in = [s.sem(f"w_in{u}") for u in range(2)]
        summed, kept = s.sem("summed"), s.sem("kept")
        pairs = chunks // 2
        assert chunks == 2 * pairs and pairs > 1
        with nc.Block() as block:
            @block.sync
            def _(sp):
                for u in range(2):
                    sp.dma_start(ring[:, u], w_dram[u]).then_inc(w_in[u], 16)
                with sp.Fori(0, pairs - 1) as i:
                    for u in range(2):
                        sp.wait_ge(summed, 2 * i + u + 1)
                        sp.dma_start(ring[:, u], w_dram[bass.ds(2 * i + u + 2, 1)].rearrange(
                            "o p k n -> p (o k) n")).then_inc(w_in[u], 16)

            @block.tensor
            def _(pe):
                with pe.Fori(0, pairs) as i:
                    for u in range(2):
                        pe.wait_ge(w_in[u], 16 * i + 16)
                        pe.wait_ge(kept, 2 * i + u + 1)
                        for k in range(kc):
                            last = nc.tensor.matmul(acc[:, u], ring[:, u, k], rhs[:, k], start=(k == 0), stop=(k == kc - 1))
                        last.then_inc(summed, 1)

            @block.scalar
            def _(act):
                act.sem_inc(kept, 2)
                with act.Fori(0, pairs) as i:
                    for u in range(2):
                        act.wait_ge(summed, 2 * i + u + 1)
                        nc.scalar.copy(keep[:, bass.ds(2 * i + u, 1)], acc[:, u]).then_inc(kept, 1)


def turn_rows(nc, g, name, rows, chunks, turned):
    with Stage(nc, name) as s:
        pt = s.ps("pt", [P, 4, TILES, P])
        done, kept = s.sem("done"), s.sem("kept")
        with nc.Block() as block:
            @block.tensor
            def _(pe):
                for c in range(chunks):
                    if c >= 4:
                        pe.wait_ge(kept, c - 3)
                    for t in range(TILES):
                        last = nc.tensor.transpose(pt[:, c % 4, t], rows[:, t, c * P:(c + 1) * P], g.ident[:])
                    last.then_inc(done, 1)

            @block.scalar
            def _(act):
                for c in range(chunks):
                    act.wait_ge(done, c + 1)
                    nc.scalar.copy(turned[:, c], pt[:, c % 4].rearrange("p t n -> p (t n)")).then_inc(kept, 1)
def head_norms(nc, name, jobs, dk, heads=HEADS):
    with Stage(nc, name) as s:
        n = len(jobs) * TILES
        square = s.sb("square", [P, 2, heads, dk])
        total, root, inv = (s.sb(x, [P, n, heads]) for x in ("total", "root", "inv"))
        gains = [s.sb(f"gain{j}", [P, dk]) for j in range(len(jobs))]
        loaded, squared, summed, rooted = s.sem("loaded"), s.sem("squared"), s.sem("summed"), s.sem("rooted")
        order, halfway, normed_ = s.sem("order"), s.sem("halfway"), s.sem("normed")

        def tile(m):
            rows, _, _ = jobs[m // TILES]
            return rows[:, m % TILES].rearrange("p (h d) -> p h d", d=dk)

        with nc.Block() as block:
            @block.sync
            def _(sp):
                for j, (_, gain, _) in enumerate(jobs):
                    sp.dma_start(gains[j][:], gain).then_inc(loaded, 16)

            @block.scalar
            def _(act):
                for m in range(n):
                    if m >= 2:
                        act.wait_ge(summed, m - 1)
                    nc.scalar.activation(square[:, m % 2], tile(m), ACT.Square).then_inc(squared, 1)
                act.wait_ge(order, 1)
                nc.scalar.activation(root[:], total[:], ACT.Sqrt).then_inc(rooted, 1)

            @block.vector
            def _(dve):
                for m in range(n):
                    dve.wait_ge(squared, m + 1)
                    nc.vector.tensor_reduce(total[:, m], square[:, m % 2], AX, ALU.add).then_inc(summed, 1)
                dve.wait_ge(summed, n)
                then = Chain(dve, order)
                then(nc.vector.tensor_scalar(total[:], total[:], 1.0 / dk, EPS, ALU.mult, ALU.add))
                dve.wait_ge(rooted, 1)
                then(nc.vector.reciprocal(inv[:], root[:]))
                for j, (_, _, scale) in enumerate(jobs):
                    if scale != 1.0:
                        part = inv[:, j * TILES:(j + 1) * TILES]
                        then(nc.vector.tensor_scalar(part, part, scale, None, ALU.mult))
                dve.wait_ge(loaded, 16 * len(jobs))
                for m in range(n):
                    nc.vector.tensor_tensor(tile(m), tile(m), inv[:, m].unsqueeze(2).to_broadcast([P, heads, dk]),
                                            ALU.mult).then_inc(halfway, 1)
                    dve.wait_ge(halfway, m + 1)
                    nc.vector.tensor_tensor(tile(m), tile(m), gains[m // TILES][:].unsqueeze(1).to_broadcast([P, heads, dk]),
                                            ALU.mult).then_inc(normed_, 1)


def forget_gates(nc, g, name, w_dram, b_dram, scratch, cum_q, cum_k):
    with Stage(nc, name) as s:
        w, b = s.sb("w", [P, KD, HEADS]), s.sb("b", [HEADS, 1])
        z, low, ones = (s.sb(x, [HEADS, SEQ]) for x in ("z", "low", "ones"))
        size, small, soft = (s.sb(x, [HEADS, SEQ]) for x in ("size", "small", "soft"))
        logs, cum = s.sb("logs", [HEADS, SEQ]), s.sb("cum", [HEADS, SEQ])
        logits, turned = s.ps("logits", [HEADS, SEQ]), s.ps("turned", [P, TILES, HEADS])
        loaded, summed, order, steps = s.sem("loaded"), s.sem("summed"), s.sem("order"), s.sem("steps")
        stored, spread, turn = s.sem("stored"), s.sem("spread"), s.sem("turn")
        with nc.Block() as block:
            @block.sync
            def _(sp):
                sp.dma_start(w[:], w_dram).then_inc(loaded, 16)
                sp.dma_start(b[:], b_dram).then_inc(loaded, 16)
                sp.wait_ge(order, 6)
                sp.dma_start(scratch, cum[:]).then_inc(stored, 16)
                sp.wait_ge(stored, 16)
                sp.dma_start(cum_k[:], scratch.partition_broadcast(P)).then_inc(spread, 16)
                sp.wait_ge(spread, 16)

            @block.tensor
            def _(pe):
                pe.wait_ge(loaded, 32)
                for k in range(KD):
                    last = nc.tensor.matmul(logits[:], w[:, k], g.hT[:, k], start=(k == 0), stop=(k == KD - 1))
                last.then_inc(summed, 1)
                pe.wait_ge(order, 6)
                for t in range(TILES):
                    last = nc.tensor.transpose(turned[:, t], cum[:, t * P:(t + 1) * P], g.ident[:HEADS, :HEADS])
                last.then_inc(turn, 1)

            @block.scalar
            def _(act):
                then = Chain(act, steps)
                act.wait_ge(order, 2)
                then(nc.scalar.activation(size[:], z[:], ACT.Abs))
                then(nc.scalar.activation(small[:], size[:], ACT.Exp, scale=-1.0))
                then(nc.scalar.activation(soft[:], small[:], ACT.Ln, bias=1.0))

            @block.vector
            def _(dve):
                then = Chain(dve, order)
                then(nc.vector.memset(ones[:], 1.0))
                dve.wait_ge(loaded, 32)
                dve.wait_ge(summed, 1)
                then(nc.vector.tensor_scalar(z[:], logits[:], b[:], None, ALU.add))
                then(nc.vector.tensor_scalar(low[:], z[:], 0.0, None, ALU.min))
                dve.wait_ge(steps, 3)
                then(nc.vector.tensor_tensor(logs[:], low[:], soft[:], ALU.subtract))
                then(nc.vector.tensor_scalar(z[:], ones[:], 0.0, None, ALU.mult))
                then(nc.vector.tensor_tensor_scan(cum[:], ones[:], logs[:], 0.0, ALU.mult, ALU.add))
                dve.wait_ge(turn, 1)
                then(nc.vector.tensor_copy(cum_q[:], turned[:]))


def attention(nc, g, name, q, k, v, o, dk, v_step=DV, v_at=0, cum_q=None, cum_k=None):
    STEPS, LOOP = TILES * HEADS, 2 * TILES
    LOOPS = STEPS // LOOP
    AHEAD = 2
    with Stage(nc, name) as s:
        qs, ks = s.sb("qs", [P, TILES, dk]), s.sb("ks", [P, TILES, dk])
        qT, kT = s.sb("qT", [dk, 2, SEQ]), s.sb("kT", [dk, 2, SEQ])
        z, p = s.sb("z", [P, 2, SEQ]), s.sb("p", [P, 2, SEQ])
        pT = s.sb("pT", [P, 2, TILES, P])
        low, total, inv = s.sb("low", [P, 2]), s.sb("total", [P, TILES]), s.sb("inv", [P, 2])
        tq, tk = s.ps("tq", [dk, SEQ]), s.ps("tk", [dk, SEQ])
        scores, tp = s.ps("scores", [P, 2, SEQ]), s.ps("tp", [P, 2, TILES, P])
        out = s.ps("out", [P, 2, BANK])
        copied, turned, kept = s.sem("copied"), s.sem("turned"), s.sem("kept")
        scored, biased, masked, maxed = s.sem("scored"), s.sem("biased"), s.sem("masked"), s.sem("maxed")
        raised, p_turned, p_kept = s.sem("raised"), s.sem("p_turned"), s.sem("p_kept")
        started = s.sem("started")
        mixed, inverted, done = s.sem("mixed"), s.sem("inverted"), s.sem("done")

        def part(start, size):
            return slice(start, start + size) if isinstance(start, int) else bass.ds(start, size)

        def step(k, r):
            return LOOP * k + r, 2 * k + r // TILES, r // TILES % 2, r % TILES

        def slots(eng, slot):
            with eng.Fori(0, LOOPS - 1) as k:
                for r in range(1, LOOP + 1):
                    slot(k, r)
            for r in range(1, LOOP):
                slot(LOOPS - 1, r)

        def exists(k, r):
            return not isinstance(k, int) or LOOP * k + r < STEPS

        with nc.Block() as block:
            @block.gpsimd
            def _(pool):
                with pool.Fori(0, HEADS) as h:
                    pool.wait_ge(turned, h + 1)
                    nc.gpsimd.tensor_copy(qs[:], q[:, :, bass.ds(h * dk, dk)]).then_inc(copied, 1)
                    nc.gpsimd.tensor_copy(ks[:], k[:, :, bass.ds(h * dk, dk)]).then_inc(copied, 1)

            @block.tensor
            def _(pe):
                def turn_head(h):
                    pe.wait_ge(copied, 2 * h + 2)
                    pe.wait_ge(kept, 2 * h + 2)
                    pe.sem_inc(started, 1)
                    for src, dst in ((qs, tq), (ks, tk)):
                        for t in range(TILES):
                            last = nc.tensor.transpose(dst[:, t * P:(t + 1) * P], src[:, t], g.ident[:])
                    last.then_inc(turned, 1)

                def score(k, r):
                    n, h, u, i = step(k, r)
                    width = (i + 1) * P
                    pe.wait_ge(kept, 2 * h + 4)
                    pe.wait_ge(biased, n + 1)
                    nc.tensor.matmul(scores[:, i % 2, :width], qT[:, u, i * P:(i + 1) * P], kT[:, u, :width],
                                     start=True, stop=True).then_inc(scored, 1)

                def turn(k, r):
                    n, h, u, i = step(k, r)
                    pe.wait_ge(raised, n + 1 + AHEAD)
                    pe.wait_ge(p_kept, n + 1)
                    for j in range(i + 1):
                        last = nc.tensor.transpose(tp[:, i % 2, j], p[:, i % 2, j * P:(j + 1) * P], g.ident[:])
                    last.then_inc(p_turned, 1)

                def mix(k, r):
                    n, h, u, i = step(k, r)
                    pe.wait_ge(p_kept, n + 1 + AHEAD)
                    pe.wait_ge(done, n + 1 + TILES - AHEAD)
                    for j in range(i + 1):
                        last = nc.tensor.matmul(out[:, i % 2, :DV], pT[:, i % 2, j], v[:, j, part(h * v_step + v_at, DV)],
                                                start=(j == 0), stop=(j == i))
                    last.then_inc(mixed, 1)

                def slot(k, r):
                    if exists(k, r + 2):
                        score(k, r + 2)
                    turn(k, r)
                    mix(k, r - 1)
                    if r % TILES == 0 and exists(k, r + TILES):
                        turn_head(2 * k + r // TILES + 1)

                pe.sem_inc(turned, 1)
                pe.sem_inc(scored, 2 * TILES)
                pe.sem_inc(p_turned, AHEAD)
                pe.sem_inc(mixed, AHEAD)
                turn_head(0)
                for r in range(3):
                    score(0, r)
                turn(0, 0)
                turn_head(1)
                slots(pe, slot)
                mix(LOOPS - 1, LOOP - 1)

            @block.scalar
            def _(act):
                def keep_head(h, u):
                    act.wait_ge(turned, h + 2)
                    act.wait_ge(scored, TILES * h + TILES)
                    nc.scalar.copy(qT[:, u], tq[:]).then_inc(kept, 1)
                    nc.scalar.copy(kT[:, u], tk[:]).then_inc(kept, 1)

                def raise_(k, r):
                    n, h, u, i = step(k, r)
                    width = (i + 1) * P
                    act.wait_ge(maxed, n + 1)
                    act.wait_ge(p_turned, n + 1)
                    act.wait_ge(done, n + 1)
                    nc.scalar.activation(p[:, i % 2, :width], z[:, i % 2, :width], ACT.Exp, bias=low[:, i % 2:i % 2 + 1],
                                         accum_out=total[:, i:i + 1]).then_inc(raised, 1)

                def keep(k, r):
                    n, h, u, i = step(k, r)
                    act.wait_ge(p_turned, n + 1 + AHEAD)
                    act.wait_ge(mixed, n + 1)
                    nc.scalar.copy(pT[:, i % 2, :i + 1], tp[:, i % 2, :i + 1]).then_inc(p_kept, 1)

                def slot(k, r):
                    if exists(k, r + 1):
                        raise_(k, r + 1)
                    keep(k, r)
                    if r % TILES == 0 and exists(k, r + TILES):
                        keep_head(2 * k + r // TILES + 1, (r // TILES + 1) % 2)

                act.sem_inc(kept, 2)
                act.sem_inc(raised, AHEAD)
                act.sem_inc(p_kept, AHEAD)
                keep_head(0, 0)
                raise_(0, 0)
                raise_(0, 1)
                keep(0, 0)
                keep_head(1, 1)
                slots(act, slot)

            @block.vector
            def _(dve):
                def bias(k, r):
                    n, h, u, i = step(k, r)
                    width = (i + 1) * P
                    dve.wait_ge(scored, n + 1 + 2 * TILES)
                    dve.wait_ge(raised, n + 1)
                    if cum_q is None:
                        nc.vector.tensor_copy(z[:, i % 2, :width], scores[:, i % 2, :width]).then_inc(biased, 1)
                    else:
                        nc.vector.scalar_tensor_tensor(
                            z[:, i % 2, :width], scores[:, i % 2, :width], cum_q[:, i, part(h, 1)],
                            cum_k[:, part(h, 1), :width].rearrange("p o t -> p (o t)"),
                            ALU.add, ALU.subtract).then_inc(biased, 1)
                    dve.wait_ge(biased, n + 1 + AHEAD)
                    diagonal = z[:, i % 2, i * P:width]
                    nc.vector.tensor_tensor(diagonal, diagonal, g.causal[:], ALU.add).then_inc(masked, 1)
                    dve.wait_ge(masked, n + 1)
                    nc.vector.tensor_reduce(low[:, i % 2:i % 2 + 1], z[:, i % 2, :width], AX, ALU.max,
                                            negate=True).then_inc(maxed, 1)

                def divide(k, r):
                    n, h, u, i = step(k, r)
                    dve.wait_ge(mixed, n + 1 + AHEAD)
                    nc.vector.reciprocal(inv[:, i % 2:i % 2 + 1], total[:, i:i + 1]).then_inc(inverted, 1)
                    dve.wait_ge(inverted, n + 1)
                    nc.vector.tensor_scalar(o[:, i, part(h * DV, DV)], out[:, i % 2, :DV], inv[:, i % 2:i % 2 + 1],
                                            None, ALU.mult).then_inc(done, 1)

                def slot(k, r):
                    if exists(k, r + 2):
                        bias(k, r + 2)
                    divide(k, r - 1)

                dve.sem_inc(biased, AHEAD)
                dve.sem_inc(done, TILES)
                for r in range(3):
                    bias(0, r)
                slots(dve, slot)
                divide(LOOPS - 1, LOOP - 1)
def route(nc, g, name, w_dram, b_dram):
    N = GROUPS + EXPERTS
    with Stage(nc, name) as s:
        w, b = s.sb("w", [P, KD, N]), s.sb("b", [P, N])
        by_group, by_expert = s.sb("by_group", [P, TILES, 8]), s.sb("by_expert", [P, TILES, EXPERTS])
        best, best_at = s.sb("best", [P, TILES, 8]), s.sb("best_at", [P, TILES, 8], U32)
        group, is_group = s.sb("group", [P, TILES, 1]), s.sb("is_group", [P, TILES, GROUPS])
        lowered, raised = s.sb("lowered", [P, TILES, GROUPS]), s.sb("raised", [P, TILES, GROUPS])
        total, top = s.sb("total", [P, TILES, 1]), s.sb("top", [P, TILES, 1])
        chosen = s.sb("chosen", [P, TILES, GROUPS, PER_GROUP])
        inside = s.sb("inside", [P, TILES, 8])
        pair, pair_at = s.sb("pair", [P, TILES, 8]), s.sb("pair_at", [P, TILES, 8], U32)
        ids, weights = s.sb("ids", [P, TILES, 2]), s.sb("weights", [P, TILES, 2])
        gap, ratio = s.sb("gap", [P, TILES, 1]), s.sb("ratio", [P, TILES, 1])
        first, second = s.sb("first", [P, TILES, EXPERTS]), s.sb("second", [P, TILES, EXPERTS])
        logits = s.ps("logits", [P, TILES, N])
        loaded, summed, order = s.sem("loaded"), s.sem("summed"), s.sem("order")
        low_ready, raised_ready = s.sem("low_ready"), s.sem("raised_ready")
        iota = lambda n: g.iota[:, :n].unsqueeze(1).to_broadcast([P, TILES, n])
        with nc.Block() as block:
            @block.sync
            def _(sp):
                sp.dma_start(w[:], w_dram).then_inc(loaded, 16)
                sp.dma_start(b[:], b_dram).then_inc(loaded, 16)

            @block.tensor
            def _(pe):
                pe.wait_ge(loaded, 32)
                for t in range(TILES):
                    for k in range(KD):
                        last = nc.tensor.matmul(logits[:, t], g.hT[:, k, t * P:(t + 1) * P], w[:, k],
                                                start=(k == 0), stop=(k == KD - 1))
                last.then_inc(summed, 1)

            @block.scalar
            def _(act):
                act.wait_ge(low_ready, 1)
                nc.scalar.activation(raised[:], lowered[:], ACT.Exp).then_inc(raised_ready, 1)
                act.wait_ge(low_ready, 2)
                nc.scalar.activation(ratio[:], gap[:], ACT.Exp).then_inc(raised_ready, 1)

            @block.vector
            def _(dve):
                then = Chain(dve, order)
                v = nc.vector
                then(v.memset(by_group[:], NEG))
                then(v.memset(inside[:], NEG))
                dve.wait_ge(loaded, 32)
                dve.wait_ge(summed, 1)
                then(v.tensor_tensor(by_group[:, :, :GROUPS], logits[:, :, :GROUPS],
                                     b[:, :GROUPS].unsqueeze(1).to_broadcast([P, TILES, GROUPS]), ALU.add))
                then(v.tensor_tensor(by_expert[:], logits[:, :, GROUPS:],
                                     b[:, GROUPS:].unsqueeze(1).to_broadcast([P, TILES, EXPERTS]), ALU.add))
                for t in range(TILES):
                    then(v.max(best[:, t], by_group[:, t]))
                    then(v.max_index(best_at[:, t], best[:, t], by_group[:, t]))
                then(v.tensor_copy(group[:], best_at[:, :, 0:1]))
                v.tensor_tensor(lowered[:], by_group[:, :, :GROUPS], best[:, :, 0:1].to_broadcast([P, TILES, GROUPS]),
                                ALU.subtract).then_inc(low_ready, 1)
                then(v.tensor_tensor(is_group[:], iota(GROUPS), group[:].to_broadcast([P, TILES, GROUPS]), ALU.is_equal))
                for t in range(TILES):
                    then(v.tensor_tensor(chosen[:, t], by_expert[:, t].rearrange("p (a e) -> p a e", a=GROUPS),
                                         is_group[:, t].unsqueeze(2).to_broadcast([P, GROUPS, PER_GROUP]), ALU.mult))
                    then(v.tensor_reduce(inside[:, t, :PER_GROUP], chosen[:, t].rearrange("p a e -> p e a"), AX, ALU.add))
                    then(v.max(pair[:, t], inside[:, t]))
                    then(v.max_index(pair_at[:, t], pair[:, t], inside[:, t]))
                v.tensor_tensor(gap[:], pair[:, :, 1:2], pair[:, :, 0:1], ALU.subtract).then_inc(low_ready, 1)
                then(v.tensor_copy(ids[:], pair_at[:, :, 0:2]))
                then(v.scalar_tensor_tensor(ids[:], group[:].to_broadcast([P, TILES, 2]), float(PER_GROUP), ids[:],
                                            ALU.mult, ALU.add))
                dve.wait_ge(raised_ready, 2)
                then(v.tensor_reduce(total[:], raised[:], AX, ALU.add))
                then(v.reciprocal(top[:], total[:]))
                then(v.tensor_scalar(total[:], ratio[:], 1.0, None, ALU.add))
                then(v.reciprocal(gap[:], total[:]))
                then(v.tensor_tensor(weights[:, :, 0:1], gap[:], top[:], ALU.mult))
                then(v.tensor_tensor(weights[:, :, 1:2], weights[:, :, 0:1], ratio[:], ALU.mult))
                for j, part in enumerate((first, second)):
                    then(v.tensor_tensor(part[:], iota(EXPERTS), ids[:, :, j:j + 1].to_broadcast([P, TILES, EXPERTS]), ALU.is_equal))
                    then(v.tensor_tensor(part[:], part[:], weights[:, :, j:j + 1].to_broadcast([P, TILES, EXPERTS]), ALU.mult))
                then(v.tensor_tensor(g.comb[:], first[:], second[:], ALU.add))


def split_rows(nc, g, name, hi, lo):
    with Stage(nc, name) as s:
        rounded, left = s.sem("rounded"), s.sem("left")
        with nc.Block() as block:
            @block.scalar
            def _(act):
                for k in range(KD):
                    nc.scalar.copy(hi[:, k], g.hT[:, k]).then_inc(rounded, 1)

            @block.vector
            def _(dve):
                for k in range(KD):
                    dve.wait_ge(rounded, k + 1)
                    nc.vector.tensor_tensor(lo[:, k], g.hT[:, k], hi[:, k].bitcast(F32), ALU.subtract).then_inc(left, 1)


def expert_chunks(nc, g, name, rising, lowering, first, chunks, h_hi, h_lo, bend, factor, share, acc, side=None):
    HALVES, BANKS = D // BANK, 4
    OUTS, J = TILES * HALVES, len(rising)
    with Stage(nc, name) as s:
        landing = [g.hT[:, 2 * m:2 * m + 2].rearrange("p a (b n) -> p (a b) n", n=P) for m in range(4)]
        if J == 2:
            extra = s.sb("extra", [P, 2, KD, P])
            landing = landing + [extra[:, m] for m in range(2)]
        raw_up = [[landing[(J + 1) * u + j] for j in range(J)] for u in range(2)]
        raw_down = [landing[(J + 1) * u + J].rearrange("p k n -> p (k n)") for u in range(2)]
        up_hi, up_lo = s.sb("up_hi", [P, 2, J, KD, P], F32R), s.sb("up_lo", [P, 2, J, KD, P], F32R)
        down_hi, down_lo = s.sb("down_hi", [P, 2, D], F32R), s.sb("down_lo", [P, 2, D], F32R)
        bent = s.sb("bent", [P, 2, SEQ])
        bent_hi, bent_lo = s.sb("bent_hi", [P, 2, SEQ], F32R), s.sb("bent_lo", [P, 2, SEQ], F32R)
        risen, low = s.ps("risen", [P, 2, J, SEQ]), s.ps("low", [P, BANKS, BANK])
        up_in, down_in = [s.sem(f"up_in{u}") for u in range(2)], [s.sem(f"down_in{u}") for u in range(2)]
        up_rounded, up_split = s.sem("up_rounded"), s.sem("up_split")
        down_rounded, down_split = s.sem("down_rounded"), s.sem("down_split")
        lifted, bent_done, made = s.sem("lifted"), s.sem("bent_done"), s.sem("made")
        rounded, split = s.sem("rounded"), s.sem("split")
        lowered, added = s.sem("lowered"), s.sem("added")
        if side is not None:
            side_w, side_sum = s.sb("side_w", [P, 2, KD, SIDE]), s.sb("side_sum", [P, 2, SIDE])
            side_in, side_out = [s.sem(f"side_in{u}") for u in range(2)], [s.sem(f"side_out{u}") for u in range(2)]
            side_made, side_summed = s.sem("side_made"), s.sem("side_summed")

        def passes(out, lhs, rhs, start, stop):
            (l_hi, l_lo), (r_hi, r_lo) = lhs, rhs
            nc.tensor.matmul(out, l_hi, r_hi, start=start, stop=False)
            nc.tensor.matmul(out, l_hi, r_lo, start=False, stop=False)
            return nc.tensor.matmul(out, l_lo, r_hi, start=False, stop=stop)

        def pairs(eng, body):
            with eng.Fori(0, chunks // 2 - 1) as i:
                for u in range(2):
                    body(2 * i + u, u, i)

        last, before = chunks - 1, chunks - 2
        with nc.Block() as block:
            def chunk(dram, n):
                return dram[first + n:first + n + 1] if isinstance(n, int) else dram[bass.ds(first + n, 1)]

            @block.sync
            def _(sp):
                def load_up(n, u):
                    for j in range(J):
                        sp.dma_start(raw_up[u][j], chunk(rising[j], n).rearrange("o p k n -> p (o k) n")).then_inc(up_in[u], 16)

                def load_down(n, u):
                    sp.dma_start(raw_down[u], chunk(lowering, n).rearrange("o p d -> p (o d)")).then_inc(down_in[u], 16)

                def load_side(n, u):
                    w = side.w[n] if isinstance(n, int) else side.w[bass.ds(n, 1)].rearrange("o p k n -> p (o k) n")
                    sp.dma_start(side_w[:, u], w).then_inc(side_in[u], 16)

                def store_side(n, u):
                    sp.wait_ge(side_summed, n + 1)
                    to = side.sums[n] if isinstance(n, int) else side.sums[bass.ds(n, 1)].rearrange("o p n -> p (o n)")
                    sp.dma_start(to, side_sum[:, u]).then_inc(side_out[u], 16)

                def load_next(n, u):
                    sp.wait_ge(up_split, n + 1)
                    load_up(n + 2, u)
                    sp.wait_ge(down_split, n + 1)
                    load_down(n + 2, u)

                def next_side(n, u):
                    if side is not None:
                        store_side(n, u)
                        load_side(n + 2, u)

                for u in range(2):
                    load_up(u, u)
                    load_down(u, u)
                    if side is not None:
                        load_side(u, u)
                load_next(0, 0)
                with sp.Fori(0, chunks // 2 - 2) as i:
                    load_next(2 * i + 1, 1)
                    next_side(2 * i, 0)
                    load_next(2 * i + 2, 0)
                    next_side(2 * i + 1, 1)
                load_next(chunks - 3, 1)
                next_side(chunks - 4, 0)
                next_side(chunks - 3, 1)
                if side is not None:
                    store_side(before, 0)
                    store_side(last, 1)
                    for u in range(2):
                        sp.wait_ge(side_out[u], 16 * (chunks // 2) + 16)

            @block.tensor
            def _(pe):
                def lift(n, u):
                    pe.wait_ge(up_split, n + 1)
                    pe.wait_ge(made, n + 1)
                    for j in range(J):
                        for k in range(KD):
                            done = passes(risen[:, u, j], (up_hi[:, u, j, k], up_lo[:, u, j, k]), (h_hi[:, k], h_lo[:, k]),
                                          k == 0, k == KD - 1)
                    done.then_inc(lifted, 1)

                def lower(n, u):
                    pe.wait_ge(down_split, n + 1)
                    pe.wait_ge(split, n + 3)
                    for m in range(OUTS):
                        t, half = m // HALVES, m % HALVES
                        tokens, columns = slice(t * P, (t + 1) * P), slice(half * BANK, (half + 1) * BANK)
                        pe.wait_ge(added, OUTS * n + m + 1)
                        passes(low[:, m % BANKS], (bent_hi[:, u, tokens], bent_lo[:, u, tokens]),
                               (down_hi[:, u, columns], down_lo[:, u, columns]), True, True).then_inc(lowered, 1)

                pe.sem_inc(lifted, 2)
                pe.sem_inc(lowered, 2 * OUTS)
                lift(0, 0)

                def step(n, u, i):
                    lift(n + 1, 1 - u)
                    lower(n, u)

                pairs(pe, step)
                lift(last, 1)
                lower(before, 0)
                lower(last, 1)

            @block.scalar
            def _(act):
                def round_up(n, u, loads):
                    act.wait_ge(up_in[u], 16 * J * loads)
                    act.wait_ge(lifted, n + 1)
                    for j in range(J):
                        nc.scalar.copy(up_hi[:, u, j], raw_up[u][j]).then_inc(up_rounded, 1)

                def round_down(n, u, loads):
                    act.wait_ge(down_in[u], 16 * loads)
                    act.wait_ge(lowered, OUTS * n + OUTS)
                    nc.scalar.copy(down_hi[:, u], raw_down[u]).then_inc(down_rounded, 1)

                def bend_chunk(n, u):
                    act.wait_ge(lifted, n + 3)
                    act.wait_ge(split, n + 1)
                    nc.scalar.activation(bent[:, u], risen[:, u, 0], bend).then_inc(bent_done, 1)
                    act.wait_ge(made, n + 3)
                    act.wait_ge(lowered, OUTS * n + OUTS)
                    nc.scalar.copy(bent_hi[:, u], bent[:, u]).then_inc(rounded, 1)

                round_up(0, 0, 1)
                round_up(1, 1, 1)
                round_down(0, 0, 1)
                bend_chunk(0, 0)

                def step(n, u, i):
                    round_up(n + 2, u, i + 2)
                    round_down(n + 1, 1 - u, i + 1 + u)
                    bend_chunk(n + 1, 1 - u)

                pairs(act, step)
                round_down(last, 1, chunks // 2)
                bend_chunk(last, 1)

            @block.gpsimd
            def _(pool):
                def split_up(n, u):
                    for j in range(J):
                        pool.wait_ge(up_rounded, J * n + j + 1)
                        done = nc.gpsimd.tensor_tensor(up_lo[:, u, j], raw_up[u][j], up_hi[:, u, j].bitcast(F32), ALU.subtract)
                    done.then_inc(up_split, 1)

                def split_down(n, u):
                    pool.wait_ge(down_rounded, n + 1)
                    nc.gpsimd.tensor_tensor(down_lo[:, u], raw_down[u], down_hi[:, u].bitcast(F32), ALU.subtract).then_inc(down_split, 1)

                def side_product(n, u, loads):
                    if side is not None:
                        pool.wait_ge(side_in[u], 16 * loads)
                        nc.gpsimd.tensor_tensor(side_w[:, u], side_w[:, u], side.c[:].unsqueeze(2).to_broadcast([P, KD, SIDE]),
                                                ALU.mult).then_inc(side_made, 1)

                split_up(0, 0)
                split_up(1, 1)
                split_down(0, 0)

                def step(n, u, i):
                    side_product(n, u, i + 1)
                    split_up(n + 2, u)
                    split_down(n + 1, 1 - u)

                pairs(pool, step)
                side_product(before, 0, chunks // 2)
                split_down(last, 1)
                side_product(last, 1, chunks // 2)

            @block.vector
            def _(dve):
                def make(n, u):
                    dve.wait_ge(bent_done, n + 1)
                    by = risen[:, u, 1] if J == 2 else factor(n)
                    nc.vector.tensor_tensor(bent[:, u], bent[:, u], by, ALU.mult).then_inc(made, 1)

                def cut(n, u):
                    dve.wait_ge(rounded, n + 1)
                    nc.vector.tensor_tensor(bent_lo[:, u], bent[:, u], bent_hi[:, u].bitcast(F32), ALU.subtract).then_inc(split, 1)

                def add(n, i, outs):
                    if outs[0] == 0:
                        dve.wait_ge(added, OUTS * n + BANKS)
                    for m in outs:
                        t, half = m // HALVES, m % HALVES
                        dve.wait_ge(lowered, OUTS * n + m + 1 + 2 * OUTS)
                        if share is None:
                            done = nc.vector.tensor_tensor(acc[:, t, half], low[:, m % BANKS], acc[:, t, half], ALU.add)
                        else:
                            done = nc.vector.scalar_tensor_tensor(acc[:, t, half], low[:, m % BANKS], share(t, i), acc[:, t, half],
                                                                  ALU.mult, ALU.add)
                        done.then_inc(added, 1)

                def side_reduce(n, u, i):
                    if side is not None:
                        dve.wait_ge(side_made, n + 1)
                        dve.wait_ge(side_out[u], 16 * i + 16)
                        nc.vector.tensor_reduce(side_sum[:, u], side_w[:, u].rearrange("p k n -> p n k"), AX, ALU.add).then_inc(
                            side_summed, 1)

                early, late = range(BANKS), range(BANKS, OUTS)
                dve.sem_inc(made, 2)
                dve.sem_inc(split, 2)
                dve.sem_inc(added, BANKS)
                if side is not None:
                    for u in range(2):
                        dve.sem_inc(side_out[u], 16)
                make(0, 0)
                cut(0, 0)

                def step(n, u, i):
                    make(n + 1, 1 - u)
                    add(n, i, early)
                    cut(n + 1, 1 - u)
                    side_reduce(n, u, i)
                    add(n, i, late)

                pairs(dve, step)
                make(last, 1)
                add(before, chunks // 2 - 1, early)
                cut(last, 1)
                side_reduce(before, 0, chunks // 2 - 1)
                add(before, chunks // 2 - 1, late)
                side_reduce(last, 1, chunks // 2 - 1)
                add(last, chunks // 2 - 1, range(OUTS))


def experts(nc, g, name, gate_dram, up_dram, down_dram, gate_row, side=None):
    assert D_EXPERT == 2 * P

    def share(t, e):
        return g.comb[:, t, e:e + 1] if isinstance(e, int) else g.comb[:, t, bass.ds(e, 1)]

    with ExitStack() as own:
        acc = own.enter_context(nc.sbuf_tensor(f"{name}_acc", [P, TILES, D // BANK, BANK], F32))
        hi, lo = (own.enter_context(nc.sbuf_tensor(f"{name}_h_{x}", [P, KD, SEQ], F32R)) for x in ("hi", "lo"))
        split_rows(nc, g, f"{name}_split", hi, lo)
        with Stage(nc, f"{name}_zero") as s:
            zeroed, side_in, acted = s.sem("zeroed"), s.sem("side_in"), s.sem("acted")
            if side is not None:
                side.c = own.enter_context(nc.sbuf_tensor(f"{name}_side_c", [P, KD], F32))
            with nc.Block() as block:
                @block.vector
                def _(dve):
                    nc.vector.memset(acc[:], 0.0).then_inc(zeroed, 1)

                @block.sync
                def _(sp):
                    if side is not None:
                        sp.dma_start(side.c[:], side.c_dram).then_inc(side_in, 16)

                @block.scalar
                def _(act):
                    if side is not None:
                        act.wait_ge(side_in, 16)
                        nc.scalar.activation(side.c[:], side.c[:], ACT.Silu).then_inc(acted, 1)
        expert_chunks(nc, g, f"{name}_chunks", [gate_dram, up_dram], down_dram, 0, EXPERTS * D_EXPERT // P, hi, lo,
                      ACT.Silu, None, share, acc, side)
        with Stage(nc, f"{name}_sum") as s:
            gated, added = s.sem("gated"), s.sem("added")
            with nc.Block() as block:
                @block.vector
                def _(dve):
                    for t in range(TILES):
                        rows = acc[:, t].rearrange("p a n -> p (a n)")
                        nc.vector.tensor_tensor(rows, rows, gate_row, ALU.mult).then_inc(gated, 1)
                        dve.wait_ge(gated, t + 1)
                        nc.vector.tensor_tensor(g.x[:, t], g.x[:, t], rows, ALU.add).then_inc(added, 1)


def split_latents(nc, g, name, kv, rope_rows, pos_dram, freq_dram, k, cos, sin):
    HALF = ROPE // 2
    BIG = 1.5 * 2.0 ** 23
    TURN_HI = 6.28125
    TURN_LO = TWO_PI - TURN_HI
    with Stage(nc, name) as s:
        pos_i, pos = s.sb("pos_i", [P, TILES], I32), s.sb("pos", [P, TILES])
        freq = s.sb("freq", [P, HALF])
        angle, turns, size = (s.sb(x, [P, TILES, HALF]) for x in ("angle", "turns", "size"))
        loaded, order, ready, split = s.sem("loaded"), s.sem("order"), s.sem("ready"), s.sem("split")
        kv_heads = [kv[:, t].rearrange("p (h d) -> p h d", h=HEADS) for t in range(TILES)]
        k_heads = [k[:, t].rearrange("p (h d) -> p h d", h=HEADS) for t in range(TILES)]
        with nc.Block() as block:
            @block.sync
            def _(sp):
                sp.dma_start(pos_i[:], pos_dram).then_inc(loaded, 16)
                sp.dma_start(freq[:], freq_dram).then_inc(loaded, 16)

            @block.gpsimd
            def _(pool):
                for t in range(TILES):
                    nc.gpsimd.tensor_copy(k_heads[t][:, :, :NOPE], kv_heads[t][:, :, :NOPE]).then_inc(split, 1)

            @block.vector
            def _(dve):
                then = Chain(dve, order)
                v = nc.vector
                dve.wait_ge(loaded, 32)
                then(v.tensor_copy(pos[:], pos_i[:]))
                then(v.tensor_tensor(angle[:], pos[:].unsqueeze(2).to_broadcast([P, TILES, HALF]),
                                     freq[:].unsqueeze(1).to_broadcast([P, TILES, HALF]), ALU.mult))
                then(v.tensor_scalar(turns[:], angle[:], 1.0 / TWO_PI, None, ALU.mult))
                then(v.tensor_scalar(turns[:], turns[:], BIG, None, ALU.add))
                then(v.tensor_scalar(turns[:], turns[:], -BIG, None, ALU.add))
                for part in (TURN_HI, TURN_LO):
                    then(v.scalar_tensor_tensor(angle[:], turns[:], -part, angle[:], ALU.mult, ALU.add))
                then(v.tensor_scalar(angle[:], angle[:], 3.1415925, -3.1415925, ALU.min, ALU.max))
                then(v.scalar_tensor_tensor(size[:], angle[:], -1.0, angle[:], ALU.mult, ALU.max))
                v.tensor_scalar(size[:], size[:], -1.0, math.pi / 2, ALU.mult, ALU.add).then_inc(ready, 1)
                for t in range(TILES):
                    v.tensor_copy(k_heads[t][:, :, NOPE:],
                                  rope_rows[:, t].unsqueeze(1).to_broadcast([P, HEADS, ROPE])).then_inc(split, 1)

            @block.scalar
            def _(act):
                act.wait_ge(ready, 1)
                nc.scalar.activation(sin[:], angle[:], ACT.Sin).then_inc(split, 1)
                nc.scalar.activation(cos[:], size[:], ACT.Sin).then_inc(split, 1)


def rotate(nc, name, rows, cos, sin):
    HALF = ROPE // 2
    with Stage(nc, name) as s:
        parts = s.sb("parts", [P, 2, 4, HEADS, HALF])
        times, turned = s.sem("times"), s.sem("turned")
        jobs = [(r, t) for r in rows for t in range(TILES)]
        with nc.Block() as block:
            @block.vector
            def _(dve):
                v = nc.vector
                for n, (r, t) in enumerate(jobs):
                    heads = r[:, t].rearrange("p (h d) -> p h d", h=HEADS)
                    x1, x2 = heads[:, :, NOPE:NOPE + HALF], heads[:, :, NOPE + HALF:]
                    c, d = (y[:, t].unsqueeze(1).to_broadcast([P, HEADS, HALF]) for y in (cos, sin))
                    part = parts[:, n % 2]
                    if n >= 2:
                        dve.wait_ge(turned, 2 * (n - 1))
                    for j, (a, b) in enumerate(((x1, c), (x2, d), (x1, d), (x2, c))):
                        v.tensor_tensor(part[:, j], a, b, ALU.mult).then_inc(times, 1)
                    dve.wait_ge(times, 4 * n + 4)
                    v.tensor_tensor(x1, part[:, 0], part[:, 1], ALU.subtract).then_inc(turned, 1)
                    v.tensor_tensor(x2, part[:, 2], part[:, 3], ALU.add).then_inc(turned, 1)
CONV, TAPS = 512, 31
CC = CONV // P
RW, RW_HEADS, RW_DIM = 512, 8, 64
RC = RW // P
LORA = 64
IN_CHUNKS = 22
SPAN = 32
BLOCKS = P // SPAN
SPANS = SEQ // SPAN
ALPHA = 2.0 ** 0.25


def turn_cols(nc, g, name, cols, chunks, keeps):
    with Stage(nc, name) as s:
        pt = s.ps("pt", [P, 2, chunks, P])
        done, kept = s.sem("done"), s.sem("kept")
        with nc.Block() as block:
            @block.tensor
            def _(pe):
                for t in range(TILES):
                    if t >= 2:
                        pe.wait_ge(kept, t - 1)
                    for c in range(chunks):
                        last = nc.tensor.transpose(pt[:, t % 2, c], cols[:, c, t * P:(t + 1) * P], g.ident[:])
                    last.then_inc(done, 1)

            @block.scalar
            def _(act):
                for t in range(TILES):
                    act.wait_ge(done, t + 1)
                    nc.scalar.copy(keeps[t], pt[:, t % 2].rearrange("p c n -> p (c n)")).then_inc(kept, 1)


def hybrid_in(nc, g, name, w_in_dram, conv_w, conv_b, pT, out):
    PAD, CONV_CHUNKS, SLOTS = TAPS - 1, 2 * CC, 2
    with Stage(nc, name) as s:
        ring = s.sb("ring", [P, SLOTS, KD, P])
        w, b = s.sb("w", [P, CC, TAPS]), s.sb("b", [P, CC])
        bent = g.mod[:, 0:CC * SEQ // D].rearrange("p a (b n) -> p (a b) n", n=SEQ)
        u = s.sb("u", [P, CC, PAD + SEQ])
        acc = s.ps("acc", [P, SLOTS, BANK])
        w_in = [s.sem(f"w_in{j}") for j in range(SLOTS)]
        summed, kept = s.sem("summed"), s.sem("kept")
        loaded, bent_done, order = s.sem("loaded"), s.sem("bent_done"), s.sem("order")
        with nc.Block() as block:
            @block.sync
            def _(sp):
                for j in range(SLOTS):
                    sp.dma_start(ring[:, j], w_in_dram[j]).then_inc(w_in[j], 16)
                sp.dma_start(w[:], conv_w).then_inc(loaded, 16)
                sp.dma_start(b[:], conv_b).then_inc(loaded, 16)
                with sp.Fori(0, IN_CHUNKS // SLOTS - 1) as i:
                    for j in range(SLOTS):
                        sp.wait_ge(summed, SLOTS * i + j + 1)
                        sp.dma_start(ring[:, j], w_in_dram[bass.ds(SLOTS * (i + 1) + j, 1)].rearrange(
                            "o p k n -> p (o k) n")).then_inc(w_in[j], 16)

            @block.tensor
            def _(pe):
                with pe.Fori(0, IN_CHUNKS // SLOTS) as i:
                    for j in range(SLOTS):
                        pe.wait_ge(w_in[j], 16 * i + 16)
                        pe.wait_ge(kept, SLOTS * i + j + 1)
                        for k in range(KD):
                            last = nc.tensor.matmul(acc[:, j], ring[:, j, k], g.hT[:, k], start=(k == 0), stop=(k == KD - 1))
                        last.then_inc(summed, 1)

            @block.scalar
            def _(act):
                def keep(start, end):
                    with act.Fori(start // SLOTS, end // SLOTS) as i:
                        for j in range(SLOTS):
                            act.wait_ge(summed, SLOTS * i + j + 1)
                            nc.scalar.copy(pT[:, bass.ds(SLOTS * i + j, 1)], acc[:, j]).then_inc(kept, 1)

                act.sem_inc(kept, SLOTS)
                keep(0, CONV_CHUNKS)
                act.wait_ge(kept, SLOTS + CONV_CHUNKS)
                nc.scalar.activation(bent, pT[:, CC:CONV_CHUNKS], ACT.Sigmoid).then_inc(bent_done, 1)
                keep(CONV_CHUNKS, IN_CHUNKS)

            @block.vector
            def _(dve):
                v = nc.vector
                v.memset(u[:, :, :PAD], 0.0).then_inc(order, 1)
                dve.wait_ge(bent_done, 1)
                v.tensor_tensor(u[:, :, PAD:], pT[:, :CC], bent, ALU.mult).then_inc(order, 1)
                dve.wait_ge(order, 2)
                dve.wait_ge(loaded, 32)
                for j in range(TAPS):
                    for c in range(CC):
                        if j == 0:
                            v.tensor_scalar(out[:, c], u[:, c, :SEQ], w[:, c, 0:1], b[:, c:c + 1],
                                            ALU.mult, ALU.add).then_inc(order, 1)
                        else:
                            dve.wait_ge(order, 2 + CC * (j - 1) + c + 1)
                            v.scalar_tensor_tensor(out[:, c], u[:, c, j:j + SEQ], w[:, c, j:j + 1], out[:, c],
                                                   ALU.mult, ALU.add).then_inc(order, 1)


def conv_norm(nc, g, name, rows, g_dram, b_dram, y):
    with Stage(nc, name) as s:
        gain, shift = s.sb("gain", [P, CONV]), s.sb("shift", [P, CONV])
        stat, ms = s.sb("stat", [P, TILES, 6]), s.sb("ms", [P, TILES, 2])
        root, rstd = s.sb("root", [P, TILES]), s.sb("rstd", [P, TILES])
        loaded, order, rooted, ready, shifted, bent = (s.sem(x) for x in ("loaded", "order", "rooted", "ready", "shifted", "bent"))
        with nc.Block() as block:
            @block.sync
            def _(sp):
                sp.dma_start(gain[:], g_dram).then_inc(loaded, 16)
                sp.dma_start(shift[:], b_dram).then_inc(loaded, 16)

            @block.scalar
            def _(act):
                act.wait_ge(ready, 1)
                nc.scalar.activation(root[:], rstd[:], ACT.Sqrt).then_inc(rooted, 1)
                for t in range(TILES):
                    act.wait_ge(shifted, t + 1)
                    nc.scalar.activation(y[:, t, :CONV], rows[:, t], ACT.Silu).then_inc(bent, 1)

            @block.vector
            def _(dve):
                then = Chain(dve, order)
                v = nc.vector
                for t in range(TILES):
                    then(v.bn_stats(stat[:, t], rows[:, t]))
                    then(v.bn_aggr(ms[:, t], stat[:, t]))
                v.tensor_scalar(rstd[:], ms[:, :, 1], LN_EPS, None, ALU.add).then_inc(ready, 1)
                dve.wait_ge(rooted, 1)
                then(v.reciprocal(rstd[:], root[:]))
                dve.wait_ge(loaded, 32)
                for t in range(TILES):
                    then(v.tensor_scalar(rows[:, t], rows[:, t], ms[:, t, 0:1], rstd[:, t:t + 1], ALU.subtract, ALU.mult))
                    then(v.tensor_tensor(rows[:, t], rows[:, t], gain[:], ALU.mult))
                    v.tensor_tensor(rows[:, t], rows[:, t], shift[:], ALU.add).then_inc(shifted, 1)


def rwkv_inputs(nc, g, name, a, pT, o):
    R_AT, K_AT, V_AT, WA_AT, G_AT = 0, RC, 2 * RC, 3 * RC, 3 * RC + 1
    N = 3 * RC + 2
    p = pT[:, 2 * CC:]
    with Stage(nc, name) as s:
        mu = s.sb("mu", [P, N])
        col = s.sb("col", [P, 5, RC])
        w2a2, g2 = s.sb("w2a2", [P, RW]), s.sb("g2", [P, RW])
        pairs, heads = s.sb("pairs", [P, P]), s.sb("heads", [P, 2])
        xm, diff = p, s.sb("diff", [P, SEQ])
        bent = s.sb("bent", [P, SEQ])
        fresh = s.sb("fresh", [P, SEQ])
        logd, total, k2 = o.alpha, o.grown, o.kappa
        a_, tmp = g.hT[:, :RC], g.hT[:, RC:]
        kk = s.sb("kk", [P, RC, SEQ])
        acc = s.ps("acc", [P, 4, SEQ])
        loaded, order, rooted = s.sem("loaded"), s.sem("order"), s.sem("rooted")
        mixed, bent_done, sent, taken = s.sem("mixed"), s.sem("bent_done"), s.sem("sent"), s.sem("taken")
        squared, normed_, grown, ready, rows = s.sem("squared"), s.sem("normed"), s.sem("grown"), s.sem("ready"), s.sem("rows")
        LOADS = 7 * 16
        W0, A0, KK, KA, RK = range(5)
        with nc.Block() as block:
            @block.sync
            def _(sp):
                for dst, src in ((mu, "mu"), (col, "rw_col"), (w2a2, "w2a2"), (g2, "rw_g2"), (pairs, "pairs"),
                                 (heads, "heads"), (fresh, "fresh")):
                    sp.dma_start(dst[:], a[src]).then_inc(loaded, 16)

            @block.scalar
            def _(act):
                act.wait_ge(mixed, N)
                nc.scalar.activation(bent[:LORA], xm[:LORA, WA_AT], ACT.Tanh).then_inc(bent_done, 1)
                nc.scalar.copy(bent[LORA:], xm[LORA:, WA_AT]).then_inc(bent_done, 1)
                nc.scalar.activation(xm[:, G_AT], xm[:, G_AT], ACT.Sigmoid).then_inc(bent_done, 1)
                for c in range(RC):
                    act.wait_ge(sent, 2 * c + 1)
                    nc.scalar.activation(logd[:, c], acc[:, 0], ACT.Sigmoid, bias=col[:, W0, c:c + 1]).then_inc(taken, 1)
                    act.wait_ge(sent, 2 * c + 2)
                    nc.scalar.activation(a_[:, c], acc[:, 1], ACT.Sigmoid, bias=col[:, A0, c:c + 1]).then_inc(taken, 1)
                for c in range(RC):
                    act.wait_ge(sent, 2 * RC + c + 1)
                    nc.scalar.activation(tmp[:, c], acc[:, 2], ACT.Sqrt).then_inc(rooted, 1)
                act.wait_ge(order, 2)
                nc.scalar.activation(o.beta[:], total[:], ACT.Exp, scale=-1.0).then_inc(grown, 1)
                nc.scalar.activation(o.alpha[:], logd[:], ACT.Exp).then_inc(grown, 1)
                act.wait_ge(grown, 1)
                nc.scalar.activation(o.grown[:], total[:], ACT.Exp).then_inc(grown, 1)
                for t in range(TILES):
                    act.wait_ge(rows, t + 1)
                    nc.scalar.copy(o.gate[:, t], acc[:, t % 2]).then_inc(taken, 1)
                act.wait_ge(rows, TILES + 1)
                nc.scalar.copy(o.bonus[:], acc[:, 3, :TILES * RW_HEADS].rearrange("p (t h) -> p t h", t=TILES)).then_inc(taken, 1)

            @block.tensor
            def _(pe):
                pe.wait_ge(loaded, LOADS)
                pe.wait_ge(bent_done, 3)
                for c in range(RC):
                    if c:
                        pe.wait_ge(taken, 2 * c - 1)
                    nc.tensor.matmul(acc[:, 0], w2a2[:LORA, c * P:(c + 1) * P], bent[:LORA], start=True, stop=True).then_inc(sent, 1)
                    if c:
                        pe.wait_ge(taken, 2 * c)
                    nc.tensor.matmul(acc[:, 1], w2a2[LORA:, c * P:(c + 1) * P], bent[LORA:], start=True, stop=True).then_inc(sent, 1)
                for c in range(RC):
                    pe.wait_ge(squared, c + 1)
                    if c:
                        pe.wait_ge(rooted, c)
                    nc.tensor.matmul(acc[:, 2], pairs[:], tmp[:, c], start=True, stop=True).then_inc(sent, 1)
                pe.wait_ge(taken, 2 * RC)
                for t in range(TILES):
                    if t >= 2:
                        pe.wait_ge(taken, 2 * RC + t - 1)
                    nc.tensor.matmul(acc[:, t % 2], xm[:, G_AT, t * P:(t + 1) * P], g2[:], start=True, stop=True).then_inc(rows, 1)
                pe.wait_ge(ready, RC)
                for t in range(TILES):
                    for c in range(RC):
                        at = t * RW_HEADS + 2 * c
                        last = nc.tensor.matmul(acc[:, 3, at:at + 2], kk[:, c, t * P:(t + 1) * P], heads[:], start=True, stop=True)
                last.then_inc(rows, 1)

            @block.vector
            def _(dve):
                v = nc.vector
                steps = s.sem("steps")
                then = Chain(dve, steps)
                dve.wait_ge(loaded, LOADS)
                for n in range(N):
                    then(v.tensor_tensor(diff[:, 1:], p[:, n, :SEQ - 1], p[:, n, 1:], ALU.subtract))
                    then(v.tensor_scalar(diff[:, 0:1], p[:, n, 0:1], -1.0, None, ALU.mult))
                    v.scalar_tensor_tensor(xm[:, n], diff[:], mu[:, n:n + 1], p[:, n], ALU.mult, ALU.add).then_inc(mixed, 1)
                    dve.wait_ge(mixed, n + 1)
                for c in range(RC):
                    then(v.tensor_scalar(kk[:, c], xm[:, K_AT + c], col[:, KK, c:c + 1], None, ALU.mult))
                    v.tensor_tensor(tmp[:, c], kk[:, c], kk[:, c], ALU.mult).then_inc(squared, 1)
                dve.wait_ge(taken, 2 * RC)
                then(v.tensor_scalar(logd[:], logd[:], -math.exp(-0.5), None, ALU.mult))
                for c in range(RC):
                    then(v.tensor_tensor_scan(total[:, c], fresh[:], logd[:, c], 0.0, ALU.mult, ALU.add))
                v.tensor_tensor(logd[:], total[:], logd[:], ALU.subtract).then_inc(order, 2)
                for c in range(RC):
                    then(v.tensor_scalar(k2[:, c], a_[:, c], -1.0, col[:, KA, c:c + 1], ALU.add, ALU.mult))
                    then(v.scalar_tensor_tensor(k2[:, c], k2[:, c], 1.0, xm[:, K_AT + c], ALU.add, ALU.mult))
                dve.wait_ge(rooted, RC)
                then(v.tensor_scalar(tmp, tmp, 1e-12, None, ALU.max))
                then(v.reciprocal(tmp, tmp))
                then(v.tensor_tensor(kk[:], kk[:], tmp, ALU.mult))
                dve.wait_ge(grown, 3)
                then(v.scalar_tensor_tensor(o.alpha[:], o.alpha[:], -1.0, kk[:], ALU.mult, ALU.mult))
                then(v.tensor_tensor(tmp, kk[:], a_, ALU.mult))
                for c in range(RC):
                    v.scalar_tensor_tensor(kk[:, c], xm[:, R_AT + c], col[:, RK, c:c + 1], k2[:, c],
                                           ALU.mult, ALU.mult).then_inc(ready, 1)
                dve.wait_ge(ready, RC)
                then(v.tensor_tensor(o.kappa[:], k2[:], o.beta[:], ALU.mult))
                then(v.tensor_tensor(o.beta[:], o.beta[:], tmp, ALU.mult))
                then(v.tensor_tensor(o.rho[:], o.grown[:], xm[:, R_AT:R_AT + RC], ALU.mult))
                then(v.tensor_copy(o.value[:], xm[:, V_AT:V_AT + RC]))
def rwkv(nc, g, name, a, o, y):
    UNITS = TILES * RW_HEADS
    units = [(t, c, h) for t in range(TILES) for h in range(2) for c in range(RC)]
    cols = [slice((2 * c + h) * RW_DIM, (2 * c + h + 1) * RW_DIM) for _, c, h in units]
    feats = [slice(h * RW_DIM, (h + 1) * RW_DIM) for _, _, h in units]
    toks = [slice(t * P, (t + 1) * P) for t, _, _ in units]
    flat = lambda buf: buf.rearrange("p a n -> p (a n)")
    own = ExitStack()
    rows = {x: own.enter_context(nc.sbuf_tensor(f"{name}_{x}_rows", [P, TILES, RW], F32)) for x in ("alpha", "beta", "kappa", "value")}
    cols_of = {"alpha": o.alpha, "beta": o.beta, "kappa": o.kappa, "value": o.value}
    for x, buf in rows.items():
        turn_cols(nc, g, f"{name}_turn_{x}", cols_of[x], RC, [buf[:, t] for t in range(TILES)])
    solved = own.enter_context(nc.sbuf_tensor(f"{name}_solved", [P, UNITS, P], F32))
    inner = nc.dram_tensor(f"{name}_inner", [BLOCKS, UNITS, SPAN, SPAN], F32, kind="Internal").ap()
    outer = nc.dram_tensor(f"{name}_outer", [BLOCKS, UNITS, SPAN, SPAN], F32, kind="Internal").ap()

    with Stage(nc, f"{name}_solve") as s:
        masks = s.sb("masks", [P, 4, P])
        m_all = s.sb("m_all", [P, UNITS, P])
        m_rows, t_cols = s.sb("m_rows", [P, SPAN, SPAN]), s.sb("t_cols", [P, SPAN, SPAN])
        prod = flat(g.hT[:, :SPAN * SPAN // SEQ]).rearrange("p (s t) -> p s t", s=SPAN)
        acc = s.ps("acc", [P, 4, RC, P])
        loaded, zeroed, paired, masked = s.sem("loaded"), s.sem("zeroed"), s.sem("paired"), s.sem("masked")
        stored, spread, times, found, back, placed = (s.sem(x) for x in ("stored", "spread", "times", "found", "back", "placed"))
        with nc.Block() as block:
            @block.sync
            def _(sp):
                sp.dma_start(masks[:], a["masks"]).then_inc(loaded, 16)
                sp.wait_ge(masked, UNITS // RC)
                for b in range(BLOCKS):
                    part = slice(b * SPAN, (b + 1) * SPAN)
                    sp.dma_start(inner[b].rearrange("m t s -> t m s"), m_all[part, :, part]).then_inc(stored, 16)
                sp.wait_ge(stored, 16 * BLOCKS)
                sp.dma_start(m_rows[:], inner.rearrange("b m t s -> (b m) t s")).then_inc(spread, 16)
                sp.wait_ge(found, SPAN)
                sp.dma_start(outer.rearrange("b m s t -> (b m) s t"), t_cols[:]).then_inc(back, 16)
                sp.wait_ge(back, 16)
                sp.wait_ge(zeroed, 1)
                for b in range(BLOCKS):
                    part = slice(b * SPAN, (b + 1) * SPAN)
                    sp.dma_start(solved[part, :, part], outer[b].rearrange("m s t -> s m t")).then_inc(placed, 16)
                sp.wait_ge(placed, 16 * BLOCKS)

            @block.gpsimd
            def _(pool):
                nc.gpsimd.memset(solved[:], 0.0).then_inc(zeroed, 1)

            @block.tensor
            def _(pe):
                for m, (t, c, h) in enumerate(units):
                    n = m // RC
                    if n >= 4 and c == 0:
                        pe.wait_ge(masked, n - 3)
                    last = nc.tensor.matmul(acc[:, n % 4, c], o.alpha[feats[m], c, toks[m]], o.beta[feats[m], c, toks[m]],
                                            start=True, stop=True)
                    if c == RC - 1:
                        last.then_inc(paired, 1)

            @block.vector
            def _(dve):
                v = nc.vector
                dve.wait_ge(loaded, 16)
                for n in range(UNITS // RC):
                    dve.wait_ge(paired, n + 1)
                    v.tensor_tensor(m_all[:, n * RC:(n + 1) * RC], acc[:, n % 4], masks[:, 0].unsqueeze(1).to_broadcast([P, RC, P]),
                                    ALU.mult).then_inc(masked, 1)
                v.memset(t_cols[:], 0.0).then_inc(times, 1)
                dve.wait_ge(times, 1)
                v.memset(flat(t_cols[:])[:, ::SPAN + 1], 1.0).then_inc(found, 1)
                dve.wait_ge(spread, 16)
                for i in range(1, SPAN):
                    dve.wait_ge(found, i)
                    v.tensor_tensor(prod[:, :i, :i], t_cols[:, :i, :i], m_rows[:, i, :i].unsqueeze(1).to_broadcast([P, i, i]),
                                    ALU.mult).then_inc(times, 1)
                    dve.wait_ge(times, i + 1)
                    v.tensor_reduce(t_cols[:, :i, i], prod[:, :i, :i], AX, ALU.add).then_inc(found, 1)

    step = own.enter_context(nc.sbuf_tensor(f"{name}_step", [P, RC, SPANS, RW_DIM], F32))
    lead = g.hT[:, :RC]
    pieces = [flat(g.hT[:, RC:])[:, :SPANS * RW_DIM], flat(g.hT[:, RC:])[:, SPANS * RW_DIM:], g.mod[:, 0], g.mod[:, 1]]
    new = [x.rearrange("p (n v) -> p n v", n=SPANS) for x in pieces]
    with Stage(nc, f"{name}_spans") as s:
        masks, span = s.sb("masks", [P, 4, P]), s.sb("span", [P, BLOCKS])
        nef = s.sb("nef", [P, 2, 3, P])
        nv, pq = s.sb("nv", [P, 2, RW_DIM]), s.sb("pq", [P, 2, 2, RW_DIM])
        beta_in, value_in, q_in = (s.sb(x, [P, 2, BLOCKS, RW_DIM]) for x in ("beta_in", "value_in", "q_in"))
        pair, mid = s.ps("pair", [P, 2, BANK]), s.ps("mid", [P, 2, BANK])
        out, state = s.ps("out", [P, 2, BANK]), s.ps("state", [P, 2, 2, BLOCKS, RW_DIM])
        loaded, paired, masked, nv_done, nv_kept = (s.sem(x) for x in ("loaded", "paired", "masked", "nv_done", "nv_kept"))
        pq_done, pq_kept, spread, q_spread, out_done = (s.sem(x) for x in ("pq_done", "pq_kept", "spread", "q_spread", "out_done"))
        out_kept, row_kept, state_done, state_kept = (s.sem(x) for x in ("out_kept", "row_kept", "state_done", "state_kept"))
        with nc.Block() as block:
            @block.sync
            def _(sp):
                sp.dma_start(masks[:], a["masks"]).then_inc(loaded, 16)
                sp.dma_start(span[:], a["span"]).then_inc(loaded, 16)

            @block.gpsimd
            def _(pool):
                pool.wait_ge(loaded, 32)
                here = span[:].unsqueeze(2).to_broadcast([P, BLOCKS, RW_DIM])
                for m, (t, c, h) in enumerate(units):
                    if m >= 2:
                        pool.wait_ge(state_done, m - 1)
                    for src, dst in (("beta", beta_in), ("value", value_in)):
                        nc.gpsimd.tensor_tensor(dst[:, m % 2], rows[src][:, t, cols[m]].unsqueeze(1).to_broadcast([P, BLOCKS, RW_DIM]),
                                                here, ALU.mult).then_inc(spread, 1)

            @block.tensor
            def _(pe):
                def open_(m):
                    t, c, h = units[m]
                    if m >= 2:
                        pe.wait_ge(masked, m - 1)
                    for j, (left, right) in enumerate(((o.kappa, o.alpha), (o.beta, o.rho), (o.kappa, o.rho))):
                        last = nc.tensor.matmul(pair[:, m % 2, j * P:(j + 1) * P], left[feats[m], c, toks[m]],
                                                right[feats[m], c, toks[m]], start=True, stop=True)
                    last.then_inc(paired, 1)

                def solve(m):
                    t, c, h = units[m]
                    pe.wait_ge(masked, m + 1)
                    if m >= 2:
                        pe.wait_ge(pq_kept, m - 1)
                    nc.tensor.matmul(mid[:, m % 2, P:P + RW_DIM], solved[:, m], rows["alpha"][:, t, cols[m]], start=True, stop=True)
                    nc.tensor.matmul(mid[:, m % 2, :RW_DIM], nef[:, m % 2, 0], rows["value"][:, t, cols[m]],
                                     start=True, stop=True).then_inc(nv_done, 1)
                    pe.wait_ge(nv_kept, m + 1)
                    nc.tensor.matmul(mid[:, m % 2, P + RW_DIM:2 * P], solved[:, m], nv[:, m % 2], start=True, stop=True).then_inc(pq_done, 1)

                def close(m):
                    t, c, h = units[m]
                    pe.wait_ge(pq_kept, m + 1)
                    if m >= 2:
                        pe.wait_ge(out_kept, m - 1)
                        pe.wait_ge(row_kept, m - 1)
                    nc.tensor.matmul(out[feats[m], m % 2, :P], pq[:, m % 2, 0], nef[:, m % 2, 1], start=True, stop=True)
                    nc.tensor.matmul(out[:, m % 2, P:P + RW_DIM], nef[:, m % 2, 1], pq[:, m % 2, 1], start=True, stop=False)
                    nc.tensor.matmul(out[:, m % 2, P:P + RW_DIM], nef[:, m % 2, 2], rows["value"][:, t, cols[m]],
                                     start=False, stop=True).then_inc(out_done, 1)
                    pe.wait_ge(spread, 2 * m + 2)
                    pe.wait_ge(q_spread, m + 1)
                    if m >= 2:
                        pe.wait_ge(state_kept, 2 * (m - 1))
                    nc.tensor.matmul(state[feats[m], m % 2, 0], pq[:, m % 2, 0], beta_in[:, m % 2], start=True, stop=True)
                    nc.tensor.matmul(state[feats[m], m % 2, 1], rows["beta"][:, t, cols[m]], q_in[:, m % 2], start=True, stop=False)
                    nc.tensor.matmul(state[feats[m], m % 2, 1], rows["kappa"][:, t, cols[m]], value_in[:, m % 2],
                                     start=False, stop=True).then_inc(state_done, 1)

                pe.wait_ge(loaded, 32)
                open_(0)
                for m in range(UNITS):
                    if m + 1 < UNITS:
                        open_(m + 1)
                    solve(m)
                    close(m)

            @block.scalar
            def _(act):
                for m, (t, c, h) in enumerate(units):
                    act.wait_ge(nv_done, m + 1)
                    if m >= 2:
                        act.wait_ge(pq_done, m - 1)
                    nc.scalar.copy(nv[:, m % 2], mid[:, m % 2, :RW_DIM]).then_inc(nv_kept, 1)
                    act.wait_ge(pq_done, m + 1)
                    if m >= 2:
                        act.wait_ge(state_done, m - 1)
                        act.wait_ge(q_spread, m - 1)
                    nc.scalar.copy(pq[:, m % 2].rearrange("p a n -> p (a n)"), mid[:, m % 2, P:2 * P]).then_inc(pq_kept, 1)
                    act.wait_ge(out_kept, m + 1)
                    nc.scalar.copy(y[:, t, CONV + cols[m].start:CONV + cols[m].stop], out[:, m % 2, P:P + RW_DIM]).then_inc(row_kept, 1)

            @block.vector
            def _(dve):
                v = nc.vector

                def mask(m):
                    dve.wait_ge(paired, m + 1)
                    if m >= 2:
                        dve.wait_ge(out_done, m - 1)
                    v.tensor_tensor(nef[:, m % 2], pair[:, m % 2, :3 * P].rearrange("p (j n) -> p j n", j=3), masks[:, 1:],
                                    ALU.mult).then_inc(masked, 1)

                dve.wait_ge(loaded, 32)
                mask(0)
                for m, (t, c, h) in enumerate(units):
                    if m + 1 < UNITS:
                        mask(m + 1)
                    dve.wait_ge(pq_kept, m + 1)
                    if m >= 2:
                        dve.wait_ge(state_done, m - 1)
                    v.tensor_tensor(q_in[:, m % 2], pq[:, m % 2, 1].unsqueeze(1).to_broadcast([P, BLOCKS, RW_DIM]),
                                    span[:].unsqueeze(2).to_broadcast([P, BLOCKS, RW_DIM]), ALU.mult).then_inc(q_spread, 1)
                    dve.wait_ge(out_done, m + 1)
                    v.tensor_tensor(lead[feats[m], c, toks[m]], out[feats[m], m % 2, :P], o.rho[feats[m], c, toks[m]],
                                    ALU.add).then_inc(out_kept, 1)
                    dve.wait_ge(state_done, m + 1)
                    spans = slice(t * BLOCKS, (t + 1) * BLOCKS)
                    v.tensor_tensor(step[feats[m], c, spans], state[feats[m], m % 2, 0],
                                    g.ident[feats[m], feats[m]].unsqueeze(1).to_broadcast([RW_DIM, BLOCKS, RW_DIM]), ALU.add).then_inc(state_kept, 1)
                    ends = o.grown[feats[m], c, t * P + SPAN - 1:(t + 1) * P:SPAN]
                    v.tensor_tensor(new[c][feats[m], spans], state[feats[m], m % 2, 1],
                                    ends.unsqueeze(2).to_broadcast([RW_DIM, BLOCKS, RW_DIM]), ALU.mult).then_inc(state_kept, 1)

    z = [flat((o.alpha, o.beta)[c // 2][:])[:, (c % 2) * SPANS * RW_DIM:(c % 2 + 1) * SPANS * RW_DIM].rearrange(
        "p (n v) -> p n v", n=SPANS) for c in range(RC)]
    apart = [flat(b[:]).rearrange("p (n h v) -> p n h v", n=SPANS, h=2) for b in (o.kappa, o.rho, rows["alpha"], rows["beta"])]
    with Stage(nc, f"{name}_state") as s:
        heads = s.sb("heads", [P, 2])
        acc = s.ps("acc", [P, 2, 2, RC, RW_DIM])
        rest = s.ps("rest", [P, 2, BANK])
        loaded, moved, stepped, apart_done, inter, added = (s.sem(x) for x in ("loaded", "moved", "stepped", "apart_done", "inter", "added"))
        with nc.Block() as block:
            @block.sync
            def _(sp):
                sp.dma_start(heads[:], a["heads"]).then_inc(loaded, 16)

            @block.tensor
            def _(pe):
                for n in range(1, SPANS - 1):
                    pe.wait_ge(stepped, 2 * RC * n)
                    for c in range(RC):
                        for h in range(2):
                            f = slice(h * RW_DIM, (h + 1) * RW_DIM)
                            last = nc.tensor.matmul(acc[f, n % 2, h, c], step[f, c, n], z[c][f, n], start=True, stop=True)
                    last.then_inc(moved, 1)
                pe.wait_ge(apart_done, 2 * RC)
                for t in range(TILES):
                    if t >= 2:
                        pe.wait_ge(added, t - 1)
                    for b in range(BLOCKS):
                        for c in range(RC):
                            at = t * P + b * SPAN
                            last = nc.tensor.matmul(rest[b * SPAN:(b + 1) * SPAN, t % 2, c * P:(c + 1) * P], lead[:, c, at:at + SPAN],
                                                    apart[c][:, t * BLOCKS + b], start=True, stop=True)
                    last.then_inc(inter, 1)

            @block.vector
            def _(dve):
                v = nc.vector
                for c in range(RC):
                    v.memset(z[c][:, 0], 0.0).then_inc(stepped, 1)
                    v.tensor_copy(z[c][:, 1], new[c][:, 0]).then_inc(stepped, 1)
                for n in range(1, SPANS - 1):
                    dve.wait_ge(moved, n)
                    for c in range(RC):
                        for h in range(2):
                            f = slice(h * RW_DIM, (h + 1) * RW_DIM)
                            v.scalar_tensor_tensor(z[c][f, n + 1], acc[f, n % 2, h, c], o.grown[f, c, (n + 1) * SPAN - 1:(n + 1) * SPAN],
                                                   new[c][f, n], ALU.mult, ALU.add).then_inc(stepped, 1)
                dve.wait_ge(loaded, 16)
                dve.wait_ge(stepped, 2 * RC * (SPANS - 1))
                for c in range(RC):
                    for h in range(2):
                        v.tensor_scalar(apart[c][:, :, h], z[c], heads[:, h:h + 1], None, ALU.mult).then_inc(apart_done, 1)
                for t in range(TILES):
                    dve.wait_ge(inter, t + 1)
                    v.tensor_tensor(y[:, t, CONV:], y[:, t, CONV:], rest[:, t % 2], ALU.add).then_inc(added, 1)

    with Stage(nc, f"{name}_norm") as s:
        gain, shift = s.sb("gain", [P, RW]), s.sb("shift", [P, RW])
        square = s.sb("square", [P, 2, RW_HEADS, RW_DIM])
        mean, var, root = (s.sb(x, [P, TILES, RW_HEADS]) for x in ("mean", "var", "root"))
        loaded, order, rooted, ready = s.sem("loaded"), s.sem("order"), s.sem("rooted"), s.sem("ready")
        wide = [P, RW_HEADS, RW_DIM]
        with nc.Block() as block:
            @block.sync
            def _(sp):
                sp.dma_start(gain[:], a["rw_gain"]).then_inc(loaded, 16)
                sp.dma_start(shift[:], a["rw_shift"]).then_inc(loaded, 16)

            @block.scalar
            def _(act):
                act.wait_ge(ready, 1)
                nc.scalar.activation(root[:], var[:], ACT.Sqrt).then_inc(rooted, 1)

            @block.vector
            def _(dve):
                v = nc.vector
                then = Chain(dve, order)
                part = lambda buf, t: buf[:, t].rearrange("p (h d) -> p h d", d=RW_DIM)
                ys = [y[:, t, CONV:].rearrange("p (h d) -> p h d", d=RW_DIM) for t in range(TILES)]
                for t in range(TILES):
                    then(v.tensor_reduce(mean[:, t], ys[t], AX, ALU.add))
                then(v.tensor_scalar(mean[:], mean[:], 1.0 / RW_DIM, None, ALU.mult))
                for t in range(TILES):
                    then(v.tensor_tensor(ys[t], ys[t], mean[:, t].unsqueeze(2).to_broadcast(wide), ALU.subtract))
                    then(v.tensor_tensor(square[:, t % 2], ys[t], ys[t], ALU.mult))
                    then(v.tensor_reduce(var[:, t], square[:, t % 2], AX, ALU.add))
                v.tensor_scalar(var[:], var[:], 1.0 / RW_DIM, GN_EPS, ALU.mult, ALU.add).then_inc(ready, 1)
                dve.wait_ge(rooted, 1)
                then(v.reciprocal(var[:], root[:]))
                dve.wait_ge(loaded, 32)
                for t in range(TILES):
                    then(v.tensor_tensor(ys[t], ys[t], var[:, t].unsqueeze(2).to_broadcast(wide), ALU.mult))
                    then(v.tensor_tensor(y[:, t, CONV:], y[:, t, CONV:], gain[:], ALU.mult))
                    then(v.tensor_tensor(y[:, t, CONV:], y[:, t, CONV:], shift[:], ALU.add))
                    then(v.tensor_tensor(square[:, t % 2], part(rows["value"], t), o.bonus[:, t].unsqueeze(2).to_broadcast(wide), ALU.mult))
                    then(v.tensor_tensor(ys[t], ys[t], square[:, t % 2], ALU.add))
                    then(v.tensor_tensor(y[:, t, CONV:], y[:, t, CONV:], o.gate[:, t], ALU.mult))
    own.close()


def layer_norm_rows(nc, g, name, g_dram, b_dram):
    with Stage(nc, name) as s:
        gain, shift = s.sb("gain", [P, D]), s.sb("shift", [P, D])
        stat, ms = s.sb("stat", [P, TILES, 2, 6]), s.sb("ms", [P, TILES, 2])
        root, rstd = s.sb("root", [P, TILES]), s.sb("rstd", [P, TILES])
        loaded, order, rooted, ready = s.sem("loaded"), s.sem("order"), s.sem("rooted"), s.sem("ready")
        with nc.Block() as block:
            @block.sync
            def _(sp):
                sp.dma_start(gain[:], g_dram).then_inc(loaded, 16)
                sp.dma_start(shift[:], b_dram).then_inc(loaded, 16)

            @block.scalar
            def _(act):
                act.wait_ge(ready, 1)
                nc.scalar.activation(root[:], rstd[:], ACT.Sqrt).then_inc(rooted, 1)

            @block.vector
            def _(dve):
                then = Chain(dve, order)
                v = nc.vector
                for t in range(TILES):
                    for half in range(2):
                        then(v.bn_stats(stat[:, t, half], g.x[:, t, half * D // 2:(half + 1) * D // 2]))
                    then(v.bn_aggr(ms[:, t], stat[:, t]))
                v.tensor_scalar(rstd[:], ms[:, :, 1], LN_EPS, None, ALU.add).then_inc(ready, 1)
                dve.wait_ge(rooted, 1)
                then(v.reciprocal(rstd[:], root[:]))
                dve.wait_ge(loaded, 32)
                for t in range(TILES):
                    then(v.tensor_scalar(g.x[:, t], g.x[:, t], ms[:, t, 0:1], rstd[:, t:t + 1], ALU.subtract, ALU.mult))
                    then(v.tensor_tensor(g.x[:, t], g.x[:, t], gain[:], ALU.mult))
                    then(v.tensor_tensor(g.x[:, t], g.x[:, t], shift[:], ALU.add))
KEYS, TOP, PEER_HEADS = 128, 16, 8
PICKS = PEER_HEADS * TOP
GROUP = 8
PART = 32


def top16(then, v, values, work, at):
    then(v.max(values[:, :8], work))
    then(v.max_index(at[:, :8], values[:, :8], work))
    then(v.match_replace(work, values[:, :8], work, NEG))
    then(v.max(values[:, 8:], work))
    then(v.max_index(at[:, 8:], values[:, 8:], work))


def peer_pick(nc, g, name, qT, keys_dram, picks):
    with Stage(nc, name) as s:
        keys = s.sb("keys", [P, 2 * PEER_HEADS, KEYS])
        score = s.sb("score", [P, 2, 4, KEYS])
        value, at = s.sb("value", [P, 2 * PEER_HEADS, TOP]), s.sb("at", [P, 2 * PEER_HEADS, TOP], U32)
        key = s.sb("key", [P, 2 * PEER_HEADS, TOP])
        both = s.sb("both", [P, TOP, TOP])
        best, place = s.sb("best", [P, PEER_HEADS, TOP]), s.sb("place", [P, PEER_HEADS, TOP], U32)
        half_at, half = s.sb("half_at", [P, PEER_HEADS, TOP], U32), s.sb("half", [P, PEER_HEADS, TOP])
        match = s.sb("match", [P, PEER_HEADS, TOP, TOP])
        low, raised = s.sb("low", [P, PEER_HEADS, TOP]), s.sb("raised", [P, 2, PEER_HEADS, TOP])
        total, inv = s.sb("total", [P, PEER_HEADS]), s.sb("inv", [P, PEER_HEADS])
        found = s.sb("found", [P, 2, 3, PICKS])
        acc, pt = s.ps("acc", [P, 2, 4, KEYS]), s.ps("pt", [P, 2, 3, P])
        loaded, scored, kept, order, used = (s.sem(x) for x in ("loaded", "scored", "kept", "order", "used"))
        low_done, raised_done, picked, turned, stored = (s.sem(x) for x in ("low_done", "raised_done", "picked", "turned", "stored"))
        SETS = 2 * PEER_HEADS // 4
        wide = [P, PEER_HEADS, TOP, TOP]
        with nc.Block() as block:
            @block.sync
            def _(sp):
                sp.dma_start(keys[:], keys_dram).then_inc(loaded, 16)

            @block.tensor
            def _(pe):
                def score_tile(t):
                    for q in range(SETS):
                        n = t * SETS + q
                        if n >= 2:
                            pe.wait_ge(kept, n - 1)
                        for j in range(4):
                            last = nc.tensor.matmul(acc[:, n % 2, j], qT[:, 4 * q + j, t * P:(t + 1) * P], keys[:, 4 * q + j],
                                                    start=True, stop=True)
                        last.then_inc(scored, 1)

                def turn(t):
                    pe.wait_ge(picked, t + 1)
                    if t >= 2:
                        pe.wait_ge(stored, t - 1)
                    for j in range(3):
                        last = nc.tensor.transpose(pt[:, t % 2, j], found[:, t % 2, j], g.ident[:])
                    last.then_inc(turned, 1)

                pe.wait_ge(loaded, 16)
                for t in range(TILES):
                    score_tile(t)
                    if t:
                        turn(t - 1)
                turn(TILES - 1)

            @block.scalar
            def _(act):
                for t in range(TILES):
                    for q in range(SETS):
                        n = t * SETS + q
                        act.wait_ge(scored, n + 1)
                        if n >= 2:
                            act.wait_ge(used, n - 1)
                        nc.scalar.copy(score[:, n % 2], acc[:, n % 2]).then_inc(kept, 1)
                    if t:
                        act.wait_ge(turned, t)
                        nc.scalar.copy(picks[:, :, (t - 1) * P:t * P], pt[:, (t - 1) % 2]).then_inc(stored, 1)
                    act.wait_ge(low_done, t + 1)
                    nc.scalar.activation(raised[:, t % 2], low[:], ACT.Exp).then_inc(raised_done, 1)
                act.wait_ge(turned, TILES)
                nc.scalar.copy(picks[:, :, (TILES - 1) * P:], pt[:, (TILES - 1) % 2]).then_inc(stored, 1)

            @block.vector
            def _(dve):
                v = nc.vector
                then = Chain(dve, order)
                for t in range(TILES):
                    for q in range(SETS):
                        n = t * SETS + q
                        dve.wait_ge(kept, n + 1)
                        for j in range(4):
                            top16(then, v, value[:, 4 * q + j], score[:, n % 2, j], at[:, 4 * q + j])
                        dve.sem_inc(used, 1)
                    then(v.tensor_copy(key[:], at[:]))
                    for h in range(PEER_HEADS):
                        then(v.tensor_tensor(both[:], value[:, 2 * h].unsqueeze(2).to_broadcast([P, TOP, TOP]),
                                             value[:, 2 * h + 1].unsqueeze(1).to_broadcast([P, TOP, TOP]), ALU.add))
                        top16(then, v, best[:, h], both[:].rearrange("p a b -> p (a b)"), place[:, h])
                    if t:
                        dve.wait_ge(raised_done, t)
                    v.tensor_tensor(low[:], best[:], best[:, :, 0:1].to_broadcast([P, PEER_HEADS, TOP]), ALU.subtract).then_inc(low_done, 1)
                    if t >= 2:
                        dve.wait_ge(turned, t - 1)
                    for j, (op, n) in enumerate(((ALU.logical_shift_right, 4), (ALU.bitwise_and, TOP - 1))):
                        then(v.tensor_scalar(half_at[:], place[:], n, None, op))
                        then(v.tensor_copy(half[:], half_at[:]))
                        for h in range(PEER_HEADS):
                            then(v.tensor_tensor(match[:, h], half[:, h].unsqueeze(2).to_broadcast([P, TOP, TOP]),
                                                 g.iota[:, :TOP].unsqueeze(1).to_broadcast([P, TOP, TOP]), ALU.is_equal))
                            then(v.tensor_tensor(match[:, h], match[:, h], key[:, 2 * h + j].unsqueeze(1).to_broadcast([P, TOP, TOP]),
                                                 ALU.mult))
                        then(v.tensor_reduce(found[:, t % 2, j].rearrange("p (h k) -> p h k", h=PEER_HEADS), match[:], AX, ALU.add))
                    dve.wait_ge(raised_done, t + 1)
                    then(v.tensor_reduce(total[:], raised[:, t % 2], AX, ALU.add))
                    then(v.reciprocal(inv[:], total[:]))
                    v.tensor_tensor(found[:, t % 2, 2].rearrange("p (h k) -> p h k", h=PEER_HEADS), raised[:, t % 2],
                                    inv[:].unsqueeze(2).to_broadcast([P, PEER_HEADS, TOP]), ALU.mult).then_inc(picked, 1)


def peer_prepare(nc, g, name, picks, keys_of, gates, numbers):
    with Stage(nc, name) as s:
        rest = s.sb("rest", [P, 2, SEQ])
        order, copied = s.sem("order"), s.sem("copied")
        with nc.Block() as block:
            @block.scalar
            def _(act):
                nc.scalar.copy(keys_of[:], picks[:, :2]).then_inc(copied, 1)
                nc.scalar.copy(numbers[:], g.iota[:].unsqueeze(2).to_broadcast([P, KEYS, GROUP])).then_inc(copied, 1)

            @block.vector
            def _(dve):
                then = Chain(dve, order)
                left = picks[:, 2]
                for j in range(3):
                    then(nc.vector.tensor_copy(gates[:, j], left))
                    if j < 2:
                        then(nc.vector.tensor_tensor(rest[:, j], left, gates[:, j], ALU.subtract))
                        left = rest[:, j]


def peer_weights(nc, name, keys_of, gates, numbers, part, weights):
    SLOTS = 4
    with Stage(nc, name) as s:
        first = s.sb("first", [P, SLOTS, KEYS, GROUP], BF16)
        match, second = s.sb("match", [P, SLOTS, PART, GROUP], BF16), s.sb("second", [P, SLOTS, 3, PART, GROUP], BF16)
        acc = s.ps("acc", [P, SLOTS, BANK])
        matched, first_made, second_made = s.sem("matched"), s.sem("first_made"), s.sem("second_made")
        summed, kept = s.sem("summed"), s.sem("kept")
        LOOPS = SEQ // (SLOTS * GROUP)
        with nc.Block() as block:
            @block.vector
            def _(dve):
                def spread(n, j, width):
                    return keys_of[:, j, bass.ds(n * GROUP, GROUP)].unsqueeze(1).to_broadcast([P, width, GROUP])

                with dve.Fori(0, LOOPS) as i:
                    for u in range(SLOTS):
                        n = SLOTS * i + u
                        dve.wait_ge(summed, n + 1)
                        nc.vector.tensor_tensor(match[:, u], numbers[:, part * PART:(part + 1) * PART], spread(n, 1, PART),
                                                ALU.is_equal).then_inc(matched, 1)
                        nc.vector.tensor_tensor(first[:, u], numbers[:], spread(n, 0, KEYS), ALU.is_equal).then_inc(first_made, 1)
                        dve.wait_ge(matched, n + 1)
                        nc.vector.tensor_tensor(
                            second[:, u], match[:, u].unsqueeze(1).to_broadcast([P, 3, PART, GROUP]),
                            gates[:, :, bass.ds(n * GROUP, GROUP)].unsqueeze(2).to_broadcast([P, 3, PART, GROUP]),
                            ALU.mult).then_inc(second_made, 1)

            @block.tensor
            def _(pe):
                pe.sem_inc(summed, SLOTS)
                with pe.Fori(0, LOOPS) as i:
                    for u in range(SLOTS):
                        n = SLOTS * i + u
                        pe.wait_ge(first_made, n + 1)
                        pe.wait_ge(second_made, n + 1)
                        pe.wait_ge(kept, n + 1)
                        for j in range(GROUP):
                            for k in range(3):
                                last = nc.tensor.matmul(acc[:, u, j * PART:(j + 1) * PART], first[:, u, :, j], second[:, u, k, :, j],
                                                        start=(k == 0), stop=(k == 2))
                        last.then_inc(summed, 1)

            @block.scalar
            def _(act):
                act.sem_inc(kept, SLOTS)
                with act.Fori(0, LOOPS) as i:
                    for u in range(SLOTS):
                        n = SLOTS * i + u
                        act.wait_ge(summed, n + 1 + SLOTS)
                        nc.scalar.copy(weights[:, bass.ds(n * GROUP, GROUP), :],
                                       acc[:, u, :GROUP * PART].rearrange("p (t j) -> p t j", t=GROUP)).then_inc(kept, 1)


def peer(nc, g, name, a):
    with ExitStack() as own:
        keys_of = own.enter_context(nc.sbuf_tensor(f"{name}_keys_of", [P, 2, SEQ], BF16))
        gates = own.enter_context(nc.sbuf_tensor(f"{name}_gates", [P, 3, SEQ], BF16))
        numbers = own.enter_context(nc.sbuf_tensor(f"{name}_numbers", [P, KEYS, GROUP], BF16))
        with nc.sbuf_tensor(f"{name}_picks", [P, 3, SEQ], F32) as picks:
            with nc.sbuf_tensor(f"{name}_qT", [P, 2 * PEER_HEADS, SEQ], F32) as qT:
                project_cols(nc, f"{name}_q", g.hT, KD, a["peer_wq"], 2 * PEER_HEADS, qT)
                peer_pick(nc, g, f"{name}_pick", qT, a["peer_keys"], picks)
            peer_prepare(nc, g, f"{name}_prepare", picks, keys_of, gates, numbers)
        weights = own.enter_context(nc.sbuf_tensor(f"{name}_weights", [P, SEQ, PART], F32))
        hi, lo = (own.enter_context(nc.sbuf_tensor(f"{name}_h_{x}", [P, KD, SEQ], F32R)) for x in ("hi", "lo"))
        split_rows(nc, g, f"{name}_split", hi, lo)
        acc = g.mod[:, 0:TILES].rearrange("p t (h n) -> p t h n", n=BANK)
        with Stage(nc, f"{name}_zero") as s:
            zeroed = s.sem("zeroed")
            with nc.Block() as block:
                @block.vector
                def _(dve):
                    nc.vector.memset(acc, 0.0).then_inc(zeroed, 1)

        def weight(n):
            return weights[:, :, n] if isinstance(n, int) else weights[:, :, bass.ds(n, 1)].rearrange("p t o -> p (t o)")

        for part in range(KEYS // PART):
            peer_weights(nc, f"{name}_weights{part}", keys_of, gates, numbers, part, weights)
            expert_chunks(nc, g, f"{name}_part{part}", [a["peer_u"]], a["peer_v"], part * PART, PART, hi, lo,
                          ACT.Gelu, weight, None, acc)
        with Stage(nc, f"{name}_sum") as s:
            gated, added = s.sem("gated"), s.sem("added")
            with nc.Block() as block:
                @block.vector
                def _(dve):
                    for t in range(TILES):
                        rows = g.mod[:, t]
                        nc.vector.tensor_tensor(rows, rows, g.mod[:, 5], ALU.mult).then_inc(gated, 1)
                        dve.wait_ge(gated, t + 1)
                        nc.vector.scalar_tensor_tensor(g.x[:, t], g.x[:, t], ALPHA, rows, ALU.mult, ALU.add).then_inc(added, 1)
def build_program(nc, a, out):
    with ExitStack() as own:
        def sb(name, shape, dtype=F32):
            return own.enter_context(nc.sbuf_tensor(name, shape, dtype))

        g = Global()
        g.x = sb("x", [P, TILES, D])
        g.hT = sb("hT", [P, KD, SEQ])
        g.mod = sb("mod", [P, 6, D])
        g.ident, g.causal, g.iota = sb("ident", [P, P]), sb("causal", [P, P]), sb("iota", [P, P])
        g.comb = sb("comb", [P, TILES, EXPERTS])
        constants(nc, a, g)

        modulation(nc, g, "ada0", a["c"], a["w_ada0"], a["b_ada"][0:1])
        normed(nc, g, "fox_norm", "rms", 1, 0, a["mix_gain"][0])
        fox(nc, g, a)
        ada1, cond = Global(), Global()
        ada1.c_dram, ada1.w, cond.c_dram, cond.w = a["c"], a["w_ada1"], a["c_2"], a["cond_w"]
        ada1.sums, cond.sums = (nc.dram_tensor(f"{x}_side_sums", [6 * D // SIDE, P, SIDE], F32, kind="Internal").ap() for x in ("ada1", "cond"))
        moe(nc, g, a, 0, ada1)

        side_modulation(nc, g, "ada1", ada1.sums, a["b_ada"][1:2])
        normed(nc, g, "mla_norm", "rms", 1, 0, a["mix_gain"][1])
        mla(nc, g, a)
        moe(nc, g, a, 1, cond)

        side_modulation(nc, g, "cond", cond.sums, a["cond_b"])
        normed(nc, g, "hybrid_norm", "ln", 1, 0)
        hybrid(nc, g, a)
        layer_norm_rows(nc, g, "ln1", a["ln1_g"], a["ln1_b"])
        normed(nc, g, "peer_norm", "ln", 4, 3)
        peer(nc, g, "peer", a)
        layer_norm_rows(nc, g, "ln2", a["ln2_g"], a["ln2_b"])

        with Stage(nc, "store") as s:
            stored = s.sem("stored")
            with nc.Block() as block:
                @block.sync
                def _(sp):
                    sp.dma_start(out.rearrange("o (t p) d -> p (o t) d", p=P), g.x[:]).then_inc(stored, 16)
                    sp.wait_ge(stored, 16)


class Global:
    pass


def fox(nc, g, a):
    with ExitStack() as own:
        qkv = own.enter_context(nc.sbuf_tensor("fox_qkv", [P, TILES, 3 * D], F32))
        o = own.enter_context(nc.sbuf_tensor("fox_o", [P, TILES, D], F32))
        cum_q = own.enter_context(nc.sbuf_tensor("fox_cum_q", [P, TILES, HEADS], F32))
        cum_k = own.enter_context(nc.sbuf_tensor("fox_cum_k", [P, HEADS, SEQ], F32))
        sums = nc.dram_tensor("fox_sums", [HEADS, SEQ], F32, kind="Internal").ap()
        q, k, v = (qkv[:, :, j * D:(j + 1) * D] for j in range(3))
        project_rows(nc, "fox_in", g.hT, KD, a["fox_w_in"], 6, BANK, keep=qkv)
        forget_gates(nc, g, "fox_gates", a["fox_w_f"], a["fox_b_f"], sums, cum_q, cum_k)
        head_norms(nc, "fox_heads", [(q, a["fox_q_norm"], FOX_DK ** -0.5), (k, a["fox_k_norm"], 1.0)], FOX_DK)
        attention(nc, g, "fox_attn", q, k, v, o, FOX_DK, cum_q=cum_q, cum_k=cum_k)
        turn_rows(nc, g, "fox_turn", o, KD, g.hT)
        project_rows(nc, "fox_out", g.hT, KD, a["fox_w_out"], 2, BANK, gate=g.mod[:, 2], x=g.x)


def mla(nc, g, a):
    with ExitStack() as own:
        def sb(name, shape):
            return own.enter_context(nc.sbuf_tensor(f"mla_{name}", shape, F32))

        q, k, kv = sb("q", [P, TILES, HEADS * QK]), sb("k", [P, TILES, HEADS * QK]), sb("kv", [P, TILES, HEADS * (NOPE + DV)])
        low, o = sb("low", [P, TILES, Q_RANK + KV_RANK + ROPE]), sb("o", [P, TILES, HEADS * DV])
        cos, sin = sb("cos", [P, TILES, ROPE // 2]), sb("sin", [P, TILES, ROPE // 2])
        kq, kkv = Q_RANK // P, KV_RANK // P
        project_rows(nc, "mla_in", g.hT, KD, a["mla_w_in"], 2, (Q_RANK + KV_RANK + ROPE) // 2, keep=low)
        head_norms(nc, "mla_q_lat", [(low[:, :, :Q_RANK], a["mla_q_lat"], 1.0)], Q_RANK, heads=1)
        head_norms(nc, "mla_kv_lat", [(low[:, :, Q_RANK:Q_RANK + KV_RANK], a["mla_kv_lat"], 1.0)], KV_RANK, heads=1)
        turn_rows(nc, g, "mla_turn_low", low, kq + kkv, g.hT)
        project_rows(nc, "mla_uq", g.hT[:, :kq], kq, a["mla_w_uq"], 4, HEADS * QK // 4, keep=q)
        project_rows(nc, "mla_ukv", g.hT[:, kq:kq + kkv], kkv, a["mla_w_ukv"], 4, BANK, keep=kv)
        split_latents(nc, g, "mla_split", kv, low[:, :, Q_RANK + KV_RANK:], a["positions"], a["freq"], k, cos, sin)
        head_norms(nc, "mla_heads", [(q, a["mla_q_norm"], QK ** -0.5), (k, a["mla_k_norm"], 1.0)], QK)
        rotate(nc, "mla_rotate", (q, k), cos, sin)
        attention(nc, g, "mla_attn", q, k, kv, o, QK, v_step=NOPE + DV, v_at=NOPE)
        turn_rows(nc, g, "mla_turn", o, KD, g.hT)
        project_rows(nc, "mla_out", g.hT, KD, a["mla_w_out"], 2, BANK, gate=g.mod[:, 2], x=g.x)


def moe(nc, g, a, layer, side):
    normed(nc, g, f"moe_norm{layer}", "rms", 4, 3, a["ffn_gain"][layer])
    route(nc, g, f"moe_route{layer}", a["moe_w_route"][layer], a["moe_b_route"][layer])
    experts(nc, g, f"moe{layer}", a["moe_gate"][layer], a["moe_up"][layer], a["moe_down"][layer], g.mod[:, 5], side)


def hybrid(nc, g, a):
    with ExitStack() as own:
        y = own.enter_context(nc.sbuf_tensor("hybrid_y", [P, TILES, D], F32))
        o = Global()
        o.alpha, o.beta, o.kappa, o.rho, o.grown, o.value = (
            own.enter_context(nc.sbuf_tensor(f"rw_{x}", [P, RC, SEQ], F32))
            for x in ("alpha", "beta", "kappa", "rho", "grown", "value"))
        o.gate = own.enter_context(nc.sbuf_tensor("rw_gate", [P, TILES, RW], F32))
        o.bonus = own.enter_context(nc.sbuf_tensor("rw_bonus", [P, TILES, RW_HEADS], F32))
        with nc.sbuf_tensor("hybrid_pT", [P, IN_CHUNKS, SEQ], F32) as pT:
            with nc.sbuf_tensor("conv_cols", [P, CC, SEQ], F32) as conv:
                hybrid_in(nc, g, "hybrid_in", a["w_in"], a["conv_w"], a["conv_b"], pT, conv)
                with nc.sbuf_tensor("conv_rows", [P, TILES, CONV], F32) as conv_rows:
                    turn_cols(nc, g, "conv_turn", conv, CC, [conv_rows[:, t] for t in range(TILES)])
                    conv_norm(nc, g, "conv_norm", conv_rows, a["conv_gain"], a["conv_shift"], y)
            rwkv_inputs(nc, g, "rw_in", a, pT, o)
        rwkv(nc, g, "rw", a, o, y)
        turn_rows(nc, g, "hybrid_turn", y, KD, g.hT)
        project_rows(nc, "hybrid_out", g.hT, KD, a["w_out"], 2, BANK, gate=g.mod[:, 2], x=g.x, alpha=ALPHA)




def row_chunks(w, width):
    k, n = w.shape
    return w.reshape(k // P, P, n // width, width).transpose(2, 1, 0, 3)


def in_columns(v):
    return v.reshape(-1, P).T


def everywhere(v):
    return np.broadcast_to(v[..., None, :], v.shape[:-1] + (P, v.shape[-1]))


def shape_constants():
    i = np.arange(P)
    same = i[:, None] // SPAN == i[None] // SPAN
    before, upto = i[:, None] < i[None], i[:, None] <= i[None]
    half = ROPE // 2
    return {
        "ident": np.eye(P),
        "causal": np.where(i[None] <= i[:, None], 0.0, NEG),
        "iota": np.broadcast_to(np.arange(P), (P, P)),
        "freq": everywhere(np.float32(10000.0) ** (-np.arange(half, dtype=np.float32) / np.float32(half))),
        "masks": np.stack([same & before.T, same & before, same & upto, same & upto], 1),
        "span": i[:, None] // SPAN == np.arange(BLOCKS)[None],
        "pairs": i[:, None] // RW_DIM == i[None] // RW_DIM,
        "heads": i[:, None] // RW_DIM == np.arange(2)[None],
        "fresh": np.broadcast_to(np.arange(SEQ) % SPAN != 0, (P, SEQ)),
    }


def laid_out(x):
    fox_w = x["fox_w_in"][0]
    route_w = np.concatenate([x["moe_w_grp"], x["moe_w_rt"]], 2)
    route_b = np.concatenate([x["moe_b_grp"], x["moe_b_rt"]], 1)
    layers = route_w.shape[0]

    def raising(w):
        return w.reshape(layers, EXPERTS, KD, P, D_EXPERT // P, P).transpose(0, 1, 4, 3, 2, 5).reshape(layers, -1, P, KD, P)

    return {
        "x": x["x"],
        "c": in_columns(x["c"][0]), "c_2": in_columns(x["c_2"][0]),
        "positions": in_columns(x["positions"][0]),
        "w_ada0": row_chunks(x["w_ada"][0], BANK), "w_ada1": row_chunks(x["w_ada"][1], SIDE), "b_ada": x["b_ada"],
        "cond_w": row_chunks(x["cond_w_2"], SIDE), "cond_b": x["cond_b_2"][None],
        "mix_gain": everywhere(x["mix_norm"]), "ffn_gain": everywhere(x["ffn_norm"]),
        "fox_w_in": row_chunks(fox_w[:, :3 * D], BANK),
        "fox_w_f": fox_w[:, 3 * D:].reshape(KD, P, HEADS).transpose(1, 0, 2),
        "fox_b_f": x["fox_b_f"][0][:, None],
        "fox_q_norm": everywhere(x["fox_q_norm"][0]), "fox_k_norm": everywhere(x["fox_k_norm"][0]),
        "fox_w_out": row_chunks(x["fox_w_out"][0], BANK),
        "mla_w_in": row_chunks(x["mla_w_in"][0], (Q_RANK + KV_RANK + ROPE) // 2),
        "mla_q_lat": everywhere(x["mla_q_lat_norm"][0]), "mla_kv_lat": everywhere(x["mla_kv_lat_norm"][0]),
        "mla_w_uq": row_chunks(x["mla_w_uq"][0], HEADS * QK // 4), "mla_w_ukv": row_chunks(x["mla_w_ukv"][0], BANK),
        "mla_q_norm": everywhere(x["mla_q_norm"][0]), "mla_k_norm": everywhere(x["mla_k_norm"][0]),
        "mla_w_out": row_chunks(x["mla_w_out"][0], BANK),
        "moe_w_route": route_w.reshape(layers, KD, P, -1).transpose(0, 2, 1, 3), "moe_b_route": everywhere(route_b),
        "moe_gate": raising(x["moe_w_gate"]), "moe_up": raising(x["moe_w_up"]),
        "moe_down": x["moe_w_down"].reshape(layers, -1, P, D),
        "w_in": row_chunks(x["w_in_2"], P), "mu": in_columns(x["mu_shift_2"]),
        "conv_w": x["conv_w_2"].T.reshape(CC, P, TAPS).transpose(1, 0, 2), "conv_b": in_columns(x["conv_b_2"]),
        "conv_gain": everywhere(x["conv_ln_g_2"]), "conv_shift": everywhere(x["conv_ln_b_2"]),
        "rw_col": np.stack([in_columns(x[n].reshape(-1)) for n in ("rw_w0_2", "rw_a0_2", "rw_kk_2", "rw_ka_2", "rw_rk_2")], 1),
        "w2a2": np.concatenate([x["rw_w2_2"], x["rw_a2_2"]], 0), "rw_g2": x["rw_g2_2"],
        "rw_gain": everywhere(x["rw_lnx_g_2"]), "rw_shift": everywhere(x["rw_lnx_b_2"]),
        "w_out": row_chunks(x["w_out_2"], BANK),
        "ln1_g": everywhere(x["ln1_g_2"]), "ln1_b": everywhere(x["ln1_b_2"]),
        "ln2_g": everywhere(x["ln2_g_2"]), "ln2_b": everywhere(x["ln2_b_2"]),
        "peer_wq": row_chunks(x["peer_wq_2"], P),
        "peer_keys": np.stack([x["peer_k1_2"], x["peer_k2_2"]], 1).reshape(2 * PEER_HEADS, KEYS, P).transpose(2, 0, 1),
        "peer_u": x["peer_u_2"].reshape(KEYS, KEYS, KD, P).transpose(1, 3, 2, 0),
        "peer_v": x["peer_v_2"].reshape(KEYS, KEYS, D).transpose(1, 0, 2),
    }


def kernel(**inputs):
    import concourse.bacc as bacc
    from concourse.bass_utils import run_bass_kernel_spmd

    nc = bacc.Bacc("TRN2", target_bir_lowering=False, num_devices=1)
    arrays = {n: np.ascontiguousarray(v) for n, v in laid_out({n: np.asarray(v) for n, v in inputs.items()}).items()}
    arrays.update({n: np.ascontiguousarray(v, dtype=np.float32) for n, v in shape_constants().items()})
    aps = {n: nc.dram_tensor(f"in_{n}", v.shape, mybir.dt.from_np(v.dtype), kind="ExternalInput").ap() for n, v in arrays.items()}
    out = nc.dram_tensor("out_rows", (1, SEQ, D), F32, kind="ExternalOutput").ap()
    build_program(nc, aps, out)
    result = run_bass_kernel_spmd(nc, [{f"in_{n}": v for n, v in arrays.items()}], core_ids=[0])
    return result.results[0]["out_rows"]
```

```python
import math
from contextlib import ExitStack, contextmanager

import numpy as np
import concourse.bass as bass
from concourse import mybir

F32 = mybir.dt.float32
F32R = mybir.dt.float32r
BF16 = mybir.dt.bfloat16
I32 = mybir.dt.int32
U32 = mybir.dt.uint32
ACT = mybir.ActivationFunctionType
ALU = mybir.AluOpType
AX = mybir.AxisListType.X

P = 128
SEQ = 512
TILES = SEQ // P
D = 1024
KD = D // P
BANK = 512
HALF = 256
SIDE = 192
EPS = 1e-6
LN_EPS = 1e-5
GN_EPS = 64e-5
HEADS = 16
FOX_DK = D // HEADS
DV = 64
Q_RANK, KV_RANK, NOPE, ROPE = 384, 256, 64, 32
QK = NOPE + ROPE
GROUPS, PER_GROUP, EXPERTS, D_EXPERT = 4, 4, 16, 256
NEG = -3.0e38
TWO_PI = 2.0 * math.pi


class Stage:

    before = None

    def __init__(self, nc, name):
        self.nc, self.name, self.ctx, self.sem_ctx, self.sems = nc, name, ExitStack(), ExitStack(), []

    def sb(self, name, shape, dtype=F32):
        return self.ctx.enter_context(self.nc.sbuf_tensor(f"{self.name}_{name}", list(shape), dtype))

    def ps(self, name, shape, dtype=F32):
        return self.ctx.enter_context(self.nc.psum_tensor(f"{self.name}_{name}", list(shape), dtype))

    def sem(self, name):
        self.sems.append(self.sem_ctx.enter_context(self.nc.semaphore(f"{self.name}_{name}")))
        return self.sems[-1]

    @contextmanager
    def block(self):
        with self.nc.Block() as block:
            if Stage.before is not None:
                @block.gpsimd
                def _(pool):
                    for sem in Stage.before.sems:
                        pool.sem_clear(sem)
            yield block

    def __enter__(self):
        return self

    def __exit__(self, *error):
        if Stage.before is not None:
            Stage.before.sem_ctx.close()
        Stage.before = self
        return self.ctx.__exit__(*error)

    @classmethod
    def finish(cls, nc):
        with cls(nc, "finish") as s:
            with s.block():
                pass
        cls.before = None


class Chain:

    def __init__(self, eng, sem):
        self.eng, self.sem, self.n = eng, sem, 0

    def __call__(self, *instructions):
        for ins in instructions:
            self.n = self.n + 1
            ins.then_inc(self.sem, 1)
        self.eng.wait_ge(self.sem, self.n)


def constants(nc, a, g):
    with Stage(nc, "const") as s:
        loaded = s.sem("loaded")
        with s.block() as block:
            @block.sync
            def _(sp):
                sp.dma_start(g.ident[:], a["ident"]).then_inc(loaded, 16)
                sp.dma_start(g.causal[:], a["causal"]).then_inc(loaded, 16)
                sp.dma_start(g.iota[:], a["iota"]).then_inc(loaded, 16)
                sp.dma_start(g.x[:], a["x"].rearrange("o (t p) d -> p (o t) d", p=P)).then_inc(loaded, 16)
                sp.wait_ge(loaded, 64)


def modulation(nc, g, name, c_dram, w_dram, b_dram):
    CH, SLOTS = 6 * D // BANK, 3
    with Stage(nc, name) as s:
        c_col, c_act = s.sb("c_col", [P, KD]), s.sb("c_act", [P, KD])
        c_rep = s.sb("c_rep", [P, KD, P])
        bias = s.sb("bias", [1, 6 * D])
        ones = s.sb("ones", [1, P])
        ring = s.sb("ring", [P, SLOTS, KD, BANK])
        acc = s.ps("acc", [P, SLOTS, BANK])
        small, acted, rep = s.sem("small"), s.sem("acted"), s.sem("rep")
        w_in = [s.sem(f"w_in{u}") for u in range(SLOTS)]
        summed, kept = s.sem("summed"), s.sem("kept")
        mod = g.mod[:].rearrange("p j d -> p (j d)")
        with s.block() as block:
            @block.sync
            def _(sp):
                sp.dma_start(c_col[:], c_dram).then_inc(small, 16)
                sp.dma_start(bias[:], b_dram).then_inc(small, 16)
                for u in range(SLOTS):
                    sp.dma_start(ring[:, u], w_dram[u]).then_inc(w_in[u], 16)
                with sp.Fori(0, CH // SLOTS - 1) as i:
                    for u in range(SLOTS):
                        sp.wait_ge(summed, SLOTS * i + u + 1)
                        sp.dma_start(ring[:, u], w_dram[bass.ds(SLOTS * i + u + SLOTS, 1)].rearrange(
                            "o p k n -> p (o k) n")).then_inc(w_in[u], 16)

            @block.scalar
            def _(act):
                act.wait_ge(small, 32)
                nc.scalar.activation(c_act[:], c_col[:], ACT.Silu).then_inc(acted, 1)
                act.sem_inc(kept, SLOTS)
                with act.Fori(0, CH // SLOTS) as i:
                    for u in range(SLOTS):
                        act.wait_ge(summed, SLOTS * i + u + 1)
                        nc.scalar.copy(mod[:, bass.ds((SLOTS * i + u) * BANK, BANK)], acc[:, u]).then_inc(kept, 1)

            @block.vector
            def _(dve):
                nc.vector.memset(ones[:], 1.0).then_inc(rep, 1)
                dve.wait_ge(acted, 1)
                nc.vector.tensor_copy(c_rep[:], c_act[:].unsqueeze(2).to_broadcast([P, KD, P])).then_inc(rep, 1)

            @block.tensor
            def _(pe):
                pe.wait_ge(rep, 2)
                pe.wait_ge(small, 32)
                with pe.Fori(0, CH // SLOTS) as i:
                    for u in range(SLOTS):
                        pe.wait_ge(w_in[u], 16 * i + 16)
                        pe.wait_ge(kept, SLOTS * i + u + 1)
                        for k in range(KD):
                            nc.tensor.matmul(acc[:, u], c_rep[:, k], ring[:, u, k], start=(k == 0), stop=False)
                        nc.tensor.matmul(acc[:, u], ones[:], bias[:, bass.ds((SLOTS * i + u) * BANK, BANK)],
                                         start=False, stop=True).then_inc(summed, 1)


def side_modulation(nc, g, name, sums_dram, b_dram):
    CH, BANKS = 6 * D // BANK, 4
    with Stage(nc, name) as s:
        sums = s.sb("sums", [P, 6 * D])
        ones, bias = s.sb("ones", [P, P]), s.sb("bias", [1, 6 * D])
        acc = s.ps("acc", [P, BANKS, BANK])
        loaded, ready, summed, kept = s.sem("loaded"), s.sem("ready"), s.sem("summed"), s.sem("kept")
        mod = g.mod[:].rearrange("p j d -> p (j d)")
        with s.block() as block:
            @block.sync
            def _(sp):
                sp.dma_start(bias[:], b_dram).then_inc(loaded, 16)
                sp.dma_start(sums[:].rearrange("p (c n) -> p c n", n=SIDE), sums_dram.rearrange("c p n -> p c n")).then_inc(loaded, 16)

            @block.vector
            def _(dve):
                nc.vector.memset(ones[:], 1.0).then_inc(ready, 1)
                dve.wait_ge(loaded, 32)
                for n in range(CH):
                    columns = slice(n * BANK, (n + 1) * BANK)
                    nc.vector.tensor_tensor(sums[0:1, columns], sums[0:1, columns], bias[:, columns], ALU.add).then_inc(ready, 1)

            @block.tensor
            def _(pe):
                for n in range(CH):
                    columns = slice(n * BANK, (n + 1) * BANK)
                    if n >= BANKS:
                        pe.wait_ge(kept, n - BANKS + 1)
                    pe.wait_ge(ready, n + 2)
                    nc.tensor.matmul(acc[:, n % BANKS], ones[:], sums[:, columns], start=True, stop=True).then_inc(summed, 1)

            @block.scalar
            def _(act):
                for n in range(CH):
                    act.wait_ge(summed, n + 1)
                    nc.scalar.copy(mod[:, n * BANK:(n + 1) * BANK], acc[:, n % BANKS]).then_inc(kept, 1)


def normed(nc, g, name, kind, scale_at, shift_at, gain=None):
    with Stage(nc, name) as s:
        h = s.sb("h", [P, 2, D])
        square = s.sb("square", [P, D])
        gain_row, factor = s.sb("gain_row", [P, D]), s.sb("factor", [P, D])
        stat = s.sb("stat", [P, TILES, 2, 6])
        ms, rstd, mean = s.sb("ms", [P, TILES, 2]), s.sb("rstd", [P, TILES]), s.sb("mean", [P, TILES])
        root = s.sb("root", [P, TILES])
        pt = s.ps("pt", [P, 2, KD, P])
        loaded, order, squared = s.sem("loaded"), s.sem("order"), s.sem("squared")
        scaled, turned, kept, shifted = s.sem("scaled"), s.sem("turned"), s.sem("kept"), s.sem("shifted")
        ready, rooted = s.sem("ready"), s.sem("rooted")
        with s.block() as block:
            @block.sync
            def _(sp):
                if gain is not None:
                    sp.dma_start(gain_row[:], gain).then_inc(loaded, 16)

            @block.scalar
            def _(act):
                if kind == "rms":
                    for t in range(TILES):
                        if t:
                            act.wait_ge(squared, t)
                        nc.scalar.activation(square[:], g.x[:, t], ACT.Square,
                                             accum_out=ms[:, t, 0:1]).then_inc(squared, 1)
                act.wait_ge(ready, 1)
                nc.scalar.activation(root[:], mean[:], ACT.Sqrt).then_inc(rooted, 1)
                for t in range(TILES):
                    act.wait_ge(turned, t + 1)
                    for half in range(2):
                        ks = slice(half * KD // 2, (half + 1) * KD // 2)
                        nc.scalar.copy(g.hT[:, ks, t * P:(t + 1) * P], pt[:, t % 2, ks]).then_inc(kept, 1)

            @block.vector
            def _(dve):
                then = Chain(dve, order)
                if gain is not None:
                    dve.wait_ge(loaded, 16)
                    then(nc.vector.scalar_tensor_tensor(factor[:], g.mod[:, scale_at], 1.0, gain_row[:], ALU.add, ALU.mult))
                else:
                    then(nc.vector.tensor_scalar(factor[:], g.mod[:, scale_at], 1.0, None, ALU.add))
                if kind == "rms":
                    dve.wait_ge(squared, TILES)
                    then(nc.vector.tensor_scalar(mean[:], ms[:, :, 0], 1.0 / D, EPS, ALU.mult, ALU.add))
                else:
                    for t in range(TILES):
                        for half in range(2):
                            then(nc.vector.bn_stats(stat[:, t, half], g.x[:, t, half * D // 2:(half + 1) * D // 2]))
                        then(nc.vector.bn_aggr(ms[:, t], stat[:, t]))
                    then(nc.vector.tensor_scalar(mean[:], ms[:, :, 1], LN_EPS, None, ALU.add))
                nc.vector.tensor_scalar(mean[:], mean[:], 0.0, None, ALU.max).then_inc(ready, 1)
                dve.wait_ge(rooted, 1)
                then(nc.vector.reciprocal(rstd[:], root[:]))
                for t in range(TILES):
                    if t >= 2:
                        dve.wait_ge(turned, t - 1)
                    if kind == "rms":
                        then(nc.vector.scalar_tensor_tensor(h[:, t % 2], g.x[:, t], rstd[:, t:t + 1], factor[:],
                                                            ALU.mult, ALU.mult))
                    else:
                        then(nc.vector.tensor_scalar(h[:, t % 2], g.x[:, t], ms[:, t, 0:1], rstd[:, t:t + 1],
                                                     ALU.subtract, ALU.mult))
                        then(nc.vector.tensor_tensor(h[:, t % 2], h[:, t % 2], factor[:], ALU.mult))
                    nc.vector.tensor_tensor(h[:, t % 2], h[:, t % 2], g.mod[:, shift_at], ALU.add).then_inc(shifted, 1)

            @block.tensor
            def _(pe):
                for t in range(TILES):
                    pe.wait_ge(shifted, t + 1)
                    if t >= 2:
                        pe.wait_ge(kept, 2 * (t - 1))
                    for k in range(KD):
                        last = nc.tensor.transpose(pt[:, t % 2, k], h[:, t % 2, k * P:(k + 1) * P], g.ident[:])
                    last.then_inc(turned, 1)


def passes(nc, out, lhs, rhs, start, stop):
    (l_hi, l_lo), (r_hi, r_lo) = lhs, rhs
    nc.tensor.matmul(out, l_hi, r_hi, start=start, stop=False)
    nc.tensor.matmul(out, l_hi, r_lo, start=False, stop=False)
    return nc.tensor.matmul(out, l_lo, r_hi, start=False, stop=stop)


def in_pairs(eng, chunks, body):
    if chunks > 2:
        with eng.Fori(0, chunks // 2 - 1) as i:
            for u in range(2):
                body(2 * i + u, u, i)
    for u in range(2):
        body(chunks - 2 + u, u, chunks // 2 - 1)


def project_rows(nc, name, lhs, kc, w_dram, chunks, width, keep=None, gate=None, x=None, alpha=1.0):
    assert chunks % 2 == 0
    with Stage(nc, name) as s:
        raw = s.sb("raw", [P, 2, kc, width])
        w_hi, w_lo = s.sb("w_hi", [P, 2, kc, width], F32R), s.sb("w_lo", [P, 2, kc, width], F32R)
        l_hi, l_lo = s.sb("l_hi", [P, kc, SEQ], F32R), s.sb("l_lo", [P, kc, SEQ], F32R)
        part = s.sb("part", [P, 2, width])
        acc = s.ps("acc", [P, 2, TILES, BANK])
        w_in = [s.sem(f"w_in{u}") for u in range(2)]
        l_rounded, l_split, w_rounded, w_split = (s.sem(x) for x in ("l_rounded", "l_split", "w_rounded", "w_split"))
        summed, kept, gated = s.sem("summed"), s.sem("kept"), s.sem("gated")

        def ahead(n):
            return not isinstance(n, int) or n + 2 < chunks

        with s.block() as block:
            @block.sync
            def _(sp):
                def load(n, u, i):
                    if ahead(n):
                        sp.wait_ge(w_split, n + 1)
                        sp.dma_start(raw[:, u], w_dram[bass.ds(n + 2, 1)].rearrange("o p k n -> p (o k) n")).then_inc(w_in[u], 16)

                for u in range(2):
                    sp.dma_start(raw[:, u], w_dram[u]).then_inc(w_in[u], 16)
                in_pairs(sp, chunks, load)

            @block.tensor
            def _(pe):
                def multiply(n, u, i):
                    pe.wait_ge(w_split, n + 1)
                    for t in range(TILES):
                        tokens = slice(t * P, (t + 1) * P)
                        pe.wait_ge(kept, TILES * n + t + 1)
                        for k in range(kc):
                            last = passes(nc, acc[:, u, t, :width], (l_hi[:, k, tokens], l_lo[:, k, tokens]),
                                          (w_hi[:, u, k], w_lo[:, u, k]), k == 0, k == kc - 1)
                        last.then_inc(summed, 1)

                pe.wait_ge(l_split, kc)
                in_pairs(pe, chunks, multiply)

            @block.scalar
            def _(act):
                def round_(u, loads):
                    act.wait_ge(w_in[u], 16 * loads)
                    nc.scalar.copy(w_hi[:, u], raw[:, u]).then_inc(w_rounded, 1)

                def step(n, u, i):
                    for t in range(TILES):
                        if keep is not None:
                            act.wait_ge(summed, TILES * n + t + 1)
                            columns = slice(n * width, (n + 1) * width) if isinstance(n, int) else bass.ds(n * width, width)
                            nc.scalar.copy(keep[:, t, columns], acc[:, u, t, :width]).then_inc(kept, 1)
                    if ahead(n):
                        act.wait_ge(summed, TILES * n + TILES)
                        round_(u, i + 2)

                for k in range(kc):
                    nc.scalar.copy(l_hi[:, k], lhs[:, k]).then_inc(l_rounded, 1)
                if keep is not None:
                    act.sem_inc(kept, 2 * TILES)
                for u in range(2):
                    round_(u, 1)
                in_pairs(act, chunks, step)

            @block.vector
            def _(dve):
                def cut(n, u):
                    dve.wait_ge(w_rounded, n + 1)
                    nc.vector.tensor_tensor(w_lo[:, u], raw[:, u], w_hi[:, u].bitcast(F32), ALU.subtract).then_inc(w_split, 1)

                def step(n, u, i):
                    for t in range(TILES):
                        if keep is None:
                            m = TILES * n + t
                            columns = slice(n * width, (n + 1) * width) if isinstance(n, int) else bass.ds(n * width, width)
                            dve.wait_ge(summed, m + 1)
                            nc.vector.tensor_tensor(part[:, t % 2], acc[:, u, t, :width], gate[:, columns],
                                                    ALU.mult).then_inc(kept, 1)
                            dve.wait_ge(kept, 2 * TILES + m + 1)
                            nc.vector.scalar_tensor_tensor(x[:, t, columns], x[:, t, columns], alpha, part[:, t % 2],
                                                           ALU.mult, ALU.add).then_inc(gated, 1)
                    if ahead(n):
                        cut(n + 2, u)

                for k in range(kc):
                    dve.wait_ge(l_rounded, k + 1)
                    nc.vector.tensor_tensor(l_lo[:, k], lhs[:, k], l_hi[:, k].bitcast(F32), ALU.subtract).then_inc(l_split, 1)
                if keep is None:
                    dve.sem_inc(kept, 2 * TILES)
                for u in range(2):
                    cut(u, u)
                in_pairs(dve, chunks, step)


def turn_rows(nc, g, name, rows, chunks, turned):
    with Stage(nc, name) as s:
        pt = s.ps("pt", [P, 4, TILES, P])
        done, kept = s.sem("done"), s.sem("kept")
        with s.block() as block:
            @block.tensor
            def _(pe):
                for c in range(chunks):
                    if c >= 4:
                        pe.wait_ge(kept, c - 3)
                    for t in range(TILES):
                        last = nc.tensor.transpose(pt[:, c % 4, t], rows[:, t, c * P:(c + 1) * P], g.ident[:])
                    last.then_inc(done, 1)

            @block.scalar
            def _(act):
                for c in range(chunks):
                    act.wait_ge(done, c + 1)
                    nc.scalar.copy(turned[:, c], pt[:, c % 4].rearrange("p t n -> p (t n)")).then_inc(kept, 1)
def head_norms(nc, name, jobs, dk, heads=HEADS):
    with Stage(nc, name) as s:
        n = len(jobs) * TILES
        square = s.sb("square", [P, 2, heads, dk])
        total, root, inv = (s.sb(x, [P, n, heads]) for x in ("total", "root", "inv"))
        gains = [s.sb(f"gain{j}", [P, dk]) for j in range(len(jobs))]
        loaded, squared, summed, rooted = s.sem("loaded"), s.sem("squared"), s.sem("summed"), s.sem("rooted")
        order, halfway, normed_ = s.sem("order"), s.sem("halfway"), s.sem("normed")

        def tile(m):
            rows, _, _ = jobs[m // TILES]
            return rows[:, m % TILES].rearrange("p (h d) -> p h d", d=dk)

        with s.block() as block:
            @block.sync
            def _(sp):
                for j, (_, gain, _) in enumerate(jobs):
                    sp.dma_start(gains[j][:], gain).then_inc(loaded, 16)

            @block.scalar
            def _(act):
                for m in range(n):
                    if m >= 2:
                        act.wait_ge(summed, m - 1)
                    nc.scalar.activation(square[:, m % 2], tile(m), ACT.Square).then_inc(squared, 1)
                act.wait_ge(order, 1)
                nc.scalar.activation(root[:], total[:], ACT.Sqrt).then_inc(rooted, 1)

            @block.vector
            def _(dve):
                for m in range(n):
                    dve.wait_ge(squared, m + 1)
                    nc.vector.tensor_reduce(total[:, m], square[:, m % 2], AX, ALU.add).then_inc(summed, 1)
                dve.wait_ge(summed, n)
                then = Chain(dve, order)
                then(nc.vector.tensor_scalar(total[:], total[:], 1.0 / dk, EPS, ALU.mult, ALU.add))
                dve.wait_ge(rooted, 1)
                then(nc.vector.reciprocal(inv[:], root[:]))
                for j, (_, _, scale) in enumerate(jobs):
                    if scale != 1.0:
                        part = inv[:, j * TILES:(j + 1) * TILES]
                        then(nc.vector.tensor_scalar(part, part, scale, None, ALU.mult))
                dve.wait_ge(loaded, 16 * len(jobs))
                for m in range(n):
                    nc.vector.tensor_tensor(tile(m), tile(m), inv[:, m].unsqueeze(2).to_broadcast([P, heads, dk]),
                                            ALU.mult).then_inc(halfway, 1)
                    dve.wait_ge(halfway, m + 1)
                    nc.vector.tensor_tensor(tile(m), tile(m), gains[m // TILES][:].unsqueeze(1).to_broadcast([P, heads, dk]),
                                            ALU.mult).then_inc(normed_, 1)


def forget_gates(nc, g, name, w_dram, b_dram, scratch, cum_q, cum_k):
    with Stage(nc, name) as s:
        w, b = s.sb("w", [P, KD, HEADS]), s.sb("b", [HEADS, 1])
        z, low, ones = (s.sb(x, [HEADS, SEQ]) for x in ("z", "low", "ones"))
        size, small, soft = (s.sb(x, [HEADS, SEQ]) for x in ("size", "small", "soft"))
        logs, cum = s.sb("logs", [HEADS, SEQ]), s.sb("cum", [HEADS, SEQ])
        logits, turned = s.ps("logits", [HEADS, SEQ]), s.ps("turned", [P, TILES, HEADS])
        loaded, summed, order, steps = s.sem("loaded"), s.sem("summed"), s.sem("order"), s.sem("steps")
        stored, spread, turn = s.sem("stored"), s.sem("spread"), s.sem("turn")
        with s.block() as block:
            @block.sync
            def _(sp):
                sp.dma_start(w[:], w_dram).then_inc(loaded, 16)
                sp.dma_start(b[:], b_dram).then_inc(loaded, 16)
                sp.wait_ge(order, 6)
                sp.dma_start(scratch, cum[:]).then_inc(stored, 16)
                sp.wait_ge(stored, 16)
                sp.dma_start(cum_k[:], scratch.partition_broadcast(P)).then_inc(spread, 16)
                sp.wait_ge(spread, 16)

            @block.tensor
            def _(pe):
                pe.wait_ge(loaded, 32)
                for k in range(KD):
                    last = nc.tensor.matmul(logits[:], w[:, k], g.hT[:, k], start=(k == 0), stop=(k == KD - 1))
                last.then_inc(summed, 1)
                pe.wait_ge(order, 6)
                for t in range(TILES):
                    last = nc.tensor.transpose(turned[:, t], cum[:, t * P:(t + 1) * P], g.ident[:HEADS, :HEADS])
                last.then_inc(turn, 1)

            @block.scalar
            def _(act):
                then = Chain(act, steps)
                act.wait_ge(order, 2)
                then(nc.scalar.activation(size[:], z[:], ACT.Abs))
                then(nc.scalar.activation(small[:], size[:], ACT.Exp, scale=-1.0))
                then(nc.scalar.activation(soft[:], small[:], ACT.Ln, bias=1.0))

            @block.vector
            def _(dve):
                then = Chain(dve, order)
                then(nc.vector.memset(ones[:], 1.0))
                dve.wait_ge(loaded, 32)
                dve.wait_ge(summed, 1)
                then(nc.vector.tensor_scalar(z[:], logits[:], b[:], None, ALU.add))
                then(nc.vector.tensor_scalar(low[:], z[:], 0.0, None, ALU.min))
                dve.wait_ge(steps, 3)
                then(nc.vector.tensor_tensor(logs[:], low[:], soft[:], ALU.subtract))
                then(nc.vector.tensor_scalar(z[:], ones[:], 0.0, None, ALU.mult))
                then(nc.vector.tensor_tensor_scan(cum[:], ones[:], logs[:], 0.0, ALU.mult, ALU.add))
                dve.wait_ge(turn, 1)
                then(nc.vector.tensor_copy(cum_q[:], turned[:]))


def attention(nc, g, name, q, k, v, o, dk, v_step=DV, v_at=0, cum_q=None, cum_k=None):
    STEPS, LOOP = TILES * HEADS, 2 * TILES
    LOOPS = STEPS // LOOP
    AHEAD = 2
    with Stage(nc, name) as s:
        qs, ks = s.sb("qs", [P, TILES, dk]), s.sb("ks", [P, TILES, dk])
        qT, kT = s.sb("qT", [dk, 2, SEQ]), s.sb("kT", [dk, 2, SEQ])
        z, p = s.sb("z", [P, 2, SEQ]), s.sb("p", [P, 2, SEQ])
        pT = s.sb("pT", [P, 2, TILES, P])
        low, total, inv = s.sb("low", [P, 2]), s.sb("total", [P, TILES]), s.sb("inv", [P, 2])
        tq, tk = s.ps("tq", [dk, SEQ]), s.ps("tk", [dk, SEQ])
        scores, tp = s.ps("scores", [P, 2, SEQ]), s.ps("tp", [P, 2, TILES, P])
        out = s.ps("out", [P, 2, BANK])
        copied, turned, kept = s.sem("copied"), s.sem("turned"), s.sem("kept")
        scored, biased, masked, maxed = s.sem("scored"), s.sem("biased"), s.sem("masked"), s.sem("maxed")
        raised, p_turned, p_kept = s.sem("raised"), s.sem("p_turned"), s.sem("p_kept")
        started = s.sem("started")
        mixed, inverted, done = s.sem("mixed"), s.sem("inverted"), s.sem("done")

        def part(start, size):
            return slice(start, start + size) if isinstance(start, int) else bass.ds(start, size)

        def step(k, r):
            return LOOP * k + r, 2 * k + r // TILES, r // TILES % 2, r % TILES

        def slots(eng, slot):
            with eng.Fori(0, LOOPS - 1) as k:
                for r in range(1, LOOP + 1):
                    slot(k, r)
            for r in range(1, LOOP):
                slot(LOOPS - 1, r)

        def exists(k, r):
            return not isinstance(k, int) or LOOP * k + r < STEPS

        with s.block() as block:
            @block.gpsimd
            def _(pool):
                with pool.Fori(0, HEADS) as h:
                    pool.wait_ge(turned, h + 1)
                    nc.gpsimd.tensor_copy(qs[:], q[:, :, bass.ds(h * dk, dk)]).then_inc(copied, 1)
                    nc.gpsimd.tensor_copy(ks[:], k[:, :, bass.ds(h * dk, dk)]).then_inc(copied, 1)

            @block.tensor
            def _(pe):
                def turn_head(h):
                    pe.wait_ge(copied, 2 * h + 2)
                    pe.wait_ge(kept, 2 * h + 2)
                    pe.sem_inc(started, 1)
                    for src, dst in ((qs, tq), (ks, tk)):
                        for t in range(TILES):
                            last = nc.tensor.transpose(dst[:, t * P:(t + 1) * P], src[:, t], g.ident[:])
                    last.then_inc(turned, 1)

                def score(k, r):
                    n, h, u, i = step(k, r)
                    width = (i + 1) * P
                    pe.wait_ge(kept, 2 * h + 4)
                    pe.wait_ge(biased, n + 1)
                    nc.tensor.matmul(scores[:, i % 2, :width], qT[:, u, i * P:(i + 1) * P], kT[:, u, :width],
                                     start=True, stop=True).then_inc(scored, 1)

                def turn(k, r):
                    n, h, u, i = step(k, r)
                    pe.wait_ge(raised, n + 1 + AHEAD)
                    pe.wait_ge(p_kept, n + 1)
                    for j in range(i + 1):
                        last = nc.tensor.transpose(tp[:, i % 2, j], p[:, i % 2, j * P:(j + 1) * P], g.ident[:])
                    last.then_inc(p_turned, 1)

                def mix(k, r):
                    n, h, u, i = step(k, r)
                    pe.wait_ge(p_kept, n + 1 + AHEAD)
                    pe.wait_ge(done, n + 1 + TILES - AHEAD)
                    for j in range(i + 1):
                        last = nc.tensor.matmul(out[:, i % 2, :DV], pT[:, i % 2, j], v[:, j, part(h * v_step + v_at, DV)],
                                                start=(j == 0), stop=(j == i))
                    last.then_inc(mixed, 1)

                def slot(k, r):
                    if exists(k, r + 2):
                        score(k, r + 2)
                    turn(k, r)
                    mix(k, r - 1)
                    if r % TILES == 0 and exists(k, r + TILES):
                        turn_head(2 * k + r // TILES + 1)

                pe.sem_inc(turned, 1)
                pe.sem_inc(scored, 2 * TILES)
                pe.sem_inc(p_turned, AHEAD)
                pe.sem_inc(mixed, AHEAD)
                turn_head(0)
                for r in range(3):
                    score(0, r)
                turn(0, 0)
                turn_head(1)
                slots(pe, slot)
                mix(LOOPS - 1, LOOP - 1)

            @block.scalar
            def _(act):
                def keep_head(h, u):
                    act.wait_ge(turned, h + 2)
                    act.wait_ge(scored, TILES * h + TILES)
                    nc.scalar.copy(qT[:, u], tq[:]).then_inc(kept, 1)
                    nc.scalar.copy(kT[:, u], tk[:]).then_inc(kept, 1)

                def raise_(k, r):
                    n, h, u, i = step(k, r)
                    width = (i + 1) * P
                    act.wait_ge(maxed, n + 1)
                    act.wait_ge(p_turned, n + 1)
                    act.wait_ge(done, n + 1)
                    nc.scalar.activation(p[:, i % 2, :width], z[:, i % 2, :width], ACT.Exp, bias=low[:, i % 2:i % 2 + 1],
                                         accum_out=total[:, i:i + 1]).then_inc(raised, 1)

                def keep(k, r):
                    n, h, u, i = step(k, r)
                    act.wait_ge(p_turned, n + 1 + AHEAD)
                    act.wait_ge(mixed, n + 1)
                    nc.scalar.copy(pT[:, i % 2, :i + 1], tp[:, i % 2, :i + 1]).then_inc(p_kept, 1)

                def slot(k, r):
                    if exists(k, r + 1):
                        raise_(k, r + 1)
                    keep(k, r)
                    if r % TILES == 0 and exists(k, r + TILES):
                        keep_head(2 * k + r // TILES + 1, (r // TILES + 1) % 2)

                act.sem_inc(kept, 2)
                act.sem_inc(raised, AHEAD)
                act.sem_inc(p_kept, AHEAD)
                keep_head(0, 0)
                raise_(0, 0)
                raise_(0, 1)
                keep(0, 0)
                keep_head(1, 1)
                slots(act, slot)

            @block.vector
            def _(dve):
                def bias(k, r):
                    n, h, u, i = step(k, r)
                    width = (i + 1) * P
                    dve.wait_ge(scored, n + 1 + 2 * TILES)
                    dve.wait_ge(raised, n + 1)
                    if cum_q is None:
                        nc.vector.tensor_copy(z[:, i % 2, :width], scores[:, i % 2, :width]).then_inc(biased, 1)
                    else:
                        nc.vector.scalar_tensor_tensor(
                            z[:, i % 2, :width], scores[:, i % 2, :width], cum_q[:, i, part(h, 1)],
                            cum_k[:, part(h, 1), :width].rearrange("p o t -> p (o t)"),
                            ALU.add, ALU.subtract).then_inc(biased, 1)
                    dve.wait_ge(biased, n + 1 + AHEAD)
                    diagonal = z[:, i % 2, i * P:width]
                    nc.vector.tensor_tensor(diagonal, diagonal, g.causal[:], ALU.add).then_inc(masked, 1)
                    dve.wait_ge(masked, n + 1)
                    nc.vector.tensor_reduce(low[:, i % 2:i % 2 + 1], z[:, i % 2, :width], AX, ALU.max,
                                            negate=True).then_inc(maxed, 1)

                def divide(k, r):
                    n, h, u, i = step(k, r)
                    dve.wait_ge(mixed, n + 1 + AHEAD)
                    nc.vector.reciprocal(inv[:, i % 2:i % 2 + 1], total[:, i:i + 1]).then_inc(inverted, 1)
                    dve.wait_ge(inverted, n + 1)
                    nc.vector.tensor_scalar(o[:, i, part(h * DV, DV)], out[:, i % 2, :DV], inv[:, i % 2:i % 2 + 1],
                                            None, ALU.mult).then_inc(done, 1)

                def slot(k, r):
                    if exists(k, r + 2):
                        bias(k, r + 2)
                    divide(k, r - 1)

                dve.sem_inc(biased, AHEAD)
                dve.sem_inc(done, TILES)
                for r in range(3):
                    bias(0, r)
                slots(dve, slot)
                divide(LOOPS - 1, LOOP - 1)
def route(nc, g, name, w_dram, b_dram):
    N = GROUPS + EXPERTS
    with Stage(nc, name) as s:
        w, b = s.sb("w", [P, KD, N]), s.sb("b", [P, N])
        by_group, by_expert = s.sb("by_group", [P, TILES, 8]), s.sb("by_expert", [P, TILES, EXPERTS])
        best, best_at = s.sb("best", [P, TILES, 8]), s.sb("best_at", [P, TILES, 8], U32)
        group, is_group = s.sb("group", [P, TILES, 1]), s.sb("is_group", [P, TILES, GROUPS])
        lowered, raised = s.sb("lowered", [P, TILES, GROUPS]), s.sb("raised", [P, TILES, GROUPS])
        total, top = s.sb("total", [P, TILES, 1]), s.sb("top", [P, TILES, 1])
        chosen = s.sb("chosen", [P, TILES, GROUPS, PER_GROUP])
        inside = s.sb("inside", [P, TILES, 8])
        pair, pair_at = s.sb("pair", [P, TILES, 8]), s.sb("pair_at", [P, TILES, 8], U32)
        ids, weights = s.sb("ids", [P, TILES, 2]), s.sb("weights", [P, TILES, 2])
        gap, ratio = s.sb("gap", [P, TILES, 1]), s.sb("ratio", [P, TILES, 1])
        first, second = s.sb("first", [P, TILES, EXPERTS]), s.sb("second", [P, TILES, EXPERTS])
        logits = s.ps("logits", [P, TILES, N])
        loaded, summed, order = s.sem("loaded"), s.sem("summed"), s.sem("order")
        low_ready, raised_ready = s.sem("low_ready"), s.sem("raised_ready")
        iota = lambda n: g.iota[:, :n].unsqueeze(1).to_broadcast([P, TILES, n])
        with s.block() as block:
            @block.sync
            def _(sp):
                sp.dma_start(w[:], w_dram).then_inc(loaded, 16)
                sp.dma_start(b[:], b_dram).then_inc(loaded, 16)

            @block.tensor
            def _(pe):
                pe.wait_ge(loaded, 32)
                for t in range(TILES):
                    for k in range(KD):
                        last = nc.tensor.matmul(logits[:, t], g.hT[:, k, t * P:(t + 1) * P], w[:, k],
                                                start=(k == 0), stop=(k == KD - 1))
                last.then_inc(summed, 1)

            @block.scalar
            def _(act):
                act.wait_ge(low_ready, 1)
                nc.scalar.activation(raised[:], lowered[:], ACT.Exp).then_inc(raised_ready, 1)
                act.wait_ge(low_ready, 2)
                nc.scalar.activation(ratio[:], gap[:], ACT.Exp).then_inc(raised_ready, 1)

            @block.vector
            def _(dve):
                then = Chain(dve, order)
                v = nc.vector
                then(v.memset(by_group[:], NEG))
                then(v.memset(inside[:], NEG))
                dve.wait_ge(loaded, 32)
                dve.wait_ge(summed, 1)
                then(v.tensor_tensor(by_group[:, :, :GROUPS], logits[:, :, :GROUPS],
                                     b[:, :GROUPS].unsqueeze(1).to_broadcast([P, TILES, GROUPS]), ALU.add))
                then(v.tensor_tensor(by_expert[:], logits[:, :, GROUPS:],
                                     b[:, GROUPS:].unsqueeze(1).to_broadcast([P, TILES, EXPERTS]), ALU.add))
                for t in range(TILES):
                    then(v.max(best[:, t], by_group[:, t]))
                    then(v.max_index(best_at[:, t], best[:, t], by_group[:, t]))
                then(v.tensor_copy(group[:], best_at[:, :, 0:1]))
                v.tensor_tensor(lowered[:], by_group[:, :, :GROUPS], best[:, :, 0:1].to_broadcast([P, TILES, GROUPS]),
                                ALU.subtract).then_inc(low_ready, 1)
                then(v.tensor_tensor(is_group[:], iota(GROUPS), group[:].to_broadcast([P, TILES, GROUPS]), ALU.is_equal))
                for t in range(TILES):
                    then(v.tensor_tensor(chosen[:, t], by_expert[:, t].rearrange("p (a e) -> p a e", a=GROUPS),
                                         is_group[:, t].unsqueeze(2).to_broadcast([P, GROUPS, PER_GROUP]), ALU.mult))
                    then(v.tensor_reduce(inside[:, t, :PER_GROUP], chosen[:, t].rearrange("p a e -> p e a"), AX, ALU.add))
                    then(v.max(pair[:, t], inside[:, t]))
                    then(v.max_index(pair_at[:, t], pair[:, t], inside[:, t]))
                v.tensor_tensor(gap[:], pair[:, :, 1:2], pair[:, :, 0:1], ALU.subtract).then_inc(low_ready, 1)
                then(v.tensor_copy(ids[:], pair_at[:, :, 0:2]))
                then(v.scalar_tensor_tensor(ids[:], group[:].to_broadcast([P, TILES, 2]), float(PER_GROUP), ids[:],
                                            ALU.mult, ALU.add))
                dve.wait_ge(raised_ready, 2)
                then(v.tensor_reduce(total[:], raised[:], AX, ALU.add))
                then(v.reciprocal(top[:], total[:]))
                then(v.tensor_scalar(total[:], ratio[:], 1.0, None, ALU.add))
                then(v.reciprocal(gap[:], total[:]))
                then(v.tensor_tensor(weights[:, :, 0:1], gap[:], top[:], ALU.mult))
                then(v.tensor_tensor(weights[:, :, 1:2], weights[:, :, 0:1], ratio[:], ALU.mult))
                for j, part in enumerate((first, second)):
                    then(v.tensor_tensor(part[:], iota(EXPERTS), ids[:, :, j:j + 1].to_broadcast([P, TILES, EXPERTS]), ALU.is_equal))
                    then(v.tensor_tensor(part[:], part[:], weights[:, :, j:j + 1].to_broadcast([P, TILES, EXPERTS]), ALU.mult))
                then(v.tensor_tensor(g.comb[:], first[:], second[:], ALU.add))


def split_rows(nc, g, name, hi, lo):
    with Stage(nc, name) as s:
        rounded, left = s.sem("rounded"), s.sem("left")
        with s.block() as block:
            @block.scalar
            def _(act):
                for k in range(KD):
                    nc.scalar.copy(hi[:, k], g.hT[:, k]).then_inc(rounded, 1)

            @block.vector
            def _(dve):
                for k in range(KD):
                    dve.wait_ge(rounded, k + 1)
                    nc.vector.tensor_tensor(lo[:, k], g.hT[:, k], hi[:, k].bitcast(F32), ALU.subtract).then_inc(left, 1)


def landing(g, rising, extra=None):
    places = [g.hT[:, 2 * m:2 * m + 2].rearrange("p a (b n) -> p (a b) n", n=P) for m in range(4)]
    if extra is not None:
        places = places + [extra[:, m] for m in range(2)]
    up = [[places[(rising + 1) * u + j] for j in range(rising)] for u in range(2)]
    return up, [places[(rising + 1) * u + rising].rearrange("p k n -> p (k n)") for u in range(2)]


def expert_chunks(nc, g, name, rising, lowering, first, chunks, h_hi, h_lo, bend, factor, share, acc, side=None, landed=False):
    HALVES, BANKS = D // BANK, 4
    OUTS, J = TILES * HALVES, len(rising)
    with Stage(nc, name) as s:
        raw_up, raw_down = landing(g, J, s.sb("extra", [P, 2, KD, P]) if J == 2 else None)
        up_hi, up_lo = s.sb("up_hi", [P, 2, J, KD, P], F32R), s.sb("up_lo", [P, 2, J, KD, P], F32R)
        down_hi, down_lo = s.sb("down_hi", [P, 2, D], F32R), s.sb("down_lo", [P, 2, D], F32R)
        bent = s.sb("bent", [P, 2, SEQ])
        bent_hi, bent_lo = s.sb("bent_hi", [P, 2, SEQ], F32R), s.sb("bent_lo", [P, 2, SEQ], F32R)
        risen, low = s.ps("risen", [P, 2, J, SEQ]), s.ps("low", [P, BANKS, BANK])
        up_in, down_in = [s.sem(f"up_in{u}") for u in range(2)], [s.sem(f"down_in{u}") for u in range(2)]
        up_rounded, up_split = s.sem("up_rounded"), s.sem("up_split")
        down_rounded, down_split = s.sem("down_rounded"), s.sem("down_split")
        lifted, bent_done, made = s.sem("lifted"), s.sem("bent_done"), s.sem("made")
        rounded, split = s.sem("rounded"), s.sem("split")
        lowered, added = s.sem("lowered"), s.sem("added")
        if side is not None:
            side_w, side_sum = s.sb("side_w", [P, 2, KD, SIDE]), s.sb("side_sum", [P, 2, SIDE])
            side_in, side_out = [s.sem(f"side_in{u}") for u in range(2)], [s.sem(f"side_out{u}") for u in range(2)]
            side_made, side_summed = s.sem("side_made"), s.sem("side_summed")

        def pairs(eng, body):
            with eng.Fori(0, chunks // 2 - 1) as i:
                for u in range(2):
                    body(2 * i + u, u, i)

        last, before = chunks - 1, chunks - 2
        with s.block() as block:
            def chunk(dram, n):
                return dram[first + n:first + n + 1] if isinstance(n, int) else dram[bass.ds(first + n, 1)]

            @block.sync
            def _(sp):
                def load_up(n, u):
                    for j in range(J):
                        sp.dma_start(raw_up[u][j], chunk(rising[j], n).rearrange("o p k n -> p (o k) n")).then_inc(up_in[u], 16)

                def load_down(n, u):
                    sp.dma_start(raw_down[u], chunk(lowering, n).rearrange("o p d -> p (o d)")).then_inc(down_in[u], 16)

                def load_side(n, u):
                    w = side.w[n] if isinstance(n, int) else side.w[bass.ds(n, 1)].rearrange("o p k n -> p (o k) n")
                    sp.dma_start(side_w[:, u], w).then_inc(side_in[u], 16)

                def store_side(n, u):
                    sp.wait_ge(side_summed, n + 1)
                    to = side.sums[n] if isinstance(n, int) else side.sums[bass.ds(n, 1)].rearrange("o p n -> p (o n)")
                    sp.dma_start(to, side_sum[:, u]).then_inc(side_out[u], 16)

                def load_next(n, u):
                    sp.wait_ge(up_split, n + 1)
                    load_up(n + 2, u)
                    sp.wait_ge(down_split, n + 1)
                    load_down(n + 2, u)

                def next_side(n, u):
                    if side is not None:
                        store_side(n, u)
                        load_side(n + 2, u)

                for u in range(2):
                    if landed:
                        sp.sem_inc(up_in[u], 16 * J)
                        sp.sem_inc(down_in[u], 16)
                    else:
                        load_up(u, u)
                        load_down(u, u)
                    if side is not None:
                        load_side(u, u)
                load_next(0, 0)
                with sp.Fori(0, chunks // 2 - 2) as i:
                    load_next(2 * i + 1, 1)
                    next_side(2 * i, 0)
                    load_next(2 * i + 2, 0)
                    next_side(2 * i + 1, 1)
                load_next(chunks - 3, 1)
                next_side(chunks - 4, 0)
                next_side(chunks - 3, 1)
                if side is not None:
                    store_side(before, 0)
                    store_side(last, 1)
                    for u in range(2):
                        sp.wait_ge(side_out[u], 16 * (chunks // 2) + 16)

            @block.tensor
            def _(pe):
                def lift(n, u):
                    pe.wait_ge(up_split, n + 1)
                    pe.wait_ge(made, n + 1)
                    for j in range(J):
                        for k in range(KD):
                            done = passes(nc, risen[:, u, j], (up_hi[:, u, j, k], up_lo[:, u, j, k]), (h_hi[:, k], h_lo[:, k]),
                                          k == 0, k == KD - 1)
                    done.then_inc(lifted, 1)

                def lower(n, u):
                    pe.wait_ge(down_split, n + 1)
                    pe.wait_ge(split, n + 3)
                    for m in range(OUTS):
                        t, half = m // HALVES, m % HALVES
                        tokens, columns = slice(t * P, (t + 1) * P), slice(half * BANK, (half + 1) * BANK)
                        pe.wait_ge(added, OUTS * n + m + 1)
                        passes(nc, low[:, m % BANKS], (bent_hi[:, u, tokens], bent_lo[:, u, tokens]),
                               (down_hi[:, u, columns], down_lo[:, u, columns]), True, True).then_inc(lowered, 1)

                pe.sem_inc(lifted, 2)
                pe.sem_inc(lowered, 2 * OUTS)
                lift(0, 0)

                def step(n, u, i):
                    lift(n + 1, 1 - u)
                    lower(n, u)

                pairs(pe, step)
                lift(last, 1)
                lower(before, 0)
                lower(last, 1)

            @block.scalar
            def _(act):
                def round_up(n, u, loads):
                    act.wait_ge(up_in[u], 16 * J * loads)
                    act.wait_ge(lifted, n + 1)
                    for j in range(J):
                        nc.scalar.copy(up_hi[:, u, j], raw_up[u][j]).then_inc(up_rounded, 1)

                def round_down(n, u, loads):
                    act.wait_ge(down_in[u], 16 * loads)
                    act.wait_ge(lowered, OUTS * n + OUTS)
                    nc.scalar.copy(down_hi[:, u], raw_down[u]).then_inc(down_rounded, 1)

                def bend_chunk(n, u):
                    act.wait_ge(lifted, n + 3)
                    act.wait_ge(split, n + 1)
                    nc.scalar.activation(bent[:, u], risen[:, u, 0], bend).then_inc(bent_done, 1)
                    act.wait_ge(made, n + 3)
                    act.wait_ge(lowered, OUTS * n + OUTS)
                    nc.scalar.copy(bent_hi[:, u], bent[:, u]).then_inc(rounded, 1)

                round_up(0, 0, 1)
                round_up(1, 1, 1)
                round_down(0, 0, 1)
                bend_chunk(0, 0)

                def step(n, u, i):
                    round_up(n + 2, u, i + 2)
                    round_down(n + 1, 1 - u, i + 1 + u)
                    bend_chunk(n + 1, 1 - u)

                pairs(act, step)
                round_down(last, 1, chunks // 2)
                bend_chunk(last, 1)

            @block.gpsimd
            def _(pool):
                def split_up(n, u):
                    for j in range(J):
                        pool.wait_ge(up_rounded, J * n + j + 1)
                        done = nc.gpsimd.tensor_tensor(up_lo[:, u, j], raw_up[u][j], up_hi[:, u, j].bitcast(F32), ALU.subtract)
                    done.then_inc(up_split, 1)

                def split_down(n, u):
                    pool.wait_ge(down_rounded, n + 1)
                    nc.gpsimd.tensor_tensor(down_lo[:, u], raw_down[u], down_hi[:, u].bitcast(F32), ALU.subtract).then_inc(down_split, 1)

                def side_product(n, u, loads):
                    if side is not None:
                        pool.wait_ge(side_in[u], 16 * loads)
                        nc.gpsimd.tensor_tensor(side_w[:, u], side_w[:, u], side.c[:].unsqueeze(2).to_broadcast([P, KD, SIDE]),
                                                ALU.mult).then_inc(side_made, 1)

                split_up(0, 0)
                split_up(1, 1)
                split_down(0, 0)

                def step(n, u, i):
                    side_product(n, u, i + 1)
                    split_up(n + 2, u)
                    split_down(n + 1, 1 - u)

                pairs(pool, step)
                side_product(before, 0, chunks // 2)
                split_down(last, 1)
                side_product(last, 1, chunks // 2)

            @block.vector
            def _(dve):
                def make(n, u):
                    dve.wait_ge(bent_done, n + 1)
                    by = risen[:, u, 1] if J == 2 else factor(n)
                    nc.vector.tensor_tensor(bent[:, u], bent[:, u], by, ALU.mult).then_inc(made, 1)

                def cut(n, u):
                    dve.wait_ge(rounded, n + 1)
                    nc.vector.tensor_tensor(bent_lo[:, u], bent[:, u], bent_hi[:, u].bitcast(F32), ALU.subtract).then_inc(split, 1)

                def add(n, i, outs):
                    if outs[0] == 0:
                        dve.wait_ge(added, OUTS * n + BANKS)
                    for m in outs:
                        t, half = m // HALVES, m % HALVES
                        dve.wait_ge(lowered, OUTS * n + m + 1 + 2 * OUTS)
                        if share is None:
                            done = nc.vector.tensor_tensor(acc[:, t, half], low[:, m % BANKS], acc[:, t, half], ALU.add)
                        else:
                            done = nc.vector.scalar_tensor_tensor(acc[:, t, half], low[:, m % BANKS], share(t, i), acc[:, t, half],
                                                                  ALU.mult, ALU.add)
                        done.then_inc(added, 1)

                def side_reduce(n, u, i):
                    if side is not None:
                        dve.wait_ge(side_made, n + 1)
                        dve.wait_ge(side_out[u], 16 * i + 16)
                        nc.vector.tensor_reduce(side_sum[:, u], side_w[:, u].rearrange("p k n -> p n k"), AX, ALU.add).then_inc(
                            side_summed, 1)

                early, late = range(BANKS), range(BANKS, OUTS)
                dve.sem_inc(made, 2)
                dve.sem_inc(split, 2)
                dve.sem_inc(added, BANKS)
                if side is not None:
                    for u in range(2):
                        dve.sem_inc(side_out[u], 16)
                make(0, 0)
                cut(0, 0)

                def step(n, u, i):
                    make(n + 1, 1 - u)
                    add(n, i, early)
                    cut(n + 1, 1 - u)
                    side_reduce(n, u, i)
                    add(n, i, late)

                pairs(dve, step)
                make(last, 1)
                add(before, chunks // 2 - 1, early)
                cut(last, 1)
                side_reduce(before, 0, chunks // 2 - 1)
                add(before, chunks // 2 - 1, late)
                side_reduce(last, 1, chunks // 2 - 1)
                add(last, chunks // 2 - 1, range(OUTS))


def experts(nc, g, name, gate_dram, up_dram, down_dram, gate_row, side=None):
    assert D_EXPERT == 2 * P

    def share(t, e):
        return g.comb[:, t, e:e + 1] if isinstance(e, int) else g.comb[:, t, bass.ds(e, 1)]

    with ExitStack() as own:
        acc = own.enter_context(nc.sbuf_tensor(f"{name}_acc", [P, TILES, D // BANK, BANK], F32))
        hi, lo = (own.enter_context(nc.sbuf_tensor(f"{name}_h_{x}", [P, KD, SEQ], F32R)) for x in ("hi", "lo"))
        split_rows(nc, g, f"{name}_split", hi, lo)
        with Stage(nc, f"{name}_zero") as s:
            zeroed, side_in, acted = s.sem("zeroed"), s.sem("side_in"), s.sem("acted")
            if side is not None:
                side.c = own.enter_context(nc.sbuf_tensor(f"{name}_side_c", [P, KD], F32))
            with s.block() as block:
                @block.vector
                def _(dve):
                    nc.vector.memset(acc[:], 0.0).then_inc(zeroed, 1)

                @block.sync
                def _(sp):
                    if side is not None:
                        sp.dma_start(side.c[:], side.c_dram).then_inc(side_in, 16)

                @block.scalar
                def _(act):
                    if side is not None:
                        act.wait_ge(side_in, 16)
                        nc.scalar.activation(side.c[:], side.c[:], ACT.Silu).then_inc(acted, 1)
        expert_chunks(nc, g, f"{name}_chunks", [gate_dram, up_dram], down_dram, 0, EXPERTS * D_EXPERT // P, hi, lo,
                      ACT.Silu, None, share, acc, side)
        with Stage(nc, f"{name}_sum") as s:
            gated, added = s.sem("gated"), s.sem("added")
            with s.block() as block:
                @block.vector
                def _(dve):
                    for t in range(TILES):
                        rows = acc[:, t].rearrange("p a n -> p (a n)")
                        nc.vector.tensor_tensor(rows, rows, gate_row, ALU.mult).then_inc(gated, 1)
                        dve.wait_ge(gated, t + 1)
                        nc.vector.tensor_tensor(g.x[:, t], g.x[:, t], rows, ALU.add).then_inc(added, 1)


def split_latents(nc, g, name, kv, rope_rows, pos_dram, freq_dram, k, cos, sin):
    HALF = ROPE // 2
    BIG = 1.5 * 2.0 ** 23
    TURN_HI = 6.28125
    TURN_LO = TWO_PI - TURN_HI
    with Stage(nc, name) as s:
        pos_i, pos = s.sb("pos_i", [P, TILES], I32), s.sb("pos", [P, TILES])
        freq = s.sb("freq", [P, HALF])
        angle, turns, size = (s.sb(x, [P, TILES, HALF]) for x in ("angle", "turns", "size"))
        loaded, order, ready, split = s.sem("loaded"), s.sem("order"), s.sem("ready"), s.sem("split")
        kv_heads = [kv[:, t].rearrange("p (h d) -> p h d", h=HEADS) for t in range(TILES)]
        k_heads = [k[:, t].rearrange("p (h d) -> p h d", h=HEADS) for t in range(TILES)]
        with s.block() as block:
            @block.sync
            def _(sp):
                sp.dma_start(pos_i[:], pos_dram).then_inc(loaded, 16)
                sp.dma_start(freq[:], freq_dram).then_inc(loaded, 16)

            @block.gpsimd
            def _(pool):
                for t in range(TILES):
                    nc.gpsimd.tensor_copy(k_heads[t][:, :, :NOPE], kv_heads[t][:, :, :NOPE]).then_inc(split, 1)

            @block.vector
            def _(dve):
                then = Chain(dve, order)
                v = nc.vector
                dve.wait_ge(loaded, 32)
                then(v.tensor_copy(pos[:], pos_i[:]))
                then(v.tensor_tensor(angle[:], pos[:].unsqueeze(2).to_broadcast([P, TILES, HALF]),
                                     freq[:].unsqueeze(1).to_broadcast([P, TILES, HALF]), ALU.mult))
                then(v.tensor_scalar(turns[:], angle[:], 1.0 / TWO_PI, None, ALU.mult))
                then(v.tensor_scalar(turns[:], turns[:], BIG, None, ALU.add))
                then(v.tensor_scalar(turns[:], turns[:], -BIG, None, ALU.add))
                for part in (TURN_HI, TURN_LO):
                    then(v.scalar_tensor_tensor(angle[:], turns[:], -part, angle[:], ALU.mult, ALU.add))
                then(v.tensor_scalar(angle[:], angle[:], 3.1415925, -3.1415925, ALU.min, ALU.max))
                then(v.scalar_tensor_tensor(size[:], angle[:], -1.0, angle[:], ALU.mult, ALU.max))
                v.tensor_scalar(size[:], size[:], -1.0, math.pi / 2, ALU.mult, ALU.add).then_inc(ready, 1)
                for t in range(TILES):
                    v.tensor_copy(k_heads[t][:, :, NOPE:],
                                  rope_rows[:, t].unsqueeze(1).to_broadcast([P, HEADS, ROPE])).then_inc(split, 1)

            @block.scalar
            def _(act):
                act.wait_ge(ready, 1)
                nc.scalar.activation(sin[:], angle[:], ACT.Sin).then_inc(split, 1)
                nc.scalar.activation(cos[:], size[:], ACT.Sin).then_inc(split, 1)


def rotate(nc, name, rows, cos, sin):
    HALF = ROPE // 2
    with Stage(nc, name) as s:
        parts = s.sb("parts", [P, 2, 4, HEADS, HALF])
        times, turned = s.sem("times"), s.sem("turned")
        jobs = [(r, t) for r in rows for t in range(TILES)]
        with s.block() as block:
            @block.vector
            def _(dve):
                v = nc.vector
                for n, (r, t) in enumerate(jobs):
                    heads = r[:, t].rearrange("p (h d) -> p h d", h=HEADS)
                    x1, x2 = heads[:, :, NOPE:NOPE + HALF], heads[:, :, NOPE + HALF:]
                    c, d = (y[:, t].unsqueeze(1).to_broadcast([P, HEADS, HALF]) for y in (cos, sin))
                    part = parts[:, n % 2]
                    if n >= 2:
                        dve.wait_ge(turned, 2 * (n - 1))
                    for j, (a, b) in enumerate(((x1, c), (x2, d), (x1, d), (x2, c))):
                        v.tensor_tensor(part[:, j], a, b, ALU.mult).then_inc(times, 1)
                    dve.wait_ge(times, 4 * n + 4)
                    v.tensor_tensor(x1, part[:, 0], part[:, 1], ALU.subtract).then_inc(turned, 1)
                    v.tensor_tensor(x2, part[:, 2], part[:, 3], ALU.add).then_inc(turned, 1)
CONV, TAPS = 512, 31
CC = CONV // P
RW, RW_HEADS, RW_DIM = 512, 8, 64
RC = RW // P
LORA = 64
IN_CHUNKS = 22
SPAN = 32
BLOCKS = P // SPAN
SPANS = SEQ // SPAN
ALPHA = 2.0 ** 0.25


def turn_cols(nc, g, name, cols, chunks, keeps):
    with Stage(nc, name) as s:
        pt = s.ps("pt", [P, 2, chunks, P])
        done, kept = s.sem("done"), s.sem("kept")
        with s.block() as block:
            @block.tensor
            def _(pe):
                for t in range(TILES):
                    if t >= 2:
                        pe.wait_ge(kept, t - 1)
                    for c in range(chunks):
                        last = nc.tensor.transpose(pt[:, t % 2, c], cols[:, c, t * P:(t + 1) * P], g.ident[:])
                    last.then_inc(done, 1)

            @block.scalar
            def _(act):
                for t in range(TILES):
                    act.wait_ge(done, t + 1)
                    nc.scalar.copy(keeps[t], pt[:, t % 2].rearrange("p c n -> p (c n)")).then_inc(kept, 1)


def hybrid_in(nc, g, name, w_in_dram, conv_w, conv_b, pT, out):
    PAD, CONV_CHUNKS, SLOTS = TAPS - 1, 2 * CC, 2
    with Stage(nc, name) as s:
        ring = s.sb("ring", [P, SLOTS, KD, P])
        w, b = s.sb("w", [P, CC, TAPS]), s.sb("b", [P, CC])
        bent = g.mod[:, 0:CC * SEQ // D].rearrange("p a (b n) -> p (a b) n", n=SEQ)
        u = s.sb("u", [P, CC, PAD + SEQ])
        acc = s.ps("acc", [P, SLOTS, BANK])
        w_in = [s.sem(f"w_in{j}") for j in range(SLOTS)]
        summed, kept = s.sem("summed"), s.sem("kept")
        loaded, bent_done, order = s.sem("loaded"), s.sem("bent_done"), s.sem("order")
        with s.block() as block:
            @block.sync
            def _(sp):
                for j in range(SLOTS):
                    sp.dma_start(ring[:, j], w_in_dram[j]).then_inc(w_in[j], 16)
                sp.dma_start(w[:], conv_w).then_inc(loaded, 16)
                sp.dma_start(b[:], conv_b).then_inc(loaded, 16)
                with sp.Fori(0, IN_CHUNKS // SLOTS - 1) as i:
                    for j in range(SLOTS):
                        sp.wait_ge(summed, SLOTS * i + j + 1)
                        sp.dma_start(ring[:, j], w_in_dram[bass.ds(SLOTS * (i + 1) + j, 1)].rearrange(
                            "o p k n -> p (o k) n")).then_inc(w_in[j], 16)

            @block.tensor
            def _(pe):
                with pe.Fori(0, IN_CHUNKS // SLOTS) as i:
                    for j in range(SLOTS):
                        pe.wait_ge(w_in[j], 16 * i + 16)
                        pe.wait_ge(kept, SLOTS * i + j + 1)
                        for k in range(KD):
                            last = nc.tensor.matmul(acc[:, j], ring[:, j, k], g.hT[:, k], start=(k == 0), stop=(k == KD - 1))
                        last.then_inc(summed, 1)

            @block.scalar
            def _(act):
                def keep(start, end):
                    with act.Fori(start // SLOTS, end // SLOTS) as i:
                        for j in range(SLOTS):
                            act.wait_ge(summed, SLOTS * i + j + 1)
                            nc.scalar.copy(pT[:, bass.ds(SLOTS * i + j, 1)], acc[:, j]).then_inc(kept, 1)

                act.sem_inc(kept, SLOTS)
                keep(0, CONV_CHUNKS)
                act.wait_ge(kept, SLOTS + CONV_CHUNKS)
                nc.scalar.activation(bent, pT[:, CC:CONV_CHUNKS], ACT.Sigmoid).then_inc(bent_done, 1)
                keep(CONV_CHUNKS, IN_CHUNKS)

            @block.vector
            def _(dve):
                v = nc.vector
                v.memset(u[:, :, :PAD], 0.0).then_inc(order, 1)
                dve.wait_ge(bent_done, 1)
                v.tensor_tensor(u[:, :, PAD:], pT[:, :CC], bent, ALU.mult).then_inc(order, 1)
                dve.wait_ge(order, 2)
                dve.wait_ge(loaded, 32)
                for j in range(TAPS):
                    for c in range(CC):
                        if j == 0:
                            v.tensor_scalar(out[:, c], u[:, c, :SEQ], w[:, c, 0:1], b[:, c:c + 1],
                                            ALU.mult, ALU.add).then_inc(order, 1)
                        else:
                            dve.wait_ge(order, 2 + CC * (j - 1) + c + 1)
                            v.scalar_tensor_tensor(out[:, c], u[:, c, j:j + SEQ], w[:, c, j:j + 1], out[:, c],
                                                   ALU.mult, ALU.add).then_inc(order, 1)


def conv_norm(nc, g, name, rows, g_dram, b_dram, y):
    with Stage(nc, name) as s:
        gain, shift = s.sb("gain", [P, CONV]), s.sb("shift", [P, CONV])
        stat, ms = s.sb("stat", [P, TILES, 6]), s.sb("ms", [P, TILES, 2])
        root, rstd = s.sb("root", [P, TILES]), s.sb("rstd", [P, TILES])
        loaded, order, rooted, ready, shifted, bent = (s.sem(x) for x in ("loaded", "order", "rooted", "ready", "shifted", "bent"))
        with s.block() as block:
            @block.sync
            def _(sp):
                sp.dma_start(gain[:], g_dram).then_inc(loaded, 16)
                sp.dma_start(shift[:], b_dram).then_inc(loaded, 16)

            @block.scalar
            def _(act):
                act.wait_ge(ready, 1)
                nc.scalar.activation(root[:], rstd[:], ACT.Sqrt).then_inc(rooted, 1)
                for t in range(TILES):
                    act.wait_ge(shifted, t + 1)
                    nc.scalar.activation(y[:, t, :CONV], rows[:, t], ACT.Silu).then_inc(bent, 1)

            @block.vector
            def _(dve):
                then = Chain(dve, order)
                v = nc.vector
                for t in range(TILES):
                    then(v.bn_stats(stat[:, t], rows[:, t]))
                    then(v.bn_aggr(ms[:, t], stat[:, t]))
                v.tensor_scalar(rstd[:], ms[:, :, 1], LN_EPS, None, ALU.add).then_inc(ready, 1)
                dve.wait_ge(rooted, 1)
                then(v.reciprocal(rstd[:], root[:]))
                dve.wait_ge(loaded, 32)
                for t in range(TILES):
                    then(v.tensor_scalar(rows[:, t], rows[:, t], ms[:, t, 0:1], rstd[:, t:t + 1], ALU.subtract, ALU.mult))
                    then(v.tensor_tensor(rows[:, t], rows[:, t], gain[:], ALU.mult))
                    v.tensor_tensor(rows[:, t], rows[:, t], shift[:], ALU.add).then_inc(shifted, 1)


def rwkv_inputs(nc, g, name, a, pT, o):
    R_AT, K_AT, V_AT, WA_AT, G_AT = 0, RC, 2 * RC, 3 * RC, 3 * RC + 1
    N = 3 * RC + 2
    p = pT[:, 2 * CC:]
    with Stage(nc, name) as s:
        mu = s.sb("mu", [P, N])
        col = s.sb("col", [P, 5, RC])
        w2a2, g2 = s.sb("w2a2", [P, RW]), s.sb("g2", [P, RW])
        pairs, heads = s.sb("pairs", [P, P]), s.sb("heads", [P, 2])
        xm, diff = p, s.sb("diff", [P, SEQ])
        bent = s.sb("bent", [P, SEQ])
        fresh = s.sb("fresh", [P, SEQ])
        logd, total, k2 = o.alpha, o.grown, o.kappa
        a_, tmp = g.hT[:, :RC], g.hT[:, RC:]
        kk = s.sb("kk", [P, RC, SEQ])
        acc = s.ps("acc", [P, 4, SEQ])
        loaded, order, rooted = s.sem("loaded"), s.sem("order"), s.sem("rooted")
        mixed, bent_done, sent, taken = s.sem("mixed"), s.sem("bent_done"), s.sem("sent"), s.sem("taken")
        squared, normed_, grown, ready, rows = s.sem("squared"), s.sem("normed"), s.sem("grown"), s.sem("ready"), s.sem("rows")
        LOADS = 7 * 16
        W0, A0, KK, KA, RK = range(5)
        with s.block() as block:
            @block.sync
            def _(sp):
                for dst, src in ((mu, "mu"), (col, "rw_col"), (w2a2, "w2a2"), (g2, "rw_g2"), (pairs, "pairs"),
                                 (heads, "heads"), (fresh, "fresh")):
                    sp.dma_start(dst[:], a[src]).then_inc(loaded, 16)

            @block.scalar
            def _(act):
                act.wait_ge(mixed, N)
                nc.scalar.activation(bent[:LORA], xm[:LORA, WA_AT], ACT.Tanh).then_inc(bent_done, 1)
                nc.scalar.copy(bent[LORA:], xm[LORA:, WA_AT]).then_inc(bent_done, 1)
                nc.scalar.activation(xm[:, G_AT], xm[:, G_AT], ACT.Sigmoid).then_inc(bent_done, 1)
                for c in range(RC):
                    act.wait_ge(sent, 2 * c + 1)
                    nc.scalar.activation(logd[:, c], acc[:, 0], ACT.Sigmoid, bias=col[:, W0, c:c + 1]).then_inc(taken, 1)
                    act.wait_ge(sent, 2 * c + 2)
                    nc.scalar.activation(a_[:, c], acc[:, 1], ACT.Sigmoid, bias=col[:, A0, c:c + 1]).then_inc(taken, 1)
                for c in range(RC):
                    act.wait_ge(sent, 2 * RC + c + 1)
                    nc.scalar.activation(tmp[:, c], acc[:, 2], ACT.Sqrt).then_inc(rooted, 1)
                act.wait_ge(order, 2)
                nc.scalar.activation(o.beta[:], total[:], ACT.Exp, scale=-1.0).then_inc(grown, 1)
                nc.scalar.activation(o.alpha[:], logd[:], ACT.Exp).then_inc(grown, 1)
                act.wait_ge(grown, 1)
                nc.scalar.activation(o.grown[:], total[:], ACT.Exp).then_inc(grown, 1)
                for t in range(TILES):
                    act.wait_ge(rows, t + 1)
                    nc.scalar.copy(o.gate[:, t], acc[:, t % 2]).then_inc(taken, 1)
                act.wait_ge(rows, TILES + 1)
                nc.scalar.copy(o.bonus[:], acc[:, 3, :TILES * RW_HEADS].rearrange("p (t h) -> p t h", t=TILES)).then_inc(taken, 1)

            @block.tensor
            def _(pe):
                pe.wait_ge(loaded, LOADS)
                pe.wait_ge(bent_done, 3)
                for c in range(RC):
                    if c:
                        pe.wait_ge(taken, 2 * c - 1)
                    nc.tensor.matmul(acc[:, 0], w2a2[:LORA, c * P:(c + 1) * P], bent[:LORA], start=True, stop=True).then_inc(sent, 1)
                    if c:
                        pe.wait_ge(taken, 2 * c)
                    nc.tensor.matmul(acc[:, 1], w2a2[LORA:, c * P:(c + 1) * P], bent[LORA:], start=True, stop=True).then_inc(sent, 1)
                for c in range(RC):
                    pe.wait_ge(squared, c + 1)
                    if c:
                        pe.wait_ge(rooted, c)
                    nc.tensor.matmul(acc[:, 2], pairs[:], tmp[:, c], start=True, stop=True).then_inc(sent, 1)
                pe.wait_ge(taken, 2 * RC)
                for t in range(TILES):
                    if t >= 2:
                        pe.wait_ge(taken, 2 * RC + t - 1)
                    nc.tensor.matmul(acc[:, t % 2], xm[:, G_AT, t * P:(t + 1) * P], g2[:], start=True, stop=True).then_inc(rows, 1)
                pe.wait_ge(ready, RC)
                for t in range(TILES):
                    for c in range(RC):
                        at = t * RW_HEADS + 2 * c
                        last = nc.tensor.matmul(acc[:, 3, at:at + 2], kk[:, c, t * P:(t + 1) * P], heads[:], start=True, stop=True)
                last.then_inc(rows, 1)

            @block.vector
            def _(dve):
                v = nc.vector
                steps = s.sem("steps")
                then = Chain(dve, steps)
                dve.wait_ge(loaded, LOADS)
                for n in range(N):
                    then(v.tensor_tensor(diff[:, 1:], p[:, n, :SEQ - 1], p[:, n, 1:], ALU.subtract))
                    then(v.tensor_scalar(diff[:, 0:1], p[:, n, 0:1], -1.0, None, ALU.mult))
                    v.scalar_tensor_tensor(xm[:, n], diff[:], mu[:, n:n + 1], p[:, n], ALU.mult, ALU.add).then_inc(mixed, 1)
                    dve.wait_ge(mixed, n + 1)
                for c in range(RC):
                    then(v.tensor_scalar(kk[:, c], xm[:, K_AT + c], col[:, KK, c:c + 1], None, ALU.mult))
                    v.tensor_tensor(tmp[:, c], kk[:, c], kk[:, c], ALU.mult).then_inc(squared, 1)
                dve.wait_ge(taken, 2 * RC)
                then(v.tensor_scalar(logd[:], logd[:], -math.exp(-0.5), None, ALU.mult))
                for c in range(RC):
                    then(v.tensor_tensor_scan(total[:, c], fresh[:], logd[:, c], 0.0, ALU.mult, ALU.add))
                v.tensor_tensor(logd[:], total[:], logd[:], ALU.subtract).then_inc(order, 2)
                for c in range(RC):
                    then(v.tensor_scalar(k2[:, c], a_[:, c], -1.0, col[:, KA, c:c + 1], ALU.add, ALU.mult))
                    then(v.scalar_tensor_tensor(k2[:, c], k2[:, c], 1.0, xm[:, K_AT + c], ALU.add, ALU.mult))
                dve.wait_ge(rooted, RC)
                then(v.tensor_scalar(tmp, tmp, 1e-12, None, ALU.max))
                then(v.reciprocal(tmp, tmp))
                then(v.tensor_tensor(kk[:], kk[:], tmp, ALU.mult))
                dve.wait_ge(grown, 3)
                then(v.scalar_tensor_tensor(o.alpha[:], o.alpha[:], -1.0, kk[:], ALU.mult, ALU.mult))
                then(v.tensor_tensor(tmp, kk[:], a_, ALU.mult))
                for c in range(RC):
                    v.scalar_tensor_tensor(kk[:, c], xm[:, R_AT + c], col[:, RK, c:c + 1], k2[:, c],
                                           ALU.mult, ALU.mult).then_inc(ready, 1)
                dve.wait_ge(ready, RC)
                then(v.tensor_tensor(o.kappa[:], k2[:], o.beta[:], ALU.mult))
                then(v.tensor_tensor(o.beta[:], o.beta[:], tmp, ALU.mult))
                then(v.tensor_tensor(o.rho[:], o.grown[:], xm[:, R_AT:R_AT + RC], ALU.mult))
                then(v.tensor_copy(o.value[:], xm[:, V_AT:V_AT + RC]))
def rwkv(nc, g, name, a, o, y):
    UNITS = TILES * RW_HEADS
    units = [(t, c, h) for t in range(TILES) for h in range(2) for c in range(RC)]
    cols = [slice((2 * c + h) * RW_DIM, (2 * c + h + 1) * RW_DIM) for _, c, h in units]
    feats = [slice(h * RW_DIM, (h + 1) * RW_DIM) for _, _, h in units]
    toks = [slice(t * P, (t + 1) * P) for t, _, _ in units]
    flat = lambda buf: buf.rearrange("p a n -> p (a n)")
    own = ExitStack()
    rows = {x: own.enter_context(nc.sbuf_tensor(f"{name}_{x}_rows", [P, TILES, RW], F32)) for x in ("alpha", "beta", "kappa", "value")}
    cols_of = {"alpha": o.alpha, "beta": o.beta, "kappa": o.kappa, "value": o.value}
    for x, buf in rows.items():
        turn_cols(nc, g, f"{name}_turn_{x}", cols_of[x], RC, [buf[:, t] for t in range(TILES)])
    solved = own.enter_context(nc.sbuf_tensor(f"{name}_solved", [P, UNITS, P], F32))
    inner = nc.dram_tensor(f"{name}_inner", [BLOCKS, UNITS, SPAN, SPAN], F32, kind="Internal").ap()
    outer = nc.dram_tensor(f"{name}_outer", [BLOCKS, UNITS, SPAN, SPAN], F32, kind="Internal").ap()

    with Stage(nc, f"{name}_solve") as s:
        masks = s.sb("masks", [P, 4, P])
        m_all = s.sb("m_all", [P, UNITS, P])
        m_rows, t_cols = s.sb("m_rows", [P, SPAN, SPAN]), s.sb("t_cols", [P, SPAN, SPAN])
        prod = flat(g.hT[:, :SPAN * SPAN // SEQ]).rearrange("p (s t) -> p s t", s=SPAN)
        acc = s.ps("acc", [P, 4, RC, P])
        loaded, zeroed, paired, masked = s.sem("loaded"), s.sem("zeroed"), s.sem("paired"), s.sem("masked")
        stored, spread, times, found, back, placed = (s.sem(x) for x in ("stored", "spread", "times", "found", "back", "placed"))
        with s.block() as block:
            @block.sync
            def _(sp):
                sp.dma_start(masks[:], a["masks"]).then_inc(loaded, 16)
                sp.wait_ge(masked, UNITS // RC)
                for b in range(BLOCKS):
                    part = slice(b * SPAN, (b + 1) * SPAN)
                    sp.dma_start(inner[b].rearrange("m t s -> t m s"), m_all[part, :, part]).then_inc(stored, 16)
                sp.wait_ge(stored, 16 * BLOCKS)
                sp.dma_start(m_rows[:], inner.rearrange("b m t s -> (b m) t s")).then_inc(spread, 16)
                sp.wait_ge(found, SPAN)
                sp.dma_start(outer.rearrange("b m s t -> (b m) s t"), t_cols[:]).then_inc(back, 16)
                sp.wait_ge(back, 16)
                sp.wait_ge(zeroed, 1)
                for b in range(BLOCKS):
                    part = slice(b * SPAN, (b + 1) * SPAN)
                    sp.dma_start(solved[part, :, part], outer[b].rearrange("m s t -> s m t")).then_inc(placed, 16)
                sp.wait_ge(placed, 16 * BLOCKS)

            @block.gpsimd
            def _(pool):
                nc.gpsimd.memset(solved[:], 0.0).then_inc(zeroed, 1)

            @block.tensor
            def _(pe):
                for m, (t, c, h) in enumerate(units):
                    n = m // RC
                    if n >= 4 and c == 0:
                        pe.wait_ge(masked, n - 3)
                    last = nc.tensor.matmul(acc[:, n % 4, c], o.alpha[feats[m], c, toks[m]], o.beta[feats[m], c, toks[m]],
                                            start=True, stop=True)
                    if c == RC - 1:
                        last.then_inc(paired, 1)

            @block.vector
            def _(dve):
                v = nc.vector
                dve.wait_ge(loaded, 16)
                for n in range(UNITS // RC):
                    dve.wait_ge(paired, n + 1)
                    v.tensor_tensor(m_all[:, n * RC:(n + 1) * RC], acc[:, n % 4], masks[:, 0].unsqueeze(1).to_broadcast([P, RC, P]),
                                    ALU.mult).then_inc(masked, 1)
                v.memset(t_cols[:], 0.0).then_inc(times, 1)
                dve.wait_ge(times, 1)
                v.memset(flat(t_cols[:])[:, ::SPAN + 1], 1.0).then_inc(found, 1)
                dve.wait_ge(spread, 16)
                for i in range(1, SPAN):
                    dve.wait_ge(found, i)
                    v.tensor_tensor(prod[:, :i, :i], t_cols[:, :i, :i], m_rows[:, i, :i].unsqueeze(1).to_broadcast([P, i, i]),
                                    ALU.mult).then_inc(times, 1)
                    dve.wait_ge(times, i + 1)
                    v.tensor_reduce(t_cols[:, :i, i], prod[:, :i, :i], AX, ALU.add).then_inc(found, 1)

    step = own.enter_context(nc.sbuf_tensor(f"{name}_step", [P, RC, SPANS, RW_DIM], F32))
    lead = g.hT[:, :RC]
    pieces = [flat(g.hT[:, RC:])[:, :SPANS * RW_DIM], flat(g.hT[:, RC:])[:, SPANS * RW_DIM:], g.mod[:, 0], g.mod[:, 1]]
    new = [x.rearrange("p (n v) -> p n v", n=SPANS) for x in pieces]
    with Stage(nc, f"{name}_spans") as s:
        masks, span = s.sb("masks", [P, 4, P]), s.sb("span", [P, BLOCKS])
        nef = s.sb("nef", [P, 2, 3, P])
        nv, pq = s.sb("nv", [P, 2, RW_DIM]), s.sb("pq", [P, 2, 2, RW_DIM])
        beta_in, value_in, q_in = (s.sb(x, [P, 2, BLOCKS, RW_DIM]) for x in ("beta_in", "value_in", "q_in"))
        pair, mid = s.ps("pair", [P, 2, BANK]), s.ps("mid", [P, 2, BANK])
        out, state = s.ps("out", [P, 2, BANK]), s.ps("state", [P, 2, 2, BLOCKS, RW_DIM])
        loaded, paired, masked, nv_done, nv_kept = (s.sem(x) for x in ("loaded", "paired", "masked", "nv_done", "nv_kept"))
        pq_done, pq_kept, spread, q_spread, out_done = (s.sem(x) for x in ("pq_done", "pq_kept", "spread", "q_spread", "out_done"))
        out_kept, row_kept, state_done, state_kept = (s.sem(x) for x in ("out_kept", "row_kept", "state_done", "state_kept"))
        with s.block() as block:
            @block.sync
            def _(sp):
                sp.dma_start(masks[:], a["masks"]).then_inc(loaded, 16)
                sp.dma_start(span[:], a["span"]).then_inc(loaded, 16)

            @block.gpsimd
            def _(pool):
                pool.wait_ge(loaded, 32)
                here = span[:].unsqueeze(2).to_broadcast([P, BLOCKS, RW_DIM])
                for m, (t, c, h) in enumerate(units):
                    if m >= 2:
                        pool.wait_ge(state_done, m - 1)
                    for src, dst in (("beta", beta_in), ("value", value_in)):
                        nc.gpsimd.tensor_tensor(dst[:, m % 2], rows[src][:, t, cols[m]].unsqueeze(1).to_broadcast([P, BLOCKS, RW_DIM]),
                                                here, ALU.mult).then_inc(spread, 1)

            @block.tensor
            def _(pe):
                def open_(m):
                    t, c, h = units[m]
                    if m >= 2:
                        pe.wait_ge(masked, m - 1)
                    for j, (left, right) in enumerate(((o.kappa, o.alpha), (o.beta, o.rho), (o.kappa, o.rho))):
                        last = nc.tensor.matmul(pair[:, m % 2, j * P:(j + 1) * P], left[feats[m], c, toks[m]],
                                                right[feats[m], c, toks[m]], start=True, stop=True)
                    last.then_inc(paired, 1)

                def solve(m):
                    t, c, h = units[m]
                    pe.wait_ge(masked, m + 1)
                    if m >= 2:
                        pe.wait_ge(pq_kept, m - 1)
                    nc.tensor.matmul(mid[:, m % 2, P:P + RW_DIM], solved[:, m], rows["alpha"][:, t, cols[m]], start=True, stop=True)
                    nc.tensor.matmul(mid[:, m % 2, :RW_DIM], nef[:, m % 2, 0], rows["value"][:, t, cols[m]],
                                     start=True, stop=True).then_inc(nv_done, 1)
                    pe.wait_ge(nv_kept, m + 1)
                    nc.tensor.matmul(mid[:, m % 2, P + RW_DIM:2 * P], solved[:, m], nv[:, m % 2], start=True, stop=True).then_inc(pq_done, 1)

                def close(m):
                    t, c, h = units[m]
                    pe.wait_ge(pq_kept, m + 1)
                    if m >= 2:
                        pe.wait_ge(out_kept, m - 1)
                        pe.wait_ge(row_kept, m - 1)
                    nc.tensor.matmul(out[feats[m], m % 2, :P], pq[:, m % 2, 0], nef[:, m % 2, 1], start=True, stop=True)
                    nc.tensor.matmul(out[:, m % 2, P:P + RW_DIM], nef[:, m % 2, 1], pq[:, m % 2, 1], start=True, stop=False)
                    nc.tensor.matmul(out[:, m % 2, P:P + RW_DIM], nef[:, m % 2, 2], rows["value"][:, t, cols[m]],
                                     start=False, stop=True).then_inc(out_done, 1)
                    pe.wait_ge(spread, 2 * m + 2)
                    pe.wait_ge(q_spread, m + 1)
                    if m >= 2:
                        pe.wait_ge(state_kept, 2 * (m - 1))
                    nc.tensor.matmul(state[feats[m], m % 2, 0], pq[:, m % 2, 0], beta_in[:, m % 2], start=True, stop=True)
                    nc.tensor.matmul(state[feats[m], m % 2, 1], rows["beta"][:, t, cols[m]], q_in[:, m % 2], start=True, stop=False)
                    nc.tensor.matmul(state[feats[m], m % 2, 1], rows["kappa"][:, t, cols[m]], value_in[:, m % 2],
                                     start=False, stop=True).then_inc(state_done, 1)

                pe.wait_ge(loaded, 32)
                open_(0)
                for m in range(UNITS):
                    if m + 1 < UNITS:
                        open_(m + 1)
                    solve(m)
                    close(m)

            @block.scalar
            def _(act):
                for m, (t, c, h) in enumerate(units):
                    act.wait_ge(nv_done, m + 1)
                    if m >= 2:
                        act.wait_ge(pq_done, m - 1)
                    nc.scalar.copy(nv[:, m % 2], mid[:, m % 2, :RW_DIM]).then_inc(nv_kept, 1)
                    act.wait_ge(pq_done, m + 1)
                    if m >= 2:
                        act.wait_ge(state_done, m - 1)
                        act.wait_ge(q_spread, m - 1)
                    nc.scalar.copy(pq[:, m % 2].rearrange("p a n -> p (a n)"), mid[:, m % 2, P:2 * P]).then_inc(pq_kept, 1)
                    act.wait_ge(out_kept, m + 1)
                    nc.scalar.copy(y[:, t, CONV + cols[m].start:CONV + cols[m].stop], out[:, m % 2, P:P + RW_DIM]).then_inc(row_kept, 1)

            @block.vector
            def _(dve):
                v = nc.vector

                def mask(m):
                    dve.wait_ge(paired, m + 1)
                    if m >= 2:
                        dve.wait_ge(out_done, m - 1)
                    v.tensor_tensor(nef[:, m % 2], pair[:, m % 2, :3 * P].rearrange("p (j n) -> p j n", j=3), masks[:, 1:],
                                    ALU.mult).then_inc(masked, 1)

                dve.wait_ge(loaded, 32)
                mask(0)
                for m, (t, c, h) in enumerate(units):
                    if m + 1 < UNITS:
                        mask(m + 1)
                    dve.wait_ge(pq_kept, m + 1)
                    if m >= 2:
                        dve.wait_ge(state_done, m - 1)
                    v.tensor_tensor(q_in[:, m % 2], pq[:, m % 2, 1].unsqueeze(1).to_broadcast([P, BLOCKS, RW_DIM]),
                                    span[:].unsqueeze(2).to_broadcast([P, BLOCKS, RW_DIM]), ALU.mult).then_inc(q_spread, 1)
                    dve.wait_ge(out_done, m + 1)
                    v.tensor_tensor(lead[feats[m], c, toks[m]], out[feats[m], m % 2, :P], o.rho[feats[m], c, toks[m]],
                                    ALU.add).then_inc(out_kept, 1)
                    dve.wait_ge(state_done, m + 1)
                    spans = slice(t * BLOCKS, (t + 1) * BLOCKS)
                    v.tensor_tensor(step[feats[m], c, spans], state[feats[m], m % 2, 0],
                                    g.ident[feats[m], feats[m]].unsqueeze(1).to_broadcast([RW_DIM, BLOCKS, RW_DIM]), ALU.add).then_inc(state_kept, 1)
                    ends = o.grown[feats[m], c, t * P + SPAN - 1:(t + 1) * P:SPAN]
                    v.tensor_tensor(new[c][feats[m], spans], state[feats[m], m % 2, 1],
                                    ends.unsqueeze(2).to_broadcast([RW_DIM, BLOCKS, RW_DIM]), ALU.mult).then_inc(state_kept, 1)

    z = [flat((o.alpha, o.beta)[c // 2][:])[:, (c % 2) * SPANS * RW_DIM:(c % 2 + 1) * SPANS * RW_DIM].rearrange(
        "p (n v) -> p n v", n=SPANS) for c in range(RC)]
    apart = [flat(b[:]).rearrange("p (n h v) -> p n h v", n=SPANS, h=2) for b in (o.kappa, o.rho, rows["alpha"], rows["beta"])]
    with Stage(nc, f"{name}_state") as s:
        heads = s.sb("heads", [P, 2])
        acc = s.ps("acc", [P, 2, 2, RC, RW_DIM])
        rest = s.ps("rest", [P, 2, BANK])
        loaded, moved, stepped, apart_done, inter, added = (s.sem(x) for x in ("loaded", "moved", "stepped", "apart_done", "inter", "added"))
        with s.block() as block:
            @block.sync
            def _(sp):
                sp.dma_start(heads[:], a["heads"]).then_inc(loaded, 16)

            @block.tensor
            def _(pe):
                for n in range(1, SPANS - 1):
                    pe.wait_ge(stepped, 2 * RC * n)
                    for c in range(RC):
                        for h in range(2):
                            f = slice(h * RW_DIM, (h + 1) * RW_DIM)
                            last = nc.tensor.matmul(acc[f, n % 2, h, c], step[f, c, n], z[c][f, n], start=True, stop=True)
                    last.then_inc(moved, 1)
                pe.wait_ge(apart_done, 2 * RC)
                for t in range(TILES):
                    if t >= 2:
                        pe.wait_ge(added, t - 1)
                    for b in range(BLOCKS):
                        for c in range(RC):
                            at = t * P + b * SPAN
                            last = nc.tensor.matmul(rest[b * SPAN:(b + 1) * SPAN, t % 2, c * P:(c + 1) * P], lead[:, c, at:at + SPAN],
                                                    apart[c][:, t * BLOCKS + b], start=True, stop=True)
                    last.then_inc(inter, 1)

            @block.vector
            def _(dve):
                v = nc.vector
                for c in range(RC):
                    v.memset(z[c][:, 0], 0.0).then_inc(stepped, 1)
                    v.tensor_copy(z[c][:, 1], new[c][:, 0]).then_inc(stepped, 1)
                for n in range(1, SPANS - 1):
                    dve.wait_ge(moved, n)
                    for c in range(RC):
                        for h in range(2):
                            f = slice(h * RW_DIM, (h + 1) * RW_DIM)
                            v.scalar_tensor_tensor(z[c][f, n + 1], acc[f, n % 2, h, c], o.grown[f, c, (n + 1) * SPAN - 1:(n + 1) * SPAN],
                                                   new[c][f, n], ALU.mult, ALU.add).then_inc(stepped, 1)
                dve.wait_ge(loaded, 16)
                dve.wait_ge(stepped, 2 * RC * (SPANS - 1))
                for c in range(RC):
                    for h in range(2):
                        v.tensor_scalar(apart[c][:, :, h], z[c], heads[:, h:h + 1], None, ALU.mult).then_inc(apart_done, 1)
                for t in range(TILES):
                    dve.wait_ge(inter, t + 1)
                    v.tensor_tensor(y[:, t, CONV:], y[:, t, CONV:], rest[:, t % 2], ALU.add).then_inc(added, 1)

    with Stage(nc, f"{name}_norm") as s:
        gain, shift = s.sb("gain", [P, RW]), s.sb("shift", [P, RW])
        square = s.sb("square", [P, 2, RW_HEADS, RW_DIM])
        mean, var, root = (s.sb(x, [P, TILES, RW_HEADS]) for x in ("mean", "var", "root"))
        loaded, order, rooted, ready = s.sem("loaded"), s.sem("order"), s.sem("rooted"), s.sem("ready")
        wide = [P, RW_HEADS, RW_DIM]
        with s.block() as block:
            @block.sync
            def _(sp):
                sp.dma_start(gain[:], a["rw_gain"]).then_inc(loaded, 16)
                sp.dma_start(shift[:], a["rw_shift"]).then_inc(loaded, 16)

            @block.scalar
            def _(act):
                act.wait_ge(ready, 1)
                nc.scalar.activation(root[:], var[:], ACT.Sqrt).then_inc(rooted, 1)

            @block.vector
            def _(dve):
                v = nc.vector
                then = Chain(dve, order)
                part = lambda buf, t: buf[:, t].rearrange("p (h d) -> p h d", d=RW_DIM)
                ys = [y[:, t, CONV:].rearrange("p (h d) -> p h d", d=RW_DIM) for t in range(TILES)]
                for t in range(TILES):
                    then(v.tensor_reduce(mean[:, t], ys[t], AX, ALU.add))
                then(v.tensor_scalar(mean[:], mean[:], 1.0 / RW_DIM, None, ALU.mult))
                for t in range(TILES):
                    then(v.tensor_tensor(ys[t], ys[t], mean[:, t].unsqueeze(2).to_broadcast(wide), ALU.subtract))
                    then(v.tensor_tensor(square[:, t % 2], ys[t], ys[t], ALU.mult))
                    then(v.tensor_reduce(var[:, t], square[:, t % 2], AX, ALU.add))
                v.tensor_scalar(var[:], var[:], 1.0 / RW_DIM, GN_EPS, ALU.mult, ALU.add).then_inc(ready, 1)
                dve.wait_ge(rooted, 1)
                then(v.reciprocal(var[:], root[:]))
                dve.wait_ge(loaded, 32)
                for t in range(TILES):
                    then(v.tensor_tensor(ys[t], ys[t], var[:, t].unsqueeze(2).to_broadcast(wide), ALU.mult))
                    then(v.tensor_tensor(y[:, t, CONV:], y[:, t, CONV:], gain[:], ALU.mult))
                    then(v.tensor_tensor(y[:, t, CONV:], y[:, t, CONV:], shift[:], ALU.add))
                    then(v.tensor_tensor(square[:, t % 2], part(rows["value"], t), o.bonus[:, t].unsqueeze(2).to_broadcast(wide), ALU.mult))
                    then(v.tensor_tensor(ys[t], ys[t], square[:, t % 2], ALU.add))
                    then(v.tensor_tensor(y[:, t, CONV:], y[:, t, CONV:], o.gate[:, t], ALU.mult))
    own.close()


def layer_norm_rows(nc, g, name, g_dram, b_dram):
    with Stage(nc, name) as s:
        gain, shift = s.sb("gain", [P, D]), s.sb("shift", [P, D])
        stat, ms = s.sb("stat", [P, TILES, 2, 6]), s.sb("ms", [P, TILES, 2])
        root, rstd = s.sb("root", [P, TILES]), s.sb("rstd", [P, TILES])
        loaded, order, rooted, ready = s.sem("loaded"), s.sem("order"), s.sem("rooted"), s.sem("ready")
        with s.block() as block:
            @block.sync
            def _(sp):
                sp.dma_start(gain[:], g_dram).then_inc(loaded, 16)
                sp.dma_start(shift[:], b_dram).then_inc(loaded, 16)

            @block.scalar
            def _(act):
                act.wait_ge(ready, 1)
                nc.scalar.activation(root[:], rstd[:], ACT.Sqrt).then_inc(rooted, 1)

            @block.vector
            def _(dve):
                then = Chain(dve, order)
                v = nc.vector
                for t in range(TILES):
                    for half in range(2):
                        then(v.bn_stats(stat[:, t, half], g.x[:, t, half * D // 2:(half + 1) * D // 2]))
                    then(v.bn_aggr(ms[:, t], stat[:, t]))
                v.tensor_scalar(rstd[:], ms[:, :, 1], LN_EPS, None, ALU.add).then_inc(ready, 1)
                dve.wait_ge(rooted, 1)
                then(v.reciprocal(rstd[:], root[:]))
                dve.wait_ge(loaded, 32)
                for t in range(TILES):
                    then(v.tensor_scalar(g.x[:, t], g.x[:, t], ms[:, t, 0:1], rstd[:, t:t + 1], ALU.subtract, ALU.mult))
                    then(v.tensor_tensor(g.x[:, t], g.x[:, t], gain[:], ALU.mult))
                    then(v.tensor_tensor(g.x[:, t], g.x[:, t], shift[:], ALU.add))
KEYS, TOP, PEER_HEADS = 128, 16, 8
PICKS = PEER_HEADS * TOP
GROUP = 8
SET = 4
PART = 32


def top16(then, v, lists):
    then(*[v.max(values[:, :8], work) for values, at, work in lists])
    then(*[v.max_index(at[:, :8], values[:, :8], work) for values, at, work in lists])
    then(*[v.match_replace(work, values[:, :8], work, NEG) for values, at, work in lists])
    then(*[v.max(values[:, 8:], work) for values, at, work in lists])
    then(*[v.max_index(at[:, 8:], values[:, 8:], work) for values, at, work in lists])


def peer_scores(nc, name, hi, lo, w_dram, keys_dram, value, at):
    LISTS = 2 * PEER_HEADS
    with Stage(nc, name) as s:
        raw = s.sb("raw", [P, 2, KD, P])
        w_hi, w_lo = s.sb("w_hi", [P, 2, KD, P], F32R), s.sb("w_lo", [P, 2, KD, P], F32R)
        keys = s.sb("keys", [P, LISTS, KEYS])
        query = s.sb("query", [P, 2, SEQ])
        score = s.sb("score", [P, 2, TILES, KEYS])
        made, scores = s.ps("made", [P, 2, BANK]), s.ps("scores", [P, 2, TILES, KEYS])
        loaded, w_in = s.sem("loaded"), [s.sem(f"w_in{u}") for u in range(2)]
        w_rounded, w_split, summed, kept = (s.sem(x) for x in ("w_rounded", "w_split", "summed", "kept"))
        scored, stored, order, used = (s.sem(x) for x in ("scored", "stored", "order", "used"))
        with s.block() as block:
            @block.sync
            def _(sp):
                for n in range(LISTS):
                    if n >= 2:
                        sp.wait_ge(w_split, n - 1)
                    sp.dma_start(raw[:, n % 2], w_dram[n]).then_inc(w_in[n % 2], 16)
                    if n == 1:
                        sp.dma_start(keys[:], keys_dram).then_inc(loaded, 16)

            @block.tensor
            def _(pe):
                def multiply(n):
                    pe.wait_ge(w_split, n + 1)
                    if n >= 2:
                        pe.wait_ge(kept, n - 1)
                    for k in range(KD):
                        last = passes(nc, made[:, n % 2], (w_hi[:, n % 2, k], w_lo[:, n % 2, k]), (hi[:, k], lo[:, k]), k == 0, k == KD - 1)
                    last.then_inc(summed, 1)

                multiply(0)
                pe.wait_ge(loaded, 16)
                for n in range(LISTS):
                    if n + 1 < LISTS:
                        multiply(n + 1)
                    pe.wait_ge(kept, n + 1)
                    if n >= 2:
                        pe.wait_ge(stored, n - 1)
                    for t in range(TILES):
                        last = nc.tensor.matmul(scores[:, n % 2, t], query[:, n % 2, t * P:(t + 1) * P], keys[:, n], start=True, stop=True)
                    last.then_inc(scored, 1)

            @block.scalar
            def _(act):
                def round_(n):
                    act.wait_ge(w_in[n % 2], 16 * (n // 2) + 16)
                    if n >= 2:
                        act.wait_ge(summed, n - 1)
                    nc.scalar.copy(w_hi[:, n % 2], raw[:, n % 2]).then_inc(w_rounded, 1)

                def keep(n):
                    act.wait_ge(summed, n + 1)
                    if n >= 2:
                        act.wait_ge(scored, n - 1)
                    nc.scalar.copy(query[:, n % 2], made[:, n % 2]).then_inc(kept, 1)

                round_(0)
                round_(1)
                keep(0)
                for n in range(LISTS):
                    if n + 2 < LISTS:
                        round_(n + 2)
                    if n + 1 < LISTS:
                        keep(n + 1)
                    act.wait_ge(scored, n + 1)
                    if n >= 2:
                        act.wait_ge(used, n - 1)
                    nc.scalar.copy(score[:, n % 2], scores[:, n % 2]).then_inc(stored, 1)

            @block.gpsimd
            def _(pool):
                for n in range(LISTS):
                    pool.wait_ge(w_rounded, n + 1)
                    nc.gpsimd.tensor_tensor(w_lo[:, n % 2], raw[:, n % 2], w_hi[:, n % 2].bitcast(F32), ALU.subtract).then_inc(w_split, 1)

            @block.vector
            def _(dve):
                then = Chain(dve, order)
                for n in range(LISTS):
                    dve.wait_ge(stored, n + 1)
                    top16(then, nc.vector, [(value[:, t, n], at[:, t, n], score[:, n % 2, t]) for t in range(TILES)])
                    dve.sem_inc(used, 1)


def peer_pick(nc, g, name, value, at, picks):
    with Stage(nc, name) as s:
        key = s.sb("key", [P, 2 * PEER_HEADS, TOP])
        both = s.sb("both", [P, SET, TOP, TOP])
        best, place = s.sb("best", [P, PEER_HEADS, TOP]), s.sb("place", [P, PEER_HEADS, TOP], U32)
        half_at, half = s.sb("half_at", [P, PEER_HEADS, TOP], U32), s.sb("half", [P, PEER_HEADS, TOP])
        match = s.sb("match", [P, PEER_HEADS, TOP, TOP])
        low, raised = s.sb("low", [P, PEER_HEADS, TOP]), s.sb("raised", [P, 2, PEER_HEADS, TOP])
        total, inv = s.sb("total", [P, PEER_HEADS]), s.sb("inv", [P, PEER_HEADS])
        found = s.sb("found", [P, 2, 3, PICKS])
        pt = s.ps("pt", [P, 2, BANK])
        order, low_done, raised_done, picked, turned, stored = (
            s.sem(x) for x in ("order", "low_done", "raised_done", "picked", "turned", "stored"))
        wide = [P, PEER_HEADS, TOP, TOP]
        with s.block() as block:
            @block.tensor
            def _(pe):
                for t in range(TILES):
                    pe.wait_ge(picked, t + 1)
                    if t >= 2:
                        pe.wait_ge(stored, t - 1)
                    for j in range(3):
                        last = nc.tensor.transpose(pt[:, t % 2, j * P:(j + 1) * P], found[:, t % 2, j], g.ident[:])
                    last.then_inc(turned, 1)

            @block.scalar
            def _(act):
                for t in range(TILES):
                    act.wait_ge(low_done, t + 1)
                    nc.scalar.activation(raised[:, t % 2], low[:], ACT.Exp).then_inc(raised_done, 1)
                    act.wait_ge(turned, t + 1)
                    nc.scalar.copy(picks[:, :, t * P:(t + 1) * P], pt[:, t % 2, :3 * P].rearrange("p (j n) -> p j n", j=3)).then_inc(stored, 1)

            @block.vector
            def _(dve):
                v = nc.vector
                then = Chain(dve, order)
                for t in range(TILES):
                    then(v.tensor_copy(key[:], at[:, t]))
                    for start in range(0, PEER_HEADS, SET):
                        heads = range(start, start + SET)
                        then(*[v.tensor_tensor(both[:, h % SET], value[:, t, 2 * h].unsqueeze(2).to_broadcast([P, TOP, TOP]),
                                               value[:, t, 2 * h + 1].unsqueeze(1).to_broadcast([P, TOP, TOP]), ALU.add) for h in heads])
                        top16(then, v, [(best[:, h], place[:, h], both[:, h % SET].rearrange("p a b -> p (a b)")) for h in heads])
                    if t:
                        dve.wait_ge(raised_done, t)
                    v.tensor_tensor(low[:], best[:], best[:, :, 0:1].to_broadcast([P, PEER_HEADS, TOP]), ALU.subtract).then_inc(low_done, 1)
                    if t >= 2:
                        dve.wait_ge(turned, t - 1)
                    for j, (op, n) in enumerate(((ALU.logical_shift_right, 4), (ALU.bitwise_and, TOP - 1))):
                        then(v.tensor_scalar(half_at[:], place[:], n, None, op))
                        then(v.tensor_copy(half[:], half_at[:]))
                        then(v.tensor_tensor(match[:], half[:].unsqueeze(3).to_broadcast(wide),
                                             g.iota[:, :TOP].unsqueeze(1).unsqueeze(1).to_broadcast(wide), ALU.is_equal))
                        then(v.tensor_tensor(match[:], match[:], key[:, j::2].unsqueeze(2).to_broadcast(wide), ALU.mult))
                        then(v.tensor_reduce(found[:, t % 2, j].rearrange("p (h k) -> p h k", h=PEER_HEADS), match[:], AX, ALU.add))
                    dve.wait_ge(raised_done, t + 1)
                    then(v.tensor_reduce(total[:], raised[:, t % 2], AX, ALU.add))
                    then(v.reciprocal(inv[:], total[:]))
                    v.tensor_tensor(found[:, t % 2, 2].rearrange("p (h k) -> p h k", h=PEER_HEADS), raised[:, t % 2],
                                    inv[:].unsqueeze(2).to_broadcast([P, PEER_HEADS, TOP]), ALU.mult).then_inc(picked, 1)


def peer_prepare(nc, g, name, picks, keys_of, gates, numbers):
    with Stage(nc, name) as s:
        rest = s.sb("rest", [P, 2, SEQ])
        order, copied = s.sem("order"), s.sem("copied")
        with s.block() as block:
            @block.scalar
            def _(act):
                nc.scalar.copy(keys_of[:], picks[:, :2]).then_inc(copied, 1)
                nc.scalar.copy(numbers[:], g.iota[:].unsqueeze(2).to_broadcast([P, KEYS, GROUP])).then_inc(copied, 1)

            @block.vector
            def _(dve):
                then = Chain(dve, order)
                left = picks[:, 2]
                for j in range(3):
                    then(nc.vector.tensor_copy(gates[:, j], left))
                    if j < 2:
                        then(nc.vector.tensor_tensor(rest[:, j], left, gates[:, j], ALU.subtract))
                        left = rest[:, j]


def peer_weights(nc, g, name, keys_of, gates, numbers, part, weights, u_dram, v_dram):
    SLOTS = 4
    with Stage(nc, name) as s:
        first = s.sb("first", [P, SLOTS, KEYS, GROUP], BF16)
        match, second = s.sb("match", [P, SLOTS, PART, GROUP], BF16), s.sb("second", [P, SLOTS, 3, PART, GROUP], BF16)
        acc = s.ps("acc", [P, SLOTS, BANK])
        matched, first_made, second_made = s.sem("matched"), s.sem("first_made"), s.sem("second_made")
        summed, kept = s.sem("summed"), s.sem("kept")
        landed = s.sem("landed")
        LOOPS = SEQ // (SLOTS * GROUP)
        raw_up, raw_down = landing(g, 1)
        with s.block() as block:
            @block.sync
            def _(sp):
                for u in range(2):
                    sp.dma_start(raw_up[u][0], u_dram[part * PART + u]).then_inc(landed, 16)
                    sp.dma_start(raw_down[u], v_dram[part * PART + u]).then_inc(landed, 16)
                sp.wait_ge(landed, 64)

            @block.vector
            def _(dve):
                def spread(n, j, width):
                    return keys_of[:, j, bass.ds(n * GROUP, GROUP)].unsqueeze(1).to_broadcast([P, width, GROUP])

                with dve.Fori(0, LOOPS) as i:
                    for u in range(SLOTS):
                        n = SLOTS * i + u
                        dve.wait_ge(summed, n + 1)
                        nc.vector.tensor_tensor(match[:, u], numbers[:, part * PART:(part + 1) * PART], spread(n, 1, PART),
                                                ALU.is_equal).then_inc(matched, 1)
                        nc.vector.tensor_tensor(first[:, u], numbers[:], spread(n, 0, KEYS), ALU.is_equal).then_inc(first_made, 1)
                        dve.wait_ge(matched, n + 1)
                        nc.vector.tensor_tensor(
                            second[:, u], match[:, u].unsqueeze(1).to_broadcast([P, 3, PART, GROUP]),
                            gates[:, :, bass.ds(n * GROUP, GROUP)].unsqueeze(2).to_broadcast([P, 3, PART, GROUP]),
                            ALU.mult).then_inc(second_made, 1)

            @block.tensor
            def _(pe):
                pe.sem_inc(summed, SLOTS)
                with pe.Fori(0, LOOPS) as i:
                    for u in range(SLOTS):
                        n = SLOTS * i + u
                        pe.wait_ge(first_made, n + 1)
                        pe.wait_ge(second_made, n + 1)
                        pe.wait_ge(kept, n + 1)
                        for j in range(GROUP):
                            for k in range(3):
                                last = nc.tensor.matmul(acc[:, u, j * PART:(j + 1) * PART], first[:, u, :, j], second[:, u, k, :, j],
                                                        start=(k == 0), stop=(k == 2))
                        last.then_inc(summed, 1)

            @block.scalar
            def _(act):
                act.sem_inc(kept, SLOTS)
                with act.Fori(0, LOOPS) as i:
                    for u in range(SLOTS):
                        n = SLOTS * i + u
                        act.wait_ge(summed, n + 1 + SLOTS)
                        nc.scalar.copy(weights[:, bass.ds(n * GROUP, GROUP), :],
                                       acc[:, u, :GROUP * PART].rearrange("p (t j) -> p t j", t=GROUP)).then_inc(kept, 1)


def peer(nc, g, name, a):
    with ExitStack() as own:
        keys_of = own.enter_context(nc.sbuf_tensor(f"{name}_keys_of", [P, 2, SEQ], BF16))
        gates = own.enter_context(nc.sbuf_tensor(f"{name}_gates", [P, 3, SEQ], BF16))
        numbers = own.enter_context(nc.sbuf_tensor(f"{name}_numbers", [P, KEYS, GROUP], BF16))
        hi, lo = (own.enter_context(nc.sbuf_tensor(f"{name}_h_{x}", [P, KD, SEQ], F32R)) for x in ("hi", "lo"))
        split_rows(nc, g, f"{name}_split", hi, lo)
        with nc.sbuf_tensor(f"{name}_picks", [P, 3, SEQ], F32) as picks:
            lists = [P, TILES, 2 * PEER_HEADS, TOP]
            with nc.sbuf_tensor(f"{name}_value", lists, F32) as value, nc.sbuf_tensor(f"{name}_at", lists, U32) as at:
                peer_scores(nc, f"{name}_scores", hi, lo, a["peer_wq"], a["peer_keys"], value, at)
                peer_pick(nc, g, f"{name}_pick", value, at, picks)
            peer_prepare(nc, g, f"{name}_prepare", picks, keys_of, gates, numbers)
        weights = own.enter_context(nc.sbuf_tensor(f"{name}_weights", [P, SEQ, PART], F32))
        acc = g.mod[:, 0:TILES].rearrange("p t (h n) -> p t h n", n=BANK)
        with Stage(nc, f"{name}_zero") as s:
            zeroed = s.sem("zeroed")
            with s.block() as block:
                @block.vector
                def _(dve):
                    nc.vector.memset(acc, 0.0).then_inc(zeroed, 1)

        def weight(n):
            return weights[:, :, n] if isinstance(n, int) else weights[:, :, bass.ds(n, 1)].rearrange("p t o -> p (t o)")

        for part in range(KEYS // PART):
            peer_weights(nc, g, f"{name}_weights{part}", keys_of, gates, numbers, part, weights, a["peer_u"], a["peer_v"])
            expert_chunks(nc, g, f"{name}_part{part}", [a["peer_u"]], a["peer_v"], part * PART, PART, hi, lo,
                          ACT.Gelu, weight, None, acc, landed=True)
        with Stage(nc, f"{name}_sum") as s:
            gated, added = s.sem("gated"), s.sem("added")
            with s.block() as block:
                @block.vector
                def _(dve):
                    for t in range(TILES):
                        rows = g.mod[:, t]
                        nc.vector.tensor_tensor(rows, rows, g.mod[:, 5], ALU.mult).then_inc(gated, 1)
                        dve.wait_ge(gated, t + 1)
                        nc.vector.scalar_tensor_tensor(g.x[:, t], g.x[:, t], ALPHA, rows, ALU.mult, ALU.add).then_inc(added, 1)
def build_program(nc, a, out):
    with ExitStack() as own:
        def sb(name, shape, dtype=F32):
            return own.enter_context(nc.sbuf_tensor(name, shape, dtype))

        g = Global()
        g.x = sb("x", [P, TILES, D])
        g.hT = sb("hT", [P, KD, SEQ])
        g.mod = sb("mod", [P, 6, D])
        g.ident, g.causal, g.iota = sb("ident", [P, P]), sb("causal", [P, P]), sb("iota", [P, P])
        g.comb = sb("comb", [P, TILES, EXPERTS])
        constants(nc, a, g)

        modulation(nc, g, "ada0", a["c"], a["w_ada0"], a["b_ada"][0:1])
        normed(nc, g, "fox_norm", "rms", 1, 0, a["mix_gain"][0])
        fox(nc, g, a)
        ada1, cond = Global(), Global()
        ada1.c_dram, ada1.w, cond.c_dram, cond.w = a["c"], a["w_ada1"], a["c_2"], a["cond_w"]
        ada1.sums, cond.sums = (nc.dram_tensor(f"{x}_side_sums", [6 * D // SIDE, P, SIDE], F32, kind="Internal").ap() for x in ("ada1", "cond"))
        moe(nc, g, a, 0, ada1)

        side_modulation(nc, g, "ada1", ada1.sums, a["b_ada"][1:2])
        normed(nc, g, "mla_norm", "rms", 1, 0, a["mix_gain"][1])
        mla(nc, g, a)
        moe(nc, g, a, 1, cond)

        side_modulation(nc, g, "cond", cond.sums, a["cond_b"])
        normed(nc, g, "hybrid_norm", "ln", 1, 0)
        hybrid(nc, g, a)
        layer_norm_rows(nc, g, "ln1", a["ln1_g"], a["ln1_b"])
        normed(nc, g, "peer_norm", "ln", 4, 3)
        peer(nc, g, "peer", a)
        layer_norm_rows(nc, g, "ln2", a["ln2_g"], a["ln2_b"])

        with Stage(nc, "store") as s:
            stored = s.sem("stored")
            with s.block() as block:
                @block.sync
                def _(sp):
                    sp.dma_start(out.rearrange("o (t p) d -> p (o t) d", p=P), g.x[:]).then_inc(stored, 16)
                    sp.wait_ge(stored, 16)
        Stage.finish(nc)


class Global:
    pass


def fox(nc, g, a):
    with nc.sbuf_tensor("fox_o", [P, TILES, D], F32) as o:
        with ExitStack() as own:
            qkv = own.enter_context(nc.sbuf_tensor("fox_qkv", [P, TILES, 3 * D], F32))
            q, k, v = (qkv[:, :, j * D:(j + 1) * D] for j in range(3))
            project_rows(nc, "fox_in", g.hT, KD, a["fox_w_in"], 3 * D // HALF, HALF, keep=qkv)
            cum_q = own.enter_context(nc.sbuf_tensor("fox_cum_q", [P, TILES, HEADS], F32))
            cum_k = own.enter_context(nc.sbuf_tensor("fox_cum_k", [P, HEADS, SEQ], F32))
            sums = nc.dram_tensor("fox_sums", [HEADS, SEQ], F32, kind="Internal").ap()
            forget_gates(nc, g, "fox_gates", a["fox_w_f"], a["fox_b_f"], sums, cum_q, cum_k)
            head_norms(nc, "fox_heads", [(q, a["fox_q_norm"], FOX_DK ** -0.5), (k, a["fox_k_norm"], 1.0)], FOX_DK)
            attention(nc, g, "fox_attn", q, k, v, o, FOX_DK, cum_q=cum_q, cum_k=cum_k)
        turn_rows(nc, g, "fox_turn", o, KD, g.hT)
        project_rows(nc, "fox_out", g.hT, KD, a["fox_w_out"], D // HALF, HALF, gate=g.mod[:, 2], x=g.x)


def mla(nc, g, a):
    kq, kkv = Q_RANK // P, KV_RANK // P
    with nc.sbuf_tensor("mla_low", [P, TILES, Q_RANK + KV_RANK + ROPE], F32) as low, nc.sbuf_tensor("mla_o", [P, TILES, HEADS * DV], F32) as o:
        project_rows(nc, "mla_in", g.hT, KD, a["mla_w_in"], 2, (Q_RANK + KV_RANK + ROPE) // 2, keep=low)
        head_norms(nc, "mla_q_lat", [(low[:, :, :Q_RANK], a["mla_q_lat"], 1.0)], Q_RANK, heads=1)
        head_norms(nc, "mla_kv_lat", [(low[:, :, Q_RANK:Q_RANK + KV_RANK], a["mla_kv_lat"], 1.0)], KV_RANK, heads=1)
        turn_rows(nc, g, "mla_turn_low", low, kq + kkv, g.hT)
        with ExitStack() as own:
            def sb(name, shape):
                return own.enter_context(nc.sbuf_tensor(f"mla_{name}", shape, F32))

            q, k, kv = sb("q", [P, TILES, HEADS * QK]), sb("k", [P, TILES, HEADS * QK]), sb("kv", [P, TILES, HEADS * (NOPE + DV)])
            cos, sin = sb("cos", [P, TILES, ROPE // 2]), sb("sin", [P, TILES, ROPE // 2])
            project_rows(nc, "mla_uq", g.hT[:, :kq], kq, a["mla_w_uq"], 4, HEADS * QK // 4, keep=q)
            project_rows(nc, "mla_ukv", g.hT[:, kq:kq + kkv], kkv, a["mla_w_ukv"], 4, BANK, keep=kv)
            split_latents(nc, g, "mla_split", kv, low[:, :, Q_RANK + KV_RANK:], a["positions"], a["freq"], k, cos, sin)
            head_norms(nc, "mla_heads", [(q, a["mla_q_norm"], QK ** -0.5), (k, a["mla_k_norm"], 1.0)], QK)
            rotate(nc, "mla_rotate", (q, k), cos, sin)
            attention(nc, g, "mla_attn", q, k, kv, o, QK, v_step=NOPE + DV, v_at=NOPE)
        turn_rows(nc, g, "mla_turn", o, KD, g.hT)
        project_rows(nc, "mla_out", g.hT, KD, a["mla_w_out"], D // HALF, HALF, gate=g.mod[:, 2], x=g.x)


def moe(nc, g, a, layer, side):
    normed(nc, g, f"moe_norm{layer}", "rms", 4, 3, a["ffn_gain"][layer])
    route(nc, g, f"moe_route{layer}", a["moe_w_route"][layer], a["moe_b_route"][layer])
    experts(nc, g, f"moe{layer}", a["moe_gate"][layer], a["moe_up"][layer], a["moe_down"][layer], g.mod[:, 5], side)


def hybrid(nc, g, a):
    with nc.sbuf_tensor("hybrid_y", [P, TILES, D], F32) as y:
        with ExitStack() as own:
            o = Global()
            o.alpha, o.beta, o.kappa, o.rho, o.grown, o.value = (
                own.enter_context(nc.sbuf_tensor(f"rw_{x}", [P, RC, SEQ], F32))
                for x in ("alpha", "beta", "kappa", "rho", "grown", "value"))
            o.gate = own.enter_context(nc.sbuf_tensor("rw_gate", [P, TILES, RW], F32))
            o.bonus = own.enter_context(nc.sbuf_tensor("rw_bonus", [P, TILES, RW_HEADS], F32))
            with nc.sbuf_tensor("hybrid_pT", [P, IN_CHUNKS, SEQ], F32) as pT:
                with nc.sbuf_tensor("conv_cols", [P, CC, SEQ], F32) as conv:
                    hybrid_in(nc, g, "hybrid_in", a["w_in"], a["conv_w"], a["conv_b"], pT, conv)
                    with nc.sbuf_tensor("conv_rows", [P, TILES, CONV], F32) as conv_rows:
                        turn_cols(nc, g, "conv_turn", conv, CC, [conv_rows[:, t] for t in range(TILES)])
                        conv_norm(nc, g, "conv_norm", conv_rows, a["conv_gain"], a["conv_shift"], y)
                rwkv_inputs(nc, g, "rw_in", a, pT, o)
            rwkv(nc, g, "rw", a, o, y)
        turn_rows(nc, g, "hybrid_turn", y, KD, g.hT)
        project_rows(nc, "hybrid_out", g.hT, KD, a["w_out"], D // HALF, HALF, gate=g.mod[:, 2], x=g.x, alpha=ALPHA)




def row_chunks(w, width):
    k, n = w.shape
    return w.reshape(k // P, P, n // width, width).transpose(2, 1, 0, 3)


def in_columns(v):
    return v.reshape(-1, P).T


def everywhere(v):
    return np.broadcast_to(v[..., None, :], v.shape[:-1] + (P, v.shape[-1]))


def shape_constants():
    i = np.arange(P)
    same = i[:, None] // SPAN == i[None] // SPAN
    before, upto = i[:, None] < i[None], i[:, None] <= i[None]
    half = ROPE // 2
    return {
        "ident": np.eye(P),
        "causal": np.where(i[None] <= i[:, None], 0.0, NEG),
        "iota": np.broadcast_to(np.arange(P), (P, P)),
        "freq": everywhere(np.float32(10000.0) ** (-np.arange(half, dtype=np.float32) / np.float32(half))),
        "masks": np.stack([same & before.T, same & before, same & upto, same & upto], 1),
        "span": i[:, None] // SPAN == np.arange(BLOCKS)[None],
        "pairs": i[:, None] // RW_DIM == i[None] // RW_DIM,
        "heads": i[:, None] // RW_DIM == np.arange(2)[None],
        "fresh": np.broadcast_to(np.arange(SEQ) % SPAN != 0, (P, SEQ)),
    }


def laid_out(x):
    fox_w = x["fox_w_in"][0]
    route_w = np.concatenate([x["moe_w_grp"], x["moe_w_rt"]], 2)
    route_b = np.concatenate([x["moe_b_grp"], x["moe_b_rt"]], 1)
    layers = route_w.shape[0]

    def raising(w):
        return w.reshape(layers, EXPERTS, KD, P, D_EXPERT // P, P).transpose(0, 1, 4, 3, 2, 5).reshape(layers, -1, P, KD, P)

    return {
        "x": x["x"],
        "c": in_columns(x["c"][0]), "c_2": in_columns(x["c_2"][0]),
        "positions": in_columns(x["positions"][0]),
        "w_ada0": row_chunks(x["w_ada"][0], BANK), "w_ada1": row_chunks(x["w_ada"][1], SIDE), "b_ada": x["b_ada"],
        "cond_w": row_chunks(x["cond_w_2"], SIDE), "cond_b": x["cond_b_2"][None],
        "mix_gain": everywhere(x["mix_norm"]), "ffn_gain": everywhere(x["ffn_norm"]),
        "fox_w_in": row_chunks(fox_w[:, :3 * D], HALF),
        "fox_w_f": fox_w[:, 3 * D:].reshape(KD, P, HEADS).transpose(1, 0, 2),
        "fox_b_f": x["fox_b_f"][0][:, None],
        "fox_q_norm": everywhere(x["fox_q_norm"][0]), "fox_k_norm": everywhere(x["fox_k_norm"][0]),
        "fox_w_out": row_chunks(x["fox_w_out"][0], HALF),
        "mla_w_in": row_chunks(x["mla_w_in"][0], (Q_RANK + KV_RANK + ROPE) // 2),
        "mla_q_lat": everywhere(x["mla_q_lat_norm"][0]), "mla_kv_lat": everywhere(x["mla_kv_lat_norm"][0]),
        "mla_w_uq": row_chunks(x["mla_w_uq"][0], HEADS * QK // 4), "mla_w_ukv": row_chunks(x["mla_w_ukv"][0], BANK),
        "mla_q_norm": everywhere(x["mla_q_norm"][0]), "mla_k_norm": everywhere(x["mla_k_norm"][0]),
        "mla_w_out": row_chunks(x["mla_w_out"][0], HALF),
        "moe_w_route": route_w.reshape(layers, KD, P, -1).transpose(0, 2, 1, 3), "moe_b_route": everywhere(route_b),
        "moe_gate": raising(x["moe_w_gate"]), "moe_up": raising(x["moe_w_up"]),
        "moe_down": x["moe_w_down"].reshape(layers, -1, P, D),
        "w_in": row_chunks(x["w_in_2"], P), "mu": in_columns(x["mu_shift_2"]),
        "conv_w": x["conv_w_2"].T.reshape(CC, P, TAPS).transpose(1, 0, 2), "conv_b": in_columns(x["conv_b_2"]),
        "conv_gain": everywhere(x["conv_ln_g_2"]), "conv_shift": everywhere(x["conv_ln_b_2"]),
        "rw_col": np.stack([in_columns(x[n].reshape(-1)) for n in ("rw_w0_2", "rw_a0_2", "rw_kk_2", "rw_ka_2", "rw_rk_2")], 1),
        "w2a2": np.concatenate([x["rw_w2_2"], x["rw_a2_2"]], 0), "rw_g2": x["rw_g2_2"],
        "rw_gain": everywhere(x["rw_lnx_g_2"]), "rw_shift": everywhere(x["rw_lnx_b_2"]),
        "w_out": row_chunks(x["w_out_2"], HALF),
        "ln1_g": everywhere(x["ln1_g_2"]), "ln1_b": everywhere(x["ln1_b_2"]),
        "ln2_g": everywhere(x["ln2_g_2"]), "ln2_b": everywhere(x["ln2_b_2"]),
        "peer_wq": row_chunks(x["peer_wq_2"], P),
        "peer_keys": np.stack([x["peer_k1_2"], x["peer_k2_2"]], 1).reshape(2 * PEER_HEADS, KEYS, P).transpose(2, 0, 1),
        "peer_u": x["peer_u_2"].reshape(KEYS, KEYS, KD, P).transpose(1, 3, 2, 0),
        "peer_v": x["peer_v_2"].reshape(KEYS, KEYS, D).transpose(1, 0, 2),
    }


def kernel(**inputs):
    import concourse.bacc as bacc
    from concourse.bass_utils import run_bass_kernel_spmd

    nc = bacc.Bacc("TRN2", target_bir_lowering=False, num_devices=1)
    arrays = {n: np.ascontiguousarray(v) for n, v in laid_out({n: np.asarray(v) for n, v in inputs.items()}).items()}
    arrays.update({n: np.ascontiguousarray(v, dtype=np.float32) for n, v in shape_constants().items()})
    aps = {n: nc.dram_tensor(f"in_{n}", v.shape, mybir.dt.from_np(v.dtype), kind="ExternalInput").ap() for n, v in arrays.items()}
    out = nc.dram_tensor("out_rows", (1, SEQ, D), F32, kind="ExternalOutput").ap()
    build_program(nc, aps, out)
    result = run_bass_kernel_spmd(nc, [{f"in_{n}": v for n, v in arrays.items()}], core_ids=[0])
    return result.results[0]["out_rows"]
```
